# Optimizing a Trainium2 kernel written in Bass

```python
import math
import jax, jax.numpy as jnp
from jax import lax
import numpy as np

D_MODEL = 1024
BATCH = 1
SEQ = 512
DEPTH = 1

NSA_HEADS = 8
NSA_GROUPS = 2
HEADS_PER_GROUP = NSA_HEADS // NSA_GROUPS
HEAD_DIM = 64
NSA_WIDTH = NSA_HEADS * HEAD_DIM
KV_WIDTH = NSA_GROUPS * HEAD_DIM
CMP_BLOCK = 32
CMP_STRIDE = 16
CMP_HIDDEN = 256
SEL_BLOCK = 64
SEL_TOPK = 16
WINDOW = 512
Q_BLOCK = 64
ROPE_THETA = 10000.0
FORCED_SCORE = 1.0e4
NEG = -1.0e30
S5_WIDTH = D_MODEL // 2
S5_GROUP = 16
S5_GROUPS = S5_WIDTH // S5_GROUP
S5_STATE = 64
DT_MIN = 1.0e-3
DT_MAX = 1.0e-1
N_BRANCHES = 2
RMS_EPS = 1.0e-6
D_IN = NSA_WIDTH + 6 * KV_WIDTH + 3 * NSA_HEADS + NSA_WIDTH + 2 * S5_WIDTH + N_BRANCHES * D_MODEL

kernel_name = "hybrid_nsa_s5_gated_block"

def _split_points():
    sizes = [NSA_WIDTH] + [KV_WIDTH] * 6 + [3 * NSA_HEADS, NSA_WIDTH, S5_WIDTH, S5_WIDTH]
    pts, acc = [], 0
    for s in sizes:
        acc += s
        pts.append(acc)
    return pts

def rmsnorm(x, g):
    xf = x.astype(jnp.float32)
    y = xf * lax.rsqrt(jnp.mean(xf * xf, axis=-1, keepdims=True) + RMS_EPS)
    return (y * g.astype(jnp.float32)).astype(x.dtype)

def rope(t, pos):
    half = t.shape[-1] // 2
    inv_freq = ROPE_THETA ** (-jnp.arange(half, dtype=jnp.float32) / half)
    ang = pos.astype(jnp.float32)[:, None] * inv_freq[None, :]
    shp = (1, t.shape[1]) + (1,) * (t.ndim - 3) + (half,)
    cos = jnp.cos(ang).reshape(shp).astype(t.dtype)
    sin = jnp.sin(ang).reshape(shp).astype(t.dtype)
    t1, t2 = t[..., :half], t[..., half:]
    return jnp.concatenate([t1 * cos - t2 * sin, t2 * cos + t1 * sin], axis=-1)

def masked_softmax(s, mask):
    s = jnp.where(mask, s.astype(jnp.float32), NEG)
    m = jnp.max(s, axis=-1, keepdims=True)
    e = jnp.exp(s - m) * mask
    return e / jnp.maximum(jnp.sum(e, axis=-1, keepdims=True), 1.0e-30)

def compress(kv, pos_emb, w1, w2):
    B, T, G, dh = kv.shape
    chunks = kv.reshape(B, T // CMP_STRIDE, CMP_STRIDE, G, dh)
    blocks = jnp.concatenate([chunks[:, :-1], chunks[:, 1:]], axis=2)
    blocks = blocks + pos_emb[None, None, :, None, :]
    flat = jnp.moveaxis(blocks, 3, 2).reshape(B, blocks.shape[1], G, CMP_BLOCK * dh)
    return jax.nn.gelu(flat @ w1) @ w2

def s5_scan(u, lam_re, lam_im, log_dt, b_re, b_im, c_re, c_im, d):
    B, T, _ = u.shape
    f32 = jnp.float32
    lam_re, lam_im = lam_re.astype(f32), lam_im.astype(f32)
    dt = jnp.exp(log_dt.astype(f32))[:, None]
    mag = jnp.exp(lam_re * dt)
    a_re, a_im = mag * jnp.cos(lam_im * dt), mag * jnp.sin(lam_im * dt)
    den = lam_re * lam_re + lam_im * lam_im
    z_re = ((a_re - 1.0) * lam_re + a_im * lam_im) / den
    z_im = (a_im * lam_re - (a_re - 1.0) * lam_im) / den
    b_re, b_im = b_re.astype(f32), b_im.astype(f32)
    bb_re = z_re[..., None] * b_re - z_im[..., None] * b_im
    bb_im = z_re[..., None] * b_im + z_im[..., None] * b_re
    ug = u.astype(f32).reshape(B, T, S5_GROUPS, S5_GROUP)
    bu_re = jnp.einsum('btgc,gpc->btgp', ug, bb_re)
    bu_im = jnp.einsum('btgc,gpc->btgp', ug, bb_im)
    ar = jnp.broadcast_to(a_re, bu_re.shape)
    ai = jnp.broadcast_to(a_im, bu_im.shape)

    def combine(e1, e2):
        a1r, a1i, b1r, b1i = e1
        a2r, a2i, b2r, b2i = e2
        return (a2r * a1r - a2i * a1i,
                a2r * a1i + a2i * a1r,
                a2r * b1r - a2i * b1i + b2r,
                a2r * b1i + a2i * b1r + b2i)

    _, _, xr, xi = lax.associative_scan(combine, (ar, ai, bu_re, bu_im), axis=1)
    y = jnp.einsum('btgp,gcp->btgc', xr, c_re.astype(f32)) - jnp.einsum('btgp,gcp->btgc', xi, c_im.astype(f32))
    y = y.reshape(B, T, S5_WIDTH) + d.astype(f32) * u.astype(f32)
    return y.astype(u.dtype)

def setup_inputs(seed: int = 0) -> dict:
    key = jax.random.key(seed)
    ks = jax.random.split(key, 24)
    nrm = jax.random.normal
    L = DEPTH
    n = jnp.arange(S5_STATE, dtype=jnp.float32)
    log_lo, log_hi = math.log(DT_MIN), math.log(DT_MAX)
    return {
        "x": nrm(ks[0], (BATCH, SEQ, D_MODEL), jnp.float32),
        "norm_g": 1.0 + 0.02 * nrm(ks[1], (L, D_MODEL), jnp.float32),
        "w_in": nrm(ks[2], (L, D_MODEL, D_IN), jnp.float32) * D_MODEL ** -0.5,
        "cmp_pos_k": 0.1 * nrm(ks[3], (L, CMP_BLOCK, HEAD_DIM), jnp.float32),
        "cmp_pos_v": 0.1 * nrm(ks[4], (L, CMP_BLOCK, HEAD_DIM), jnp.float32),
        "cmp_w1_k": nrm(ks[5], (L, CMP_BLOCK * HEAD_DIM, CMP_HIDDEN), jnp.float32) * (CMP_BLOCK * HEAD_DIM) ** -0.5,
        "cmp_w2_k": nrm(ks[6], (L, CMP_HIDDEN, HEAD_DIM), jnp.float32) * CMP_HIDDEN ** -0.5,
        "cmp_w1_v": nrm(ks[7], (L, CMP_BLOCK * HEAD_DIM, CMP_HIDDEN), jnp.float32) * (CMP_BLOCK * HEAD_DIM) ** -0.5,
        "cmp_w2_v": nrm(ks[8], (L, CMP_HIDDEN, HEAD_DIM), jnp.float32) * CMP_HIDDEN ** -0.5,
        "s5_lam_re": -0.5 + 0.01 * nrm(ks[9], (L, S5_GROUPS, S5_STATE), jnp.float32),
        "s5_lam_im": math.pi * n + 0.01 * nrm(ks[10], (L, S5_GROUPS, S5_STATE), jnp.float32),
        "s5_log_dt": jax.random.uniform(ks[11], (L, S5_GROUPS), jnp.float32, log_lo, log_hi),
        "s5_b_re": nrm(ks[12], (L, S5_GROUPS, S5_STATE, S5_GROUP), jnp.float32) * (2 * S5_GROUP) ** -0.5,
        "s5_b_im": nrm(ks[13], (L, S5_GROUPS, S5_STATE, S5_GROUP), jnp.float32) * (2 * S5_GROUP) ** -0.5,
        "s5_c_re": nrm(ks[14], (L, S5_GROUPS, S5_GROUP, S5_STATE), jnp.float32) * S5_STATE ** -0.5,
        "s5_c_im": nrm(ks[15], (L, S5_GROUPS, S5_GROUP, S5_STATE), jnp.float32) * S5_STATE ** -0.5,
        "s5_d": nrm(ks[16], (L, S5_WIDTH), jnp.float32),
        "w_glu": nrm(ks[17], (L, S5_WIDTH, S5_WIDTH), jnp.float32) * S5_WIDTH ** -0.5,
        "b_glu": 0.01 * nrm(ks[18], (L, S5_WIDTH), jnp.float32),
        "w_proj_nsa": nrm(ks[19], (L, NSA_WIDTH, D_MODEL), jnp.float32) * NSA_WIDTH ** -0.5,
        "w_proj_s5": nrm(ks[20], (L, S5_WIDTH, D_MODEL), jnp.float32) * S5_WIDTH ** -0.5,
        "w_out": nrm(ks[21], (L, D_MODEL, D_MODEL), jnp.float32) * D_MODEL ** -0.5,
        "final_g": 1.0 + 0.02 * nrm(ks[22], (D_MODEL,), jnp.float32),
    }

def reference(x, norm_g, w_in, cmp_pos_k, cmp_pos_v, cmp_w1_k, cmp_w2_k, cmp_w1_v, cmp_w2_v,
              s5_lam_re, s5_lam_im, s5_log_dt, s5_b_re, s5_b_im, s5_c_re, s5_c_im, s5_d,
              w_glu, b_glu, w_proj_nsa, w_proj_s5, w_out, final_g):
    B, T, _ = x.shape
    G, R, dh = NSA_GROUPS, HEADS_PER_GROUP, HEAD_DIM
    NC = T // CMP_STRIDE - 1
    NS = T // SEL_BLOCK
    NQB = T // Q_BLOCK
    n_top = min(SEL_TOPK, NS)
    scale = HEAD_DIM ** -0.5
    pos = jnp.arange(T)

    c_start = jnp.arange(NC) * CMP_STRIDE
    s_start = jnp.arange(NS) * SEL_BLOCK
    overlap = ((c_start[:, None] < s_start[None, :] + SEL_BLOCK) &
               (c_start[:, None] + CMP_BLOCK > s_start[None, :])).astype(jnp.float32)
    cmp_end = c_start + CMP_BLOCK - 1
    blk = jnp.arange(NS)
    b_ix = jnp.arange(B)[:, None, None, None]
    g_ix = jnp.arange(G)[None, :, None, None]

    for l in range(DEPTH):
        h = rmsnorm(x, norm_g[l])
        proj = h @ w_in[l]
        (q, kc, vc, ksl, vsl, kwi, vwi, gl, gate_nsa, u, gate_s5, mg) = jnp.split(proj, _split_points(), axis=-1)

        q = q.reshape(B, T, G, R, dh)
        qr = rope(q, pos)
        kc, vc = kc.reshape(B, T, G, dh), vc.reshape(B, T, G, dh)
        k_cmp = compress(kc, cmp_pos_k[l], cmp_w1_k[l], cmp_w2_k[l])
        v_cmp = compress(vc, cmp_pos_v[l], cmp_w1_v[l], cmp_w2_v[l])
        ksl = rope(ksl.reshape(B, T, G, dh), pos)
        k_sel = ksl.reshape(B, NS, SEL_BLOCK, G, dh).transpose(0, 3, 1, 2, 4)
        v_sel = vsl.reshape(B, NS, SEL_BLOCK, G, dh).transpose(0, 3, 1, 2, 4)
        kwi = rope(kwi.reshape(B, T, G, dh), pos)
        k_win = jnp.pad(kwi, ((0, 0), (WINDOW, 0), (0, 0), (0, 0)))
        v_win = jnp.pad(vwi.reshape(B, T, G, dh), ((0, 0), (WINDOW, 0), (0, 0), (0, 0)))

        def nsa_block(args):
            qb, q_blk, qr_blk = args
            t = qb * Q_BLOCK + jnp.arange(Q_BLOCK)
            s_c = jnp.einsum('bqgrd,bcgd->bgrqc', q_blk, k_cmp) * scale
            p_cmp = masked_softmax(s_c, cmp_end[None, :] <= t[:, None])
            o_cmp = jnp.einsum('bgrqc,bcgd->bqgrd', p_cmp.astype(v_cmp.dtype), v_cmp)
            imp = jnp.einsum('bgrqc,cn->bgqn', p_cmp, overlap)
            cur = t // SEL_BLOCK
            forced = (blk[None] == 0) | (blk[None] == cur[:, None]) | (blk[None] == cur[:, None] - 1)
            causal_blk = blk[None] * SEL_BLOCK <= t[:, None]
            imp = jnp.where(forced, FORCED_SCORE, jnp.where(causal_blk, imp, -1.0))
            _, idx = lax.top_k(imp, n_top)
            kg = k_sel[b_ix, g_ix, idx]
            vg = v_sel[b_ix, g_ix, idx]
            s_s = jnp.einsum('bqgrd,bgqnkd->bgrqnk', qr_blk, kg) * scale
            kpos = idx[..., None] * SEL_BLOCK + jnp.arange(SEL_BLOCK)
            m_s = (kpos <= t[:, None, None]).reshape(B, G, 1, Q_BLOCK, n_top * SEL_BLOCK)
            p_s = masked_softmax(s_s.reshape(B, G, R, Q_BLOCK, n_top * SEL_BLOCK), m_s)
            o_sel = jnp.einsum('bgrqm,bgqmd->bqgrd', p_s.astype(vg.dtype),
                               vg.reshape(B, G, Q_BLOCK, n_top * SEL_BLOCK, dh))
            start = qb * Q_BLOCK
            kw = lax.dynamic_slice_in_dim(k_win, start, Q_BLOCK + WINDOW, axis=1)
            vw = lax.dynamic_slice_in_dim(v_win, start, Q_BLOCK + WINDOW, axis=1)
            wpos = start - WINDOW + jnp.arange(Q_BLOCK + WINDOW)
            m_w = (wpos[None] <= t[:, None]) & (wpos[None] > t[:, None] - WINDOW) & (wpos[None] >= 0)
            s_w = jnp.einsum('bqgrd,bkgd->bgrqk', qr_blk, kw) * scale
            p_w = masked_softmax(s_w, m_w)
            o_win = jnp.einsum('bgrqk,bkgd->bqgrd', p_w.astype(vw.dtype), vw)
            return (o_cmp, o_sel, o_win)

        q_blocks = q.reshape(B, NQB, Q_BLOCK, G, R, dh).swapaxes(0, 1)
        qr_blocks = qr.reshape(B, NQB, Q_BLOCK, G, R, dh).swapaxes(0, 1)
        o_c, o_s, o_w = lax.map(nsa_block, (jnp.arange(NQB), q_blocks, qr_blocks))
        unblock = lambda o: o.swapaxes(0, 1).reshape(B, T, G, R, dh)
        gates = jax.nn.sigmoid(gl.reshape(B, T, G, R, 3))
        o_nsa = (gates[..., 0:1] * unblock(o_c) + gates[..., 1:2] * unblock(o_s)
                 + gates[..., 2:3] * unblock(o_w)).reshape(B, T, NSA_WIDTH)
        branch_a = (o_nsa * jax.nn.silu(gate_nsa)) @ w_proj_nsa[l]

        y = s5_scan(u, s5_lam_re[l], s5_lam_im[l], s5_log_dt[l], s5_b_re[l], s5_b_im[l],
                    s5_c_re[l], s5_c_im[l], s5_d[l])
        z = jax.nn.gelu(y)
        o_s5 = z * jax.nn.sigmoid(z @ w_glu[l] + b_glu[l])
        branch_b = (o_s5 * jax.nn.silu(gate_s5)) @ w_proj_s5[l]

        mg_a, mg_b = jnp.split(mg, N_BRANCHES, axis=-1)
        merged = jax.nn.sigmoid(mg_a) * branch_a + jax.nn.sigmoid(mg_b) * branch_b
        x = x + merged @ w_out[l]

    return rmsnorm(x, final_g)


_drawn_inputs = setup_inputs


def setup_inputs(seed=0):
    import zlib

    import numpy as np

    out = dict(_drawn_inputs(seed))
    spreads = {}
    factors = {'norm_g': 8.0,
     'cmp_pos_k': 8.0,
     'cmp_pos_v': 6.572,
     'cmp_w1_k': 3.311,
     'cmp_w2_k': 3.319,
     's5_lam_re': 64.0,
     's5_lam_im': 48.568,
     's5_log_dt': 50.04,
     's5_b_re': 64.0,
     's5_b_im': 64.0,
     's5_c_re': 64.0,
     's5_c_im': 64.0,
     'b_glu': 64.0,
     'final_g': 7.978}
    for name, (base, spread) in spreads.items():
        noise = np.random.default_rng([zlib.crc32(name.encode()), seed]).standard_normal(out[name].shape)
        drawn = base * np.exp(spread * noise) if base else spread * noise
        out[name] = __import__('jax').numpy.asarray(drawn.astype(out[name].dtype))
    for name, factor in factors.items():
        out[name] = (out[name] * factor).astype(out[name].dtype)
    return out
```

```python
from contextlib import ExitStack

import concourse.bass as bass
from concourse import mybir

F32 = mybir.dt.float32
F32R = mybir.dt.float32r
ALU = mybir.AluOpType
ACT = mybir.ActivationFunctionType
AX_X = mybir.AxisListType.X

P = 128
T, D = 512, 1024
NT = T // P
KT = D // P
HEADS, GROUPS, DH = 8, 2, 64
HPG = HEADS // GROUPS
NC = 32
S5W = 512
SG, SC, SN = 32, 16, 64
CH = 8
NCH = T // CH
SHIFT = (CH - 1) * SC
GP = SG // 2
EPS = 1.0e-6
BIG = 1.0e30
TWO_PI = 6.283185307179586
MAGIC = 12582912.0
PI_A, PI_B = 6.28125, 0.0019340515136718750
PI_C = TWO_PI - PI_A - PI_B

COL = dict(q=0, kc=512, vc=640, ksl=768, vsl=896, kwi=1024, vwi=1152, gl=1280, gn=1304, u=1816, gs=2328,
           mga=2840, mgb=3864)

NRAW, NSPLIT = 3, 2
BLK = 1024


def weight_blocks():
    b = [(f"u{t}", 1) for t in range(4)] + [(f"q{t}", 1) for t in range(4)]
    b += [(n, 1) for n in ("ksl", "kwi", "kc", "vc", "vsl", "vwi", "gl")]
    b += [(f"w1k{i}", 0) for i in range(4)] + [(f"w1v{i}", 0) for i in range(4)]
    b += [(f"glu{i}", 1) for i in range(2)] + [(f"gs{t}", 1) for t in range(4)] + [(f"gn{t}", 1) for t in range(4)]
    for dp in range(4):
        b += [(f"pb{dp}", 1), (f"mgb{2 * dp}", 1), (f"mgb{2 * dp + 1}", 1)]
        b += [(f"pa{dp}", 1), (f"mga{2 * dp}", 1), (f"mga{2 * dp + 1}", 1)]
    b += [(f"wo{q}_{h}", 1) for q in range(4) for h in range(2)]
    return b


def attention_units():
    return [(i, b, g, r) for i in range(NT) for b in range(2) for g in range(GROUPS) for r in range(HPG)]


FILL = {}
_fill_jobs = [f"glu{t}" for t in range(4)] + [f"gs{t}" for t in range(4)] + [f"gn{t}" for t in range(4)]
for _n, _j in enumerate(_fill_jobs):
    FILL.setdefault(22 + _n * 3, []).append(_j)
D_TERM_AT, GELU_AT, Z_SPLIT_AT = 14, 16, 18


def bank_plan():
    uses, reads, jobs = [0] * 8, [0] * 8, {}

    def use(job, bank, nreads=1, nfills=1):
        before = reads[bank]
        uses[bank] += nfills
        reads[bank] += nreads
        jobs[job] = (bank, before, uses[bank], reads[bank])

    ring = [0]

    def pj(job, nreads=1, banks=tuple(range(8))):
        use(job, banks[ring[0] % len(banks)], nreads)
        ring[0] += 1

    for kt in range(KT):
        pj(f"xT{kt}")
    for r in range(2):
        pj(f"CT{r}", 2)
    for t in range(4):
        pj(f"u{t}")
    for t in range(4):
        pj(f"q{t}", 8)
    for n in ("ksl", "kwi"):
        pj(n, 5)
    for m in range(8):
        pj(f"WT{m}")
    pj("KR0")
    pj("KR1")
    pj("kc", 8)
    for j in range(CH):
        pj(f"TT{j}")
    pj("vc", 8)
    for n in ("vsl", "vwi", "gl"):
        pj(n)
    for m in range(4):
        pj(f"S{m}")
    for n in ("HK", "HV", "KCMP"):
        pj(n)
    pj("VCMP", 4)
    for m in range(2):
        pj(f"SCC{m}")
    for m in range(4):
        pj(f"Y{m}")
    for m in range(2):
        pj(f"PET{m}")
    for i in range(4):
        pj(f"OC{i}")
    ring[0] = 0
    units = attention_units()
    for u in range(len(units) + 3):
        if u < len(units):
            use(f"SC{u}", 2 + u % 2)
        if 0 <= u - 2 < len(units):
            use(f"PT{u - 2}", 4 + u % 2)
        if 0 <= u - 3 < len(units) and (u - 3) % 8 == 0:
            use(f"O{(u - 3) // 8}", 6 + (u - 3) // 8 % 2, nfills=0)
        for j in FILL.get(u, []):
            pj(j, 1, (0, 1))
    ring[0] = 2
    for c in range(4):
        pj(f"OT{c}")
    for dp in range(4):
        for kind in ("B", "MB", "A", "MA"):
            for d in (2 * dp, 2 * dp + 1):
                pj(f"{kind}{d}")
    for q in range(4):
        for m in range(2):
            pj(f"W{q}_{m}")
    return jobs


def build_program(nc, a, out):
    blocks = weight_blocks()
    block_at = {n: k for k, (n, _) in enumerate(blocks)}
    split_at, k_split = {}, 0
    for n, split in blocks:
        if split:
            split_at[n] = k_split
            k_split += 1
    split_names = [n for n, s in blocks if s]
    units = attention_units()
    NU = len(units)
    J = bank_plan()

    ctx = ExitStack()
    with ctx:
        def sb(name, shape, dt=F32):
            return ctx.enter_context(nc.sbuf_tensor(name, shape, dt))

        def shared(name, size, *sets):
            made = {}
            for tensors in sets:
                with ExitStack() as once:
                    for n, shape, dt in tensors:
                        made[n] = once.enter_context(nc.sbuf_tensor(n, shape, dt))
            sb(name, [P, size])
            return made

        hT_hi = sb("hT_hi", [P, KT, T], F32R)
        hT_lo = sb("hT_lo", [P, KT, T], F32R)
        raw = sb("raw", [P, NRAW, BLK])
        w_hi = sb("w_hi", [P, NSPLIT, BLK], F32R)
        w_lo = sb("w_lo", [P, NSPLIT, BLK], F32R)
        m = shared("room_x", 4096,
                   [("x_sb", [P, NT, D], F32)],
                   [("u_perm", [P, 4, CH, NCH], F32), ("o_tok", [P, NT, 512], F32)],
                   [("sg_nsa", [P, 4, T], F32)],
                   [("r_sb", [P, NT, D], F32)])
        x_sb, u_perm, o_tok, sg_nsa, r_sb = (m[n] for n in ("x_sb", "u_perm", "o_tok", "sg_nsa", "r_sb"))
        qr = sb("qr", [P, HPG, T])
        qn = sb("qn", [P, HPG, T])
        m = shared("room_k", 1024, [("bb", [P, 2, GP, SC], F32)], [("kr", [P, 2, T], F32)])
        bb, kr = m["bb"], m["kr"]
        m = shared("room_v", 1024, [("c_nat", [P, 2, 4, SN], F32), ("b_nat", [P, 2, GP, SC], F32)],
                   [("v_tok", [P, NT, 2, P], F32)])
        c_nat, b_nat, v_tok = m["c_nat"], m["b_nat"], m["v_tok"]
        m = shared("room_flat_v", 1024, [("flat_v", [P, 16, GROUPS, NC], F32)], [("e_cmp", [P, NT, HEADS, NC], F32)])
        flat_v, e_cmp = m["flat_v"], m["e_cmp"]
        m = shared("room_flat_k", 1024, [("flat_k", [P, 16, GROUPS, NC], F32)], [("peT", [P, NT, GROUPS, P], F32)],
                   [("gfin", [P, D], F32)])
        flat_k, peT, gfin = m["flat_k"], m["peT"], m["gfin"]
        m = shared("room_s1", 4096,
                   [("W_re", [P, GP, CH, SC], F32), ("W_im", [P, GP, CH, SC], F32)],
                   [("U_sh", [P, SG, NCH], F32), ("Y_sb", [P, SG, NCH], F32)],
                   [("oT_hi", [P, 4, T], F32R), ("oT_lo", [P, 4, T], F32R)])
        W, U_sh, Y_sb, oT_hi, oT_lo = (m["W_re"], m["W_im"]), m["U_sh"], m["Y_sb"], m["oT_hi"], m["oT_lo"]
        m = shared("room_s2", 4096,
                   [("E_re", [P, GP, CH, SC], F32), ("E_nim", [P, GP, CH, SC], F32)],
                   [("prob", [P, 3, T], F32), ("probT", [P, 2, T], F32), ("o_part", [P, T], F32)],
                   [("m_hi", [P, KT, T], F32R)])
        E, prob, probT, o_part, m_hi = (m["E_re"], m["E_nim"]), m["prob"], m["probT"], m["o_part"], m["m_hi"]
        m = shared("room_s3", 4096,
                   [("WT_re", [P, GP, P], F32), ("WT_im", [P, GP, P], F32)],
                   [("z_hi", [P, 4, T], F32R), ("z_lo", [P, 4, T], F32R)],
                   [("m_lo", [P, KT, T], F32R)])
        WT, z_hi, z_lo, m_lo = (m["WT_re"], m["WT_im"]), m["z_hi"], m["z_lo"], m["m_lo"]
        m = shared("room_s4", 4096,
                   [("pr_a", [P, GP, CH, SC], F32), ("pr_b", [P, GP, CH, SC], F32)],
                   [("TT", [P, SG, CH, SC], F32)],
                   [("f_hi", [P, 4, T], F32R), ("f_lo", [P, 4, T], F32R)])
        pr_a, pr_b, TT, f_hi, f_lo = m["pr_a"], m["pr_b"], m["TT"], m["f_hi"], m["f_lo"]
        m = shared("room_t", 2080,
                   [("rope", [P, 4, T], F32)],
                   [("X", [P, 2, GP, NCH + 1], F32)],
                   [("z", [P, 4, T], F32)])
        rope, X, z = m["rope"], m["X"], m["z"]
        m = shared("room_m", 2048,
                   [("swapped", [P, 4, T], F32)],
                   [("sx_a", [P, 1024], F32), ("sx_b", [P, 1024], F32)],
                   [("yT", [P, 4, T], F32)],
                   [("tmp", [P, 4, T], F32)])
        swapped, sx_a, sx_b, yT, tmp = m["swapped"], m["sx_a"], m["sx_b"], m["yT"], m["tmp"]
        v_blk = sb("v_blk", [P, GROUPS, HPG * DH])
        KR = sb("KR", [P, SG, SC])
        causal = sb("causal", [P, T])
        ident_wide = sb("ident_wide", [P, SHIFT + P])
        ident = ident_wide[:, SHIFT:SHIFT + P]
        CT = sb("CT", [P, 2, GP, SC])
        s5p = sb("s5p", [P, 24, GP])
        pw = sb("pw", [P, 2, CH, GP])
        pq = sb("pq", [P, 2, CH, GP])
        pwt = sb("pwt", [P, 2, CH, GP])
        hid = sb("hid", [P, 2, 2, GROUPS * NC])
        w2 = sb("w2", [P, 2, 2, DH])
        kcT = sb("kcT", [P, NC])
        pos = sb("pos", [P, 2, 16])
        cmask = sb("cmask", [P, 2, NT, NC])
        gate = sb("gate", [P, NT, HEADS, 3])
        nmax_c = sb("nmax_c", [P, NT, HEADS])
        den_c = sb("den_c", [P, NT, HEADS])
        coef_c = sb("coef_c", [P, NT, HEADS])
        nmax = sb("nmax", [P, NU])
        den = sb("den", [P, NU])
        coef = sb("coef", [P, NU])
        g_in = sb("g_in", [P, KT])
        d_col = sb("d_col", [P, 4])
        bias_glu = sb("bias_glu", [P, 4])
        half_bias = sb("half_bias", [P, 4])
        rms = sb("rms", [P, 6, NT])
        ssq4 = sb("ssq4", [P, NT, 4])

        bank = [ctx.enter_context(nc.psum_tensor(f"bank{i}", [P, 512], F32)) for i in range(8)]

        def sem(name):
            return ctx.enter_context(nc.semaphore(name))

        filled = [sem(f"bank{i}_filled") for i in range(8)]
        drained = [sem(f"bank{i}_drained") for i in range(8)]
        x_in, consts_in, s5_in, cmp_in, x_again, gfin_in, g_in_loaded = (sem(n) for n in (
            "x_in", "consts_in", "s5_in", "cmp_in", "x_again", "gfin_in", "g_in_loaded"))
        raw_full = [sem(f"raw{i}_full") for i in range(NRAW)]
        hi_done, lo_done, part_used = (sem(n) for n in ("w_hi_done", "w_lo_done", "w_part_used"))
        ssq_done, var_done, sqrt_done, xs_done, hhi_done = (sem(n) for n in (
            "ssq_done", "variance_done", "sqrt_done", "x_scaled", "hT_hi_done"))
        dve, act = sem("dve_chain"), sem("act_chain")
        s5_dt, s5_arg, s5_act, w_built, e_built = (sem(n) for n in (
            "s5_dt", "s5_arguments", "s5_functions", "W_built", "E_built"))
        u_out, u_in, scan_done, y_out, y_in, yd_done, z_done, z_split = (sem(n) for n in (
            "u_scratch_out", "U_in", "scan_done", "y_scratch_out", "y_in", "y_with_D", "z_done",
            "z_split"))
        qr_done, kr_done, gate_done, flat_zero, vz_done = (sem(n) for n in (
            "q_roped", "k_roped", "gates_done", "flat_zeroed", "v_blk_zeroed"))
        cs_done, ce_done, cm_done, p_done, pv_done, o_done = (sem(n) for n in (
            "cmp_shifted", "cmp_exp", "cmp_masked", "prob_done", "pv_done", "o_tok_done"))
        bias_done, th_done, f_split, oT_split, m_split, r_done, fin_sq, fin_var, fin_sqrt, y_ready, stored = (sem(n) for n in (
            "half_bias_done", "tanh_done", "f_split", "oT_split", "merged_split", "residual_done", "final_squares", "final_variance",
            "final_sqrt", "out_ready", "stored"))

        u_scr = nc.dram_tensor("u_scratch", (S5W, CH, NCH), F32, kind="Internal").ap()
        y_scr = nc.dram_tensor("y_scratch", (S5W, CH, NCH), F32, kind="Internal").ap()

        def bk(job):
            return bank[J[job][0]]

        def open_bank(eng, job):
            b, before, _, _ = J[job]
            if before:
                eng.wait_ge(drained[b], before)

        def fill(ins, job):
            ins.then_inc(filled[J[job][0]], 1)

        def wait_fill(eng, job):
            b, _, fills, _ = J[job]
            eng.wait_ge(filled[b], fills)

        def drain(ins, job):
            ins.then_inc(drained[J[job][0]], 1)

        def wait_drained(eng, job):
            b, _, _, reads = J[job]
            eng.wait_ge(drained[b], reads)

        def last_job(name):
            base = name.rstrip("0123456789")
            n = name[len(base):]
            if base == "glu":
                return f"glu{2 * int(n) + 1}"
            if base in ("pa", "pb"):
                return f"{base[1].upper()}{2 * int(n) + 1}"
            if base in ("mga", "mgb"):
                return f"M{base[2].upper()}{n}"
            if name[:3] == "w1k" or name[:3] == "w1v":
                return f"H{name[2].upper()}" if name[3] == "3" else None
            if name[:2] == "wo":
                return f"W{name[2]}_1" if name[4] == "1" else None
            return name

        part_at = {n: k + 1 for k, n in enumerate(n for n, _ in blocks if last_job(n) is None)}

        def wait_used(eng, name):
            if last_job(name) is None:
                eng.wait_ge(part_used, part_at[name])
            else:
                wait_fill(eng, last_job(name))

        def slot(name):
            return split_at[name] % NSPLIT

        def block_source(name):
            w_in = a["w_in"][0]
            if name[:3] == "w1k" or name[:3] == "w1v":
                w, i = a["cmp_w1_" + name[2]][0], int(name[3])
                return w.rearrange("(kt p) n -> p kt n", p=P)[:, 4 * i:4 * i + 4, :], (4, 256)
            if name[:3] == "glu":
                i = int(name[3])
                return a["w_glu"][0].rearrange("(kt p) n -> p kt n", p=P)[:, :, 256 * i:256 * i + 256], (4, 256)
            if name[:2] in ("pa", "pb"):
                w, i = a["w_proj_nsa" if name[1] == "a" else "w_proj_s5"][0], int(name[2])
                return w.rearrange("(kt p) n -> p kt n", p=P)[:, :, 256 * i:256 * i + 256], (4, 256)
            if name[:2] == "wo":
                q, h = int(name[2]), int(name[4])
                w = a["w_out"][0].rearrange("(kt p) n -> p kt n", p=P)
                return w[:, 4 * h:4 * h + 4, 256 * q:256 * q + 256], (4, 256)
            base = name.rstrip("0123456789")
            c = COL[base] + 128 * int(name[len(base):] or 0)
            n = 24 if name == "gl" else 128
            return w_in.rearrange("(kt p) n -> p kt n", p=P)[:, :, c:c + n], (KT, n)

        def view(buf, s, dims):
            return buf[:, s, 0:dims[0] * dims[1]].rearrange("p (k n) -> p k n", n=dims[1])

        def wdims(name):
            return block_source(name)[1]

        ctx.enter_context(nc.allow_non_contiguous_dma(reason="small parameter vectors, one element per partition"))
        block = ctx.enter_context(nc.Block())

        @block.sync
        def _(sp):
            sp.dma_start(x_sb[:, :, :], a["x"][0].rearrange("(i p) d -> p i d", p=P)).then_inc(x_in, 16)

            def u_to_scratch():
                for t in range(4):
                    wait_drained(sp, f"u{t}")
                    sp.dma_start(u_scr[P * t:P * t + P], u_perm[:, t]).then_inc(u_out, 16)

            def u_from_scratch():
                sp.wait_ge(u_out, 64)
                for m in range(8):
                    wait_drained(sp, f"WT{m}")
                wait_drained(sp, "KR0")
                wait_drained(sp, "KR1")
                by_pos = u_scr.rearrange("(g c) s k -> s c g k", c=SC)
                for e in range(CH):
                    sp.dma_start(U_sh[SC * e:SC * e + SC], by_pos[CH - 1 - e]).then_inc(u_in, 16)

            def y_through_scratch():
                for m in range(4):
                    wait_drained(sp, f"Y{m}")
                by_pos = y_scr.rearrange("(g c) s k -> s c g k", c=SC)
                for j in range(CH):
                    sp.dma_start(by_pos[j], Y_sb[SC * j:SC * j + SC]).then_inc(y_out, 16)
                sp.wait_ge(y_out, 16 * CH)
                sp.wait_ge(scan_done, 1)
                sp.dma_start(yT[:, :, :], y_scr.rearrange("(t p) s k -> p t (s k)", p=P)).then_inc(y_in, 16)

            for k, (name, split) in enumerate(blocks):
                if k >= NRAW:
                    before, was_split = blocks[k - NRAW]
                    if was_split:
                        sp.wait_ge(lo_done, split_at[before] + 1)
                    else:
                        wait_used(sp, before)
                src, dims = block_source(name)
                sp.dma_start(view(raw, k % NRAW, dims), src).then_inc(raw_full[k % NRAW], 16)
                if name == "q3":
                    u_to_scratch()
                if name == "vc":
                    u_from_scratch()
                if name == "glu1":
                    y_through_scratch()
                if name == "pa1":
                    sp.wait_ge(oT_split, 4)
                    sp.dma_start(r_sb[:, :, :], a["x"][0].rearrange("(i p) d -> p i d", p=P)).then_inc(x_again, 16)
                    sp.dma_start(gfin[:, :], a["final_g"].partition_broadcast(P)).then_inc(gfin_in, 16)
            for i in range(NT):
                sp.wait_ge(y_ready, i + 1)
                sp.dma_start(out[0, P * i:P * i + P, :], r_sb[:, i, :]).then_inc(stored, 16)
            sp.wait_ge(stored, 16 * NT)

        @block.gpsimd
        def _(pl):
            nc.gpsimd.memset(flat_k[:, :, :, NC - 1:NC], 0.0).then_inc(flat_zero, 1)
            nc.gpsimd.memset(flat_v[:, :, :, NC - 1:NC], 0.0).then_inc(flat_zero, 1)
            nc.gpsimd.memset(v_blk[:, :, :], 0.0).then_inc(vz_done, 1)
            for j, name in enumerate(split_names):
                pl.wait_ge(hi_done, j + 1)
                dims, k = wdims(name), block_at[name]
                w = view(raw, k % NRAW, dims)
                nc.gpsimd.tensor_tensor(view(w_lo, j % NSPLIT, dims), w, view(w_hi, j % NSPLIT, dims).bitcast(F32),
                                        ALU.subtract).then_inc(lo_done, 1)

        @block.scalar
        def _(ac):
            def load(dst, src, s):
                ac.dma_start(dst, src).then_inc(s, 16)

            load(ident_wide[:, :], a["ident"], consts_in)
            load(g_in[:, :], a["norm_g"][0].rearrange("(k p) -> p k", p=P), g_in_loaded)
            for r, n in enumerate(("s5_lam_re", "s5_lam_im")):
                flat = a[n][0].rearrange("g p -> (g p)")
                load(s5p[:, r, :], flat.rearrange("(q p) -> p q", p=P), s5_in)
            dt2 = a["s5_log_dt"][0].rearrange("(q r) -> r q", r=2)
            for par in range(2):
                load(s5p[SN * par:SN * par + SN, 2, :], dt2[par].partition_broadcast(SN), s5_in)
            for r, n in enumerate(("s5_b_re", "s5_b_im")):
                flat = a[n][0].rearrange("g p c -> (g p) c")
                load(b_nat[:, r], flat.rearrange("(q p) c -> p q c", p=P), s5_in)
            for r, n in enumerate(("s5_c_re", "s5_c_im")):
                load(c_nat[:, r], a[n][0].rearrange("g c p -> (g c) p").rearrange("(t q) p -> q t p", q=P), s5_in)
            load(rope[:, :, :], a["rope"], consts_in)
            load(causal[:, :], a["causal"], consts_in)
            load(cmask[:, :, :, :], a["cmask"], consts_in)
            for r, n in enumerate("kv"):
                load(w2[:, r], a["cmp_w2_" + n][0].rearrange("(h p) d -> p h d", p=P), cmp_in)
                pv = a["cmp_pos_" + n][0].rearrange("(k j) d -> j d k", j=2)
                for jp in range(2):
                    load(pos[DH * jp:DH * jp + DH, r, :], pv[jp], cmp_in)
            load(d_col[:, :], a["s5_d"][0].rearrange("(t p) -> p t", p=P), cmp_in)
            load(bias_glu[:, :], a["b_glu"][0].rearrange("(t p) -> p t", p=P), cmp_in)

            def split_hi(j):
                name = split_names[j]
                dims, k = wdims(name), block_at[name]
                ac.wait_ge(raw_full[k % NRAW], 16 * (k // NRAW + 1))
                if j >= NSPLIT:
                    wait_used(ac, split_names[j - NSPLIT])
                nc.scalar.activation(view(w_hi, j % NSPLIT, dims), view(raw, k % NRAW, dims), ACT.Copy)\
                    .then_inc(hi_done, 1)

            def after(name):
                if split_at[name] + NSPLIT < len(split_names):
                    split_hi(split_at[name] + NSPLIT)

            def evacuate(job, dst, src, func=ACT.Copy, **kw):
                wait_fill(ac, job)
                drain(nc.scalar.activation(dst, src, func, **kw), job)

            ac.wait_ge(x_in, 16)
            for i in range(NT):
                junk = (qr, qn)[i // 2][:, 2 * (i % 2):2 * (i % 2) + 2, :].rearrange("p a b -> p (a b)")
                nc.scalar.activation(junk, x_sb[:, i, :], ACT.Square, accum_out=rms[:, 0, i:i + 1]).then_inc(ssq_done, 1)
            ac.wait_ge(var_done, 1)
            nc.scalar.activation(rms[:, 2, :], rms[:, 1, :], ACT.Sqrt).then_inc(sqrt_done, 1)
            split_hi(0)
            split_hi(1)
            ac.wait_ge(s5_in, 16 * 8)
            nc.scalar.activation(s5p[:, 3, :], s5p[:, 2, :], ACT.Exp).then_inc(s5_dt, 1)
            ac.wait_ge(g_in_loaded, 16)
            for kt in range(KT):
                wait_fill(ac, f"xT{kt}")
                nc.scalar.activation(hT_hi[:, kt, :], bk(f"xT{kt}")[:, :], ACT.Copy, scale=g_in[:, kt:kt + 1])\
                    .then_inc(hhi_done, 1)
            ac.wait_ge(s5_arg, 1)
            nc.scalar.activation(s5p[:, 6, :], s5p[:, 4, :], ACT.Exp).then_inc(s5_act, 1)
            nc.scalar.activation(s5p[:, 7, :], s5p[:, 5, :], ACT.Sin).then_inc(s5_act, 1)
            nc.scalar.activation(s5p[:, 8, :], s5p[:, 5, :], ACT.Sin, scale=0.5).then_inc(s5_act, 1)

            for t in range(4):
                evacuate(f"u{t}", u_perm[:, t], bk(f"u{t}")[:, :].rearrange("p (k s) -> p s k", s=CH))
                after(f"u{t}")
            for t in range(4):
                g = t // 2
                for half in range(2):
                    evacuate(f"q{t}", qn[DH * g:DH * g + DH, 2 * (t % 2) + half, :],
                             bk(f"q{t}")[DH * half:DH * half + DH, :], scale=-0.125)
                after(f"q{t}")
            after("ksl")
            after("kwi")
            for m in range(0, 8, 2):
                evacuate(f"WT{m}", WT[m // 4][:, 4 * (m % 4):4 * (m % 4) + 4, :].rearrange("p a b -> p (a b)"),
                         bk(f"WT{m}")[:, :])
            for par in range(2):
                evacuate(f"KR{par}", KR[:, par::2, :], bk(f"KR{par}")[:, 0:GP * SC].rearrange("p (q c) -> p q c", c=SC))
            after("kc")
            ac.wait_ge(w_built, 1)
            ac.wait_ge(e_built, 1)
            for j in range(CH):
                evacuate(f"TT{j}", TT[:, :, j, :], bk(f"TT{j}")[:, :].rearrange("p (g c) -> p g c", c=SC))
            after("vc")
            for b, n in enumerate(("vsl", "vwi")):
                evacuate(n, v_tok[:, :, b, :], bk(n)[:, :].rearrange("p (i c) -> p i c", i=NT))
                if b == 0:
                    after(n)
            evacuate("gl", gate[:, :, :, :].rearrange("p i h b -> p (i h b)"), bk("gl")[:, 0:NT * 24], ACT.Tanh, scale=0.5)
            ac.wait_ge(kr_done, 2)
            for m in range(4):
                hf, ri = m // 2, m % 2
                evacuate(f"S{m}", X[:, ri, 8 * hf:8 * hf + 8, 1:NCH + 1],
                         bk(f"S{m}")[:, :].rearrange("p (q k) -> p q k", k=NCH))
            for r, n in enumerate(("HK", "HV")):
                evacuate(n, hid[:, r].rearrange("p h n -> p (h n)"), bk(n)[:, 0:128], ACT.Gelu_apprx_tanh)
            after("vwi")
            after("gl")
            evacuate("KCMP", kcT[:, :], bk("KCMP")[:, 0:NC])
            for g in range(GROUPS):
                ac.wait_ge(cs_done, g + 1)
                e = e_cmp[:, :, HPG * g:HPG * g + HPG, :]
                nc.scalar.activation(e, e, ACT.Exp, scale=-1.0).then_inc(ce_done, 1)
            for m in range(4):
                first = 16 * (m // 2) + m % 2
                evacuate(f"Y{m}", Y_sb[:, first:first + 15:2, :], bk(f"Y{m}")[:, :].rearrange("p (q k) -> p q k", k=NCH))
            for m in range(2):
                evacuate(f"PET{m}", peT[:, 2 * m:2 * m + 2].rearrange("p a b c -> p (a b c)"), bk(f"PET{m}")[:, :])

            tanh_user = [None]

            def tanh_free(user):
                if tanh_user[0]:
                    wait_drained(ac, tanh_user[0])
                tanh_user[0] = user

            def fill_part(job):
                kind, t = job[:-1], int(job[-1])
                wait_fill(ac, job)
                tanh_free(job)
                bias = half_bias[:, t:t + 1] if kind == "glu" else 0.0
                nc.scalar.activation(tmp[:, 0, :], bk(job)[:, :], ACT.Tanh, scale=0.5, bias=bias).then_inc(th_done, 1)
                if kind != "glu":
                    after(job)
                elif t % 2:
                    after(f"glu{t // 2}")

            ac.wait_ge(bias_done, 1)
            for u in range(NU + 3):
                if u < NU:
                    n = P * (units[u][0] + 1)
                    wait_drained(ac, f"SC{u}")
                    nc.scalar.activation(prob[:, u % 3, 0:n], prob[:, u % 3, 0:n], ACT.Exp, scale=-1.0,
                                         bias=nmax[:, u:u + 1], accum_out=den[:, u:u + 1]).then_inc(p_done, 1)
                if u == GELU_AT:
                    wait_fill(ac, "Y3")
                    for t in range(4):
                        ac.wait_ge(yd_done, t + 1)
                        nc.scalar.activation(z[:, t, :].rearrange("p (k j) -> p j k", j=CH),
                                             yT[:, t, :].rearrange("p (j k) -> p j k", k=NCH),
                                             ACT.Gelu_apprx_tanh).then_inc(z_done, 1)
                    ac.wait_ge(z_done, 4)
                for job in FILL.get(u, []):
                    fill_part(job)
            for dp in range(4):
                for kind, user in (("MB", "B"), ("MA", "A")):
                    for d in (2 * dp, 2 * dp + 1):
                        if d % 2 == 0:
                            after(f"p{user.lower()}{dp}")
                        wait_fill(ac, f"{kind}{d}")
                        tanh_free(f"{user}{d}")
                        drain(nc.scalar.activation(tmp[:, 0, :], bk(f"{kind}{d}")[:, :], ACT.Tanh, scale=0.5), f"{kind}{d}")
                        after(f"mg{user.lower()}{d}")
            for q in range(4):
                after(f"wo{q}_0")
                after(f"wo{q}_1")
                for i in range(NT):
                    ac.wait_ge(r_done, 2 * q + i // 2 + 1)
                    junk = (qr, qn)[q // 2][:, 2 * (q % 2) + i // 2, 256 * (i % 2):256 * (i % 2) + 256]
                    nc.scalar.activation(junk, r_sb[:, i, 256 * q:256 * q + 256], ACT.Square,
                                         accum_out=ssq4[:, i, q:q + 1]).then_inc(fin_sq, 1)
            ac.wait_ge(fin_var, 1)
            nc.scalar.activation(rms[:, 2, :], rms[:, 1, :], ACT.Sqrt).then_inc(fin_sqrt, 1)

        @block.tensor
        def _(pe):
            def mm3(dst, w, x, first, last):
                nc.tensor.matmul(dst, w[0], x[1], start=first, stop=False, skip_group_check=True)
                nc.tensor.matmul(dst, w[1], x[0], start=False, stop=False, skip_group_check=True)
                return nc.tensor.matmul(dst, w[0], x[0], start=False, stop=last, skip_group_check=True)

            def weights(name):
                pe.wait_ge(lo_done, split_at[name] + 1)
                dims = wdims(name)
                return [view(w, slot(name), dims) for w in (w_hi, w_lo)]

            def hT(kt, cols=slice(0, T)):
                return hT_hi[:, kt, cols], hT_lo[:, kt, cols]

            def channel_major(job, name):
                w = weights(name)
                open_bank(pe, job)
                for kt in range(KT):
                    ins = mm3(bk(job)[:, :], [v[:, kt, :] for v in w], hT(kt), kt == 0, kt == KT - 1)
                fill(ins, job)

            def token_major(job, name):
                w = weights(name)
                n = wdims(name)[1]
                open_bank(pe, job)
                for i in range(NT):
                    for kt in range(KT):
                        ins = mm3(bk(job)[:, n * i:n * i + n], hT(kt, slice(P * i, P * i + P)), [v[:, kt, :] for v in w],
                                  kt == 0, kt == KT - 1)
                fill(ins, job)

            def half_block(job, name, x, cols):
                w = weights(name)
                open_bank(pe, job)
                for kt in range(4):
                    ins = mm3(bk(job)[:, :], [v[:, kt, cols:cols + P] for v in w], [v[:, kt, :] for v in x], kt == 0, kt == 3)
                fill(ins, job)

            def four_transposes(job, sources):
                open_bank(pe, job)
                for n, src in enumerate(sources):
                    ins = nc.tensor.transpose(bk(job)[:, P * n:P * n + P], src, ident)
                fill(ins, job)

            pe.wait_ge(consts_in, 16 * 4)
            pe.wait_ge(xs_done, NT)
            for kt in range(KT):
                four_transposes(f"xT{kt}", [x_sb[:, i, P * kt:P * kt + P] for i in range(NT)])
            pe.wait_ge(s5_in, 16 * 8)
            for r in range(2):
                open_bank(pe, f"CT{r}")
                for t in range(4):
                    ins = nc.tensor.transpose(bk(f"CT{r}")[0:SN, P * t:P * t + P], c_nat[:, r, t, :], ident)
                fill(ins, f"CT{r}")
            wait_drained(pe, f"xT{KT - 1}")
            for kt in range(KT):
                wait_drained(pe, f"xT{kt}")
            for n in ("u0", "u1", "u2", "u3", "q0", "q1", "q2", "q3", "ksl", "kwi"):
                channel_major(n, n)
            pe.wait_ge(w_built, 1)
            for m in range(8):
                four_transposes(f"WT{m}", [W[m // 4][:, 4 * (m % 4) + n].rearrange("p e c -> p (e c)") for n in range(4)])
            for par in range(2):
                rows = slice(SN * par, SN * par + SN)
                open_bank(pe, f"KR{par}")
                for gp in range(GP):
                    dst = bk(f"KR{par}")[:, SC * gp:SC * gp + SC]
                    for ri in range(2):
                        ins = nc.tensor.matmul(dst, W[ri][rows, gp].rearrange("p e c -> p (e c)"), CT[rows, ri, gp, :],
                                               start=(ri == 0), stop=(ri == 1), skip_group_check=True)
                fill(ins, f"KR{par}")
            channel_major("kc", "kc")
            wait_drained(pe, "KR0")
            wait_drained(pe, "KR1")
            for j in range(CH):
                open_bank(pe, f"TT{j}")
                fill(nc.tensor.matmul(bk(f"TT{j}")[:, :], ident_wide[:, SC * j:SC * j + P],
                                      KR[:, :, :].rearrange("p g c -> p (g c)"), start=True, stop=True), f"TT{j}")
            channel_major("vc", "vc")
            for n in ("vsl", "vwi", "gl"):
                token_major(n, n)
            pe.wait_ge(u_in, 16 * CH)
            for m in range(4):
                hf, ri = m // 2, m % 2
                open_bank(pe, f"S{m}")
                if m == 0:
                    for k in range(8):
                        wait_drained(pe, f"WT{k}")
                for par in range(2):
                    for k in range(8):
                        gp = 8 * hf + k
                        ins = nc.tensor.matmul(bk(f"S{m}")[SN * par:SN * par + SN, NCH * k:NCH * k + NCH],
                                               WT[ri][:, gp, SN * par:SN * par + SN], U_sh[:, 2 * gp + par, :],
                                               start=True, stop=True, skip_group_check=True)
                fill(ins, f"S{m}")
            pe.wait_ge(flat_zero, 2)
            for r, (n, flat) in enumerate((("k", flat_k), ("v", flat_v))):
                job = "H" + n.upper()
                wait_drained(pe, {"k": "kc", "v": "vc"}[n])
                open_bank(pe, job)
                for i in range(4):
                    k = block_at[f"w1{n}{i}"]
                    pe.wait_ge(raw_full[k % NRAW], 16 * (k // NRAW + 1))
                    w1 = view(raw, k % NRAW, (4, 256))
                    for kk in range(4):
                        for half in range(2):
                            first, last = i == 0 and kk == 0, i == 3 and kk == 3
                            ins = nc.tensor.matmul(bk(job)[:, 64 * half:64 * half + 64], w1[:, kk, P * half:P * half + P],
                                                   flat[:, 4 * i + kk].rearrange("p g n -> p (g n)"),
                                                   start=first and half == 0, stop=last, skip_group_check=True)
                    if i < 3:
                        ins.then_inc(part_used, 1)
                fill(ins, job)
            pe.wait_ge(cmp_in, 16 * 8)
            wait_drained(pe, "HK")
            open_bank(pe, "KCMP")
            for g in range(GROUPS):
                for half in range(2):
                    ins = nc.tensor.matmul(bk("KCMP")[DH * g:DH * g + DH, 0:NC], w2[:, 0, half, :],
                                           hid[:, 0, half, NC * g:NC * g + NC], start=(half == 0), stop=(half == 1))
            fill(ins, "KCMP")
            wait_drained(pe, "HV")
            open_bank(pe, "VCMP")
            for r in range(HPG):
                for g in range(GROUPS):
                    for half in range(2):
                        ins = nc.tensor.matmul(bk("VCMP")[NC * r:NC * r + NC, DH * g:DH * g + DH],
                                               hid[:, 1, half, NC * g:NC * g + NC], w2[:, 1, half, :],
                                               start=(half == 0), stop=(half == 1))
            fill(ins, "VCMP")
            wait_drained(pe, "KCMP")
            for t in range(4):
                wait_drained(pe, f"q{t}")
            for g in range(GROUPS):
                open_bank(pe, f"SCC{g}")
                rows = slice(DH * g, DH * g + DH)
                for i in range(NT):
                    for r in range(HPG):
                        c = (i * HPG + r) * NC
                        ins = nc.tensor.matmul(bk(f"SCC{g}")[:, c:c + NC], qn[rows, r, P * i:P * i + P], kcT[rows, :],
                                               start=True, stop=True, skip_group_check=True)
                fill(ins, f"SCC{g}")
            for j in range(CH):
                wait_drained(pe, f"TT{j}")
            pe.wait_ge(scan_done, 1)
            pe.wait_ge(e_built, 1)
            for m in range(4):
                par, gps = m % 2, range(8 * (m // 2), 8 * (m // 2) + 8)
                rows = slice(SN * par, SN * par + SN)
                open_bank(pe, f"Y{m}")
                yb = bk(f"Y{m}")
                for k, gp in enumerate(gps):
                    nc.tensor.matmul(yb[:, NCH * k:NCH * k + NCH], TT[:, 2 * gp + par, :, :].rearrange("p j c -> p (j c)"),
                                     U_sh[:, 2 * gp + par, :], start=(k == 0), stop=False, skip_group_check=True)
                for k, gp in enumerate(gps):
                    for ri in range(2):
                        ins = nc.tensor.matmul(yb[:, NCH * k:NCH * k + NCH],
                                               E[ri][rows, gp].rearrange("p j c -> p (j c)"), X[rows, ri, gp, 0:NCH],
                                               start=False, stop=(ri == 1), skip_group_check=True)
                fill(ins, f"Y{m}")
            for m in range(2):
                pe.wait_ge(cm_done, GROUPS)
                four_transposes(f"PET{m}", [e_cmp[:, 2 * m + ii, HPG * g:HPG * g + HPG, :].rearrange("p h c -> p (h c)")
                                            for ii in range(2) for g in range(GROUPS)])
            wait_drained(pe, "VCMP")
            for i in range(NT):
                wait_drained(pe, f"PET{i // 2}")
                open_bank(pe, f"OC{i}")
                for g in range(GROUPS):
                    ins = nc.tensor.matmul(bk(f"OC{i}")[:, 256 * g:256 * g + 256], peT[:, i, g, :], v_blk[:, g, :],
                                           start=True, stop=True, skip_group_check=True)
                fill(ins, f"OC{i}")

            def scores(u):
                i, b, g, r = units[u]
                rows = slice(DH * g, DH * g + DH)
                open_bank(pe, f"SC{u}")
                fill(nc.tensor.matmul(bk(f"SC{u}")[:, 0:P * (i + 1)], qr[rows, r, P * i:P * i + P],
                                      kr[rows, b, 0:P * (i + 1)], start=True, stop=True), f"SC{u}")

            def transposes(u):
                i = units[u][0]
                pe.wait_ge(p_done, u + 1)
                open_bank(pe, f"PT{u}")
                for kt in range(i + 1):
                    ins = nc.tensor.transpose(bk(f"PT{u}")[:, P * kt:P * kt + P], prob[:, u % 3, P * kt:P * kt + P],
                                              ident)
                fill(ins, f"PT{u}")

            def weighted_values(u):
                i, b, g, r = units[u]
                wait_drained(pe, f"PT{u}")
                if u % 8 == 0:
                    open_bank(pe, f"O{u // 8}")
                h = g * HPG + r
                for kt in range(i + 1):
                    ins = nc.tensor.matmul(bk(f"O{u // 8}")[:, DH * h:DH * h + DH], probT[:, u % 2, P * kt:P * kt + P],
                                           v_tok[:, kt, b, DH * g:DH * g + DH], start=(kt == 0), stop=(kt == i))
                ins.then_inc(pv_done, 1)

            pe.wait_ge(qr_done, 8)
            pe.wait_ge(kr_done, 2)
            wait_drained(pe, "vsl")
            wait_drained(pe, "vwi")
            for u in range(NU + 3):
                if u < NU:
                    scores(u)
                if 0 <= u - 2 < NU:
                    transposes(u - 2)
                if 0 <= u - 3 < NU:
                    weighted_values(u - 3)
                for job in FILL.get(u, []):
                    kind, t = job[:-1], int(job[-1])
                    if kind == "glu":
                        pe.wait_ge(z_split, 4)
                        half_block(job, f"glu{t // 2}", (z_hi, z_lo), P * (t % 2))
                    else:
                        channel_major(job, job)
            pe.wait_ge(o_done, NT)
            for c in range(4):
                four_transposes(f"OT{c}", [o_tok[:, i, P * c:P * c + P] for i in range(NT)])
            for dp in range(4):
                pe.wait_ge(f_split, 4)
                for d in (2 * dp, 2 * dp + 1):
                    half_block(f"B{d}", f"pb{dp}", (f_hi, f_lo), P * (d % 2))
                for d in (2 * dp, 2 * dp + 1):
                    channel_major(f"MB{d}", f"mgb{d}")
                pe.wait_ge(oT_split, 4)
                for d in (2 * dp, 2 * dp + 1):
                    half_block(f"A{d}", f"pa{dp}", (oT_hi, oT_lo), P * (d % 2))
                for d in (2 * dp, 2 * dp + 1):
                    channel_major(f"MA{d}", f"mga{d}")
            for q in range(4):
                for h in range(2):
                    w = weights(f"wo{q}_{h}")
                    for m in range(2):
                        job = f"W{q}_{m}"
                        if h == 0:
                            open_bank(pe, job)
                        for ii in range(2):
                            i = 2 * m + ii
                            for kk in range(4):
                                kt = 4 * h + kk
                                pe.wait_ge(m_split, kt + 1) if q == 0 and m == 0 and ii == 0 else None
                                x = [v[:, kt, P * i:P * i + P] for v in (m_hi, m_lo)]
                                ins = mm3(bk(job)[:, 256 * ii:256 * ii + 256], x, [v[:, kk, :] for v in w],
                                          kt == 0 and ii == 0, kt == KT - 1)
                        if h == 1:
                            fill(ins, job)
                    if h == 0:
                        ins.then_inc(part_used, 1)

        @block.vector
        def _(ve):
            V = nc.vector
            chain = [0]

            def link(ins):
                chain[0] += 1
                ins.then_inc(dve, 1)
                ve.wait_ge(dve, chain[0])

            def tt(o, x, y, op):
                link(V.tensor_tensor(o, x, y, op))

            def ts(o, x, s1, s2, op0, op1=None):
                link(V.tensor_scalar(o, x, s1, s2, op0, op1) if op1 is not None else V.tensor_scalar(o, x, s1, None, op0))

            def stt(o, x, s, y, op0, op1):
                link(V.scalar_tensor_tensor(out=o, in0=x, scalar=s, in1=y, op0=op0, op1=op1))

            MUL, ADD, SUB = ALU.mult, ALU.add, ALU.subtract

            def inverse_root(signal_var, signal_sqrt):
                V.tensor_scalar(rms[:, 1, :], rms[:, 0, :], 1.0 / D, EPS, MUL, ADD).then_inc(signal_var, 1)
                ve.wait_ge(signal_sqrt, 1)
                link(V.reciprocal(rms[:, 3, :], rms[:, 2, :]))
                tt(rms[:, 4, :], rms[:, 3, :], rms[:, 3, :], MUL)
                tt(rms[:, 4, :], rms[:, 4, :], rms[:, 1, :], MUL)
                ts(rms[:, 4, :], rms[:, 4, :], -0.5, 1.5, MUL, ADD)
                tt(rms[:, 3, :], rms[:, 3, :], rms[:, 4, :], MUL)

            ve.wait_ge(ssq_done, NT)
            inverse_root(var_done, sqrt_done)
            for i in range(NT):
                V.tensor_scalar(x_sb[:, i, :], x_sb[:, i, :], rms[:, 3, i:i + 1], None, MUL).then_inc(xs_done, 1)

            row = lambda n: s5p[:, n, :]
            LRE, LIM, DT, MRE, ARG, MAG, SIN, SINH, N, ARE, AIM, DEN, AM1, ZRE, ZIM, T1, T2 = (
                row(n) for n in (0, 1, 3, 4, 5, 6, 7, 8, 9, 10, 11, 12, 13, 14, 15, 16, 17))
            ve.wait_ge(s5_dt, 1)
            tt(MRE, LRE, DT, MUL)
            tt(ARG, LIM, DT, MUL)
            ts(N, ARG, 1.0 / TWO_PI, MAGIC, MUL, ADD)
            ts(N, N, MAGIC, None, SUB)
            stt(ARG, N, -PI_A, ARG, MUL, ADD)
            stt(ARG, N, -PI_B, ARG, MUL, ADD)
            stt(ARG, N, -PI_C, ARG, MUL, ADD)
            V.tensor_scalar(ARG, ARG, 3.1415925, -3.1415925, ALU.min, ALU.max).then_inc(s5_arg, 1)

            ve.wait_ge(g_in_loaded, 16)
            for kt in range(KT):
                ve.wait_ge(hhi_done, kt + 1)
                drain(V.scalar_tensor_tensor(out=hT_lo[:, kt, :], in0=bk(f"xT{kt}")[:, :], scalar=g_in[:, kt:kt + 1],
                                             in1=hT_hi[:, kt, :].bitcast(F32), op0=MUL, op1=SUB), f"xT{kt}")
            for r in range(2):
                wait_fill(ve, f"CT{r}")
                cv = bk(f"CT{r}")[0:SN, :].rearrange("p (q r c) -> p r q c", r=2, c=SC)
                for par in range(2):
                    drain(V.tensor_scalar(CT[SN * par:SN * par + SN, r], cv[:, par], (1.0, -1.0)[r], None, MUL), f"CT{r}")
            ve.wait_ge(s5_act, 3)
            tt(T1, SINH, SINH, MUL)
            ts(T1, T1, -2.0, 1.0, MUL, ADD)
            tt(ARE, MAG, T1, MUL)
            tt(AIM, MAG, SIN, MUL)
            tt(T1, LRE, LRE, MUL)
            tt(T2, LIM, LIM, MUL)
            tt(DEN, T1, T2, ADD)
            link(V.reciprocal(DEN, DEN))
            ts(AM1, ARE, -1.0, None, ADD)
            tt(T1, AM1, LRE, MUL)
            tt(T2, AIM, LIM, MUL)
            tt(T1, T1, T2, ADD)
            tt(ZRE, T1, DEN, MUL)
            tt(T1, AIM, LRE, MUL)
            tt(T2, AM1, LIM, MUL)
            tt(T1, T1, T2, SUB)
            tt(ZIM, T1, DEN, MUL)

            def per_channel(v):
                return v.unsqueeze(2).broadcast_to((P, GP, SC))

            ta, tb = (t[:, :, 0, :] for t in (pr_a, pr_b))
            for o, (z0, z1), op in ((bb[:, 0], (ZRE, ZIM), SUB), (bb[:, 1], (ZIM, ZRE), ADD)):
                tt(ta, b_nat[:, 0], per_channel(z0), MUL)
                tt(tb, b_nat[:, 1], per_channel(z1), MUL)
                tt(o, ta, tb, op)

            def powers(dst, base_re, base_im):
                link(V.tensor_copy(dst[:, 0, 0], base_re))
                link(V.tensor_copy(dst[:, 1, 0], base_im))
                for n in (1, 2, 4):
                    t0, t1 = pwt[:, 0, 0:n], pwt[:, 1, 0:n]
                    fr, fi = (dst[:, r, n - 1].unsqueeze(1).broadcast_to((P, n, GP)) for r in range(2))
                    tt(t0, dst[:, 0, 0:n], fr, MUL)
                    tt(t1, dst[:, 1, 0:n], fi, MUL)
                    tt(dst[:, 0, n:2 * n], t0, t1, SUB)
                    tt(t0, dst[:, 0, 0:n], fi, MUL)
                    tt(t1, dst[:, 1, 0:n], fr, MUL)
                    tt(dst[:, 1, n:2 * n], t0, t1, ADD)

            powers(pw, ARE, AIM)
            powers(pq, pw[:, 0, CH - 1], pw[:, 1, CH - 1])

            def times_powers(dst_re, dst_im, re, im, n, neg, signal):
                shape = (P, GP, n, SC)
                pr, pi = (pw[:, r, 0:n].rearrange("p k q -> p q k").unsqueeze(3).broadcast_to(shape) for r in range(2))
                xr, xi = (v.unsqueeze(2).broadcast_to(shape) for v in (re, im))
                pa, pb = pr_a[:, :, 0:n, :], pr_b[:, :, 0:n, :]
                tt(pa, pr, xr, MUL)
                tt(pb, pi, xi, MUL)
                tt(dst_re, pa, pb, ADD if neg else SUB)
                tt(pa, pr, xi, MUL)
                tt(pb, pi, xr, MUL)
                V.tensor_tensor(dst_im, pa, pb, SUB if neg else ADD).then_inc(signal, 1)
                ve.wait_ge(signal, 1)

            for r in range(2):
                link(V.tensor_copy(W[r][:, :, 0, :], bb[:, r]))
            times_powers(W[0][:, :, 1:CH, :], W[1][:, :, 1:CH, :], bb[:, 0], bb[:, 1], CH - 1, False, w_built)
            times_powers(E[0][:, :, :, :], E[1][:, :, :, :], CT[:, 0], CT[:, 1], CH, True, e_built)

            ve.wait_ge(consts_in, 16 * 4)
            for t in range(4):
                job, g = f"q{t}", t // 2
                ve.wait_ge(drained[J[job][0]], J[job][1] + 2)
                dst = slice(DH * g, DH * g + DH)
                for half in range(2):
                    r = 2 * (t % 2) + half
                    src = slice(DH * half, DH * half + DH)
                    drain(V.tensor_tensor(qr[dst, r, :], bk(job)[src, :], rope[src, 0, :], MUL), job)
                    for s in range(2):
                        src = slice(DH * half + 32 * s, DH * half + 32 * s + 32)
                        to = slice(DH * g + 32 * (1 - s), DH * g + 32 * (1 - s) + 32)
                        drain(V.tensor_tensor(swapped[to, r, :], bk(job)[src, :], rope[src, 1, :], MUL), job)
                wait_drained(ve, job)
                for half in range(2):
                    r = 2 * (t % 2) + half
                    V.tensor_tensor(qr[dst, r, :], qr[dst, r, :], swapped[dst, r, :], ADD).then_inc(qr_done, 1)
            ve.wait_ge(qr_done, 8)
            for b, job in enumerate(("ksl", "kwi")):
                wait_fill(ve, job)
                drain(V.tensor_tensor(kr[:, b, :], bk(job)[:, :], rope[:, 2, :], MUL), job)
                for s in range(4):
                    src = slice(32 * s, 32 * s + 32)
                    to = slice(32 * (s ^ 1), 32 * (s ^ 1) + 32)
                    drain(V.tensor_tensor(swapped[to, b, :], bk(job)[src, :], rope[src, 3, :], MUL), job)
                wait_drained(ve, job)
                V.tensor_tensor(kr[:, b, :], kr[:, b, :], swapped[:, b, :], ADD).then_inc(kr_done, 1)
            for m in range(1, 8, 2):
                wait_fill(ve, f"WT{m}")
                drain(V.tensor_copy(WT[m // 4][:, 4 * (m % 4):4 * (m % 4) + 4, :].rearrange("p a b -> p (a b)"),
                                    bk(f"WT{m}")[:, :]), f"WT{m}")
            ve.wait_ge(cmp_in, 16 * 8)
            V.tensor_scalar(half_bias[:, :], bias_glu[:, :], 0.5, None, MUL).then_inc(bias_done, 1)
            for r, (job, flat) in enumerate((("kc", flat_k), ("vc", flat_v))):
                wait_fill(ve, job)
                for jp in range(2):
                    to = slice(DH * jp, DH * jp + DH)
                    for g in range(GROUPS):
                        src = bk(job)[DH * g:DH * g + DH, :].rearrange("p (n k j) -> p j k n", k=8, j=2)
                        for kh in range(2):
                            ins = V.tensor_tensor(flat[to, 8 * kh:8 * kh + 8, g, 0:NC - 1], src[:, jp, :, kh:kh + NC - 1],
                                                  pos[to, r, 8 * kh:8 * kh + 8].unsqueeze(2).broadcast_to((DH, 8, NC - 1)),
                                                  ADD)
                            drain(ins, job)
            wait_drained(ve, "vc")
            wait_drained(ve, "gl")
            V.tensor_scalar(gate[:, :, :, :], gate[:, :, :, :], 1.0, None, ADD).then_inc(gate_done, 1)

            ve.wait_ge(kr_done, 2)
            link(V.memset(X[:, :, :, 0:1], 0.0))
            for m in range(4):
                wait_drained(ve, f"S{m}")
            runs = X[:, :, :, 1:NCH + 1].rearrange("p r q (m j) -> p r q m j", j=8)

            def step(dst, src, are, aim, shape):
                n = 1
                for s in shape[1:]:
                    n *= s
                sub = "p (a b c) -> p a b c" if len(shape) == 4 else "p (a b) -> p a b"
                kw = dict(zip("abc", shape[1:]))
                t0, t1 = (t[:, 0:n].rearrange(sub, **kw) for t in (sx_a, sx_b))
                for o, (s0, s1), op in ((dst[0], (src[0], src[1]), SUB), (dst[1], (src[1], src[0]), ADD)):
                    tt(t0, s0, are, MUL)
                    tt(t1, s1, aim, MUL)
                    tt(t0, t0, t1, op)
                    tt(o, o, t0, ADD)

            for j in range(1, 8):
                A = [pw[:, r, CH - 1].unsqueeze(2).broadcast_to((P, GP, 8)) for r in range(2)]
                step([runs[:, r, :, :, j] for r in range(2)], [runs[:, r, :, :, j - 1] for r in range(2)], *A, (P, GP, 8))
            for k in range(1, 8):
                A = [pq[:, r, CH - 1].unsqueeze(2) for r in range(2)]
                step([runs[:, r, :, k, 7:8] for r in range(2)], [runs[:, r, :, k - 1, 7:8] for r in range(2)], *A,
                     (P, GP, 1))
            A = [pq[:, r, 0:7].rearrange("p k q -> p q k").unsqueeze(2).broadcast_to((P, GP, 7, 7)) for r in range(2)]
            step([runs[:, r, :, 1:8, 0:7] for r in range(2)],
                 [runs[:, r, :, 0:7, 7:8].broadcast_to((P, GP, 7, 7)) for r in range(2)], *A, (P, GP, 7, 7))
            ve.sem_inc(scan_done, 1)

            ve.wait_ge(vz_done, 1)
            wait_fill(ve, "VCMP")
            for r in range(HPG):
                rows = slice(NC * r, NC * r + NC)
                drain(V.tensor_copy(v_blk[rows, :, DH * r:DH * r + DH],
                                    bk("VCMP")[rows, 0:GROUPS * DH].rearrange("p (g d) -> p g d", g=GROUPS)), "VCMP")
            wait_fill(ve, "HV")
            for g in range(GROUPS):
                job, hs = f"SCC{g}", slice(HPG * g, HPG * g + HPG)
                e = e_cmp[:, :, hs, :]
                wait_fill(ve, job)
                drain(V.tensor_tensor(e, bk(job)[:, :].rearrange("p (i h c) -> p i h c", i=NT, h=HPG),
                                      cmask[:, 1].unsqueeze(2).broadcast_to((P, NT, HPG, NC)), ADD), job)
                wait_drained(ve, job)
                link(V.tensor_reduce(nmax_c[:, :, hs], e, AX_X, ALU.min))
                V.tensor_tensor(e, e, nmax_c[:, :, hs].unsqueeze(3).broadcast_to((P, NT, HPG, NC)), SUB).then_inc(cs_done, 1)
            for g in range(GROUPS):
                hs = slice(HPG * g, HPG * g + HPG)
                e = e_cmp[:, :, hs, :]
                ve.wait_ge(ce_done, g + 1)
                V.tensor_tensor(e, e, cmask[:, 0].unsqueeze(2).broadcast_to((P, NT, HPG, NC)), MUL).then_inc(cm_done, 1)
                ve.wait_ge(cm_done, g + 1)
                link(V.tensor_reduce(den_c[:, :, hs], e, AX_X, ALU.add))
            ve.wait_ge(gate_done, 1)
            ts(den_c[:, :, :], den_c[:, :, :], 1.0e-30, None, ALU.max)
            link(V.reciprocal(coef_c[:, :, :], den_c[:, :, :]))
            tt(coef_c[:, :, :], coef_c[:, :, :], gate[:, :, :, 0], MUL)
            for i in range(NT):
                wait_fill(ve, f"OC{i}")
                cc = coef_c[:, i, :].unsqueeze(2).broadcast_to((P, HEADS, DH))
                drain(V.tensor_tensor(o_tok[:, i, :].rearrange("p (h d) -> p h d", h=HEADS),
                                      bk(f"OC{i}")[:, :].rearrange("p (h d) -> p h d", h=HEADS), cc, MUL), f"OC{i}")
            for i in range(NT):
                wait_drained(ve, f"OC{i}")

            def fill_part(n, job):
                kind, t = job[:-1], int(job[-1])
                ve.wait_ge(th_done, n + 1)
                if kind == "glu":
                    drain(V.scalar_tensor_tensor(out=z[:, t, :], in0=tmp[:, 0, :], scalar=1.0, in1=z[:, t, :],
                                                 op0=ADD, op1=MUL), job)
                    wait_drained(ve, job)
                elif kind == "gs":
                    drain(V.scalar_tensor_tensor(out=tmp[:, 1, :], in0=tmp[:, 0, :], scalar=1.0, in1=bk(job)[:, :],
                                                 op0=ADD, op1=MUL), job)
                    wait_drained(ve, job)
                    tt(z[:, t, :], z[:, t, :], tmp[:, 1, :], MUL)
                    link(V.tensor_copy(f_hi[:, t, :], z[:, t, :]))
                    V.tensor_tensor(f_lo[:, t, :], z[:, t, :], f_hi[:, t, :].bitcast(F32), SUB).then_inc(f_split, 1)
                else:
                    drain(V.scalar_tensor_tensor(out=sg_nsa[:, t, :], in0=tmp[:, 0, :], scalar=1.0, in1=bk(job)[:, :],
                                                 op0=ADD, op1=MUL), job)

            def merge_branch(k):
                i, b = k // 2, k % 2
                c = slice(HEADS * k, HEADS * k + HEADS)
                ve.wait_ge(pv_done, 8 * k + 8)
                link(V.reciprocal(coef[:, c], den[:, c]))
                tt(coef[:, c], coef[:, c], gate[:, i, :, 1 + b], MUL)
                job = f"O{k}"
                drain(V.tensor_tensor(o_part[:, :].rearrange("p (h d) -> p h d", h=HEADS),
                                      bk(job)[:, :].rearrange("p (h d) -> p h d", h=HEADS),
                                      coef[:, c].unsqueeze(2).broadcast_to((P, HEADS, DH)), MUL), job)
                wait_drained(ve, job)
                if b == 0:
                    tt(o_tok[:, i, :], o_tok[:, i, :], o_part[:, :], ADD)
                else:
                    V.tensor_tensor(o_tok[:, i, :], o_tok[:, i, :], o_part[:, :], ADD).then_inc(o_done, 1)
                    ve.wait_ge(o_done, i + 1)

            wait_fill(ve, "Y3")
            ve.wait_ge(gate_done, 1)
            fills = 0
            for u in range(NU + 3):
                if u < NU:
                    n = P * (units[u][0] + 1)
                    wait_fill(ve, f"SC{u}")
                    if u >= 3:
                        wait_fill(ve, f"PT{u - 3}")
                    drain(V.tensor_tensor_reduce(prob[:, u % 3, 0:n], bk(f"SC{u}")[:, 0:n], causal[:, T - n:T], 1.0, 3.0e38,
                                                 ADD, ALU.min, nmax[:, u:u + 1]), f"SC{u}")
                if 0 <= u - 2 < NU:
                    v = u - 2
                    n = P * (units[v][0] + 1)
                    wait_fill(ve, f"PT{v}")
                    if v >= 2:
                        ve.wait_ge(pv_done, v - 1)
                    drain(V.tensor_copy(probT[:, v % 2, 0:n], bk(f"PT{v}")[:, 0:n]), f"PT{v}")
                if 0 <= u - 3 < NU and (u - 3) % 8 == 7:
                    pass
                if u >= 12 and (u - 12) % 8 == 0:
                    merge_branch((u - 12) // 8)
                if u == D_TERM_AT:
                    ve.wait_ge(y_in, 16)
                    for t in range(4):
                        V.scalar_tensor_tensor(out=yT[:, t, :], in0=u_perm[:, t].rearrange("p s k -> p (s k)"),
                                               scalar=d_col[:, t:t + 1], in1=yT[:, t, :], op0=MUL, op1=ADD)\
                         .then_inc(yd_done, 1)
                if u == Z_SPLIT_AT:
                    for t in range(4):
                        ve.wait_ge(z_done, t + 1)
                        link(V.tensor_copy(z_hi[:, t, :], z[:, t, :]))
                        V.tensor_tensor(z_lo[:, t, :], z[:, t, :], z_hi[:, t, :].bitcast(F32), SUB).then_inc(z_split, 1)
                    ve.wait_ge(z_split, 4)
                    ve.wait_ge(yd_done, 4)
                for job in FILL.get(u, []):
                    fill_part(fills, job)
                    fills += 1
            for k in range((NU + 3 - 1 - 12) // 8 + 1, NU // 8):
                merge_branch(k)
            for t in range(4):
                wait_drained(ve, f"gn{t}")
            for c in range(4):
                job = f"OT{c}"
                wait_fill(ve, job)
                drain(V.tensor_tensor(tmp[:, 1, :], bk(job)[:, :], sg_nsa[:, c, :], MUL), job)
                wait_drained(ve, job)
                link(V.tensor_copy(oT_hi[:, c, :], tmp[:, 1, :]))
                V.tensor_tensor(oT_lo[:, c, :], tmp[:, 1, :], oT_hi[:, c, :].bitcast(F32), SUB).then_inc(oT_split, 1)
                ve.wait_ge(oT_split, c + 1)
            for dp in range(4):
                for d in (2 * dp, 2 * dp + 1):
                    wait_drained(ve, f"MB{d}")
                    wait_fill(ve, f"B{d}")
                    drain(V.scalar_tensor_tensor(out=tmp[:, 1 + d % 2, :], in0=tmp[:, 0, :], scalar=1.0,
                                                 in1=bk(f"B{d}")[:, :], op0=ADD, op1=MUL), f"B{d}")
                for d in (2 * dp, 2 * dp + 1):
                    wait_drained(ve, f"MA{d}")
                    wait_fill(ve, f"A{d}")
                    drain(V.scalar_tensor_tensor(out=tmp[:, 3, :], in0=tmp[:, 0, :], scalar=1.0,
                                                 in1=bk(f"A{d}")[:, :], op0=ADD, op1=MUL), f"A{d}")
                    wait_drained(ve, f"A{d}")
                    wait_drained(ve, f"B{d}")
                    tt(tmp[:, 3, :], tmp[:, 3, :], tmp[:, 1 + d % 2, :], ADD)
                    link(V.tensor_copy(m_hi[:, d, :], tmp[:, 3, :]))
                    V.tensor_tensor(m_lo[:, d, :], tmp[:, 3, :], m_hi[:, d, :].bitcast(F32), SUB).then_inc(m_split, 1)
                    ve.wait_ge(m_split, d + 1)
            ve.wait_ge(x_again, 16)
            for q in range(4):
                for m in range(2):
                    job = f"W{q}_{m}"
                    wait_fill(ve, job)
                    r2 = r_sb[:, 2 * m:2 * m + 2, 256 * q:256 * q + 256]
                    V.scalar_tensor_tensor(out=r2, in0=bk(job)[:, :].rearrange("p (i c) -> p i c", i=2), scalar=0.125,
                                           in1=r2, op0=MUL, op1=ADD).then_inc(r_done, 1)
            ve.wait_ge(fin_sq, 4 * NT)
            link(V.tensor_reduce(rms[:, 0, :], ssq4[:, :, :], AX_X, ALU.add))
            inverse_root(fin_var, fin_sqrt)
            ve.wait_ge(gfin_in, 16)
            for i in range(NT):
                V.scalar_tensor_tensor(out=r_sb[:, i, :], in0=r_sb[:, i, :], scalar=rms[:, 3, i:i + 1], in1=gfin[:, :],
                                       op0=MUL, op1=MUL).then_inc(y_ready, 1)


def shape_constants():
    import numpy as np
    f = np.float32
    half = DH // 2
    inv_freq = f(10000.0) ** (-np.arange(half, dtype=f) / f(half))
    ang = np.arange(T, dtype=f)[None, :] * inv_freq[:, None]
    cos, sin = np.cos(ang).astype(f), np.sin(ang).astype(f)
    cos2, sin2 = np.tile(cos, (4, 1)), np.tile(np.concatenate([sin, -sin]), (2, 1))
    rope = np.stack([cos2 * f(-0.125), sin2 * f(-0.125), cos2, sin2], axis=1)
    causal = np.zeros((P, T), f)
    q, k = np.arange(P)[:, None], np.arange(P)[None, :]
    causal[:, T - P:] = np.where(k > q, f(BIG), f(0))
    t = (np.arange(NT)[None, :] * P + np.arange(P)[:, None])[:, :, None]
    c = np.arange(NC)[None, None, :]
    seen = (16 * c + 31 <= t) & (c < NC - 1)
    cmask = np.stack([seen.astype(f), np.where(seen, f(0), f(BIG))], axis=1)
    return {"ident": np.eye(P, SHIFT + P, SHIFT, dtype=f), "rope": rope.astype(f), "causal": causal, "cmask": cmask}


_INS = ["x", "norm_g", "w_in", "cmp_pos_k", "cmp_pos_v", "cmp_w1_k", "cmp_w2_k", "cmp_w1_v", "cmp_w2_v", "s5_lam_re",
        "s5_lam_im", "s5_log_dt", "s5_b_re", "s5_b_im", "s5_c_re", "s5_c_im", "s5_d", "w_glu", "b_glu", "w_proj_nsa",
        "w_proj_s5", "w_out", "final_g"]


def kernel(**inputs):
    import numpy as np
    import concourse.bacc as bacc
    from concourse.bass_utils import run_bass_kernel_spmd as run

    nc = bacc.Bacc("TRN2", target_bir_lowering=False, num_devices=1)
    arrays, args = {}, {}
    given = {n: np.ascontiguousarray(inputs[n]) for n in _INS} | shape_constants()
    for name, v in given.items():
        v = np.ascontiguousarray(v)
        arrays[f"in_{name}"] = v
        args[name] = nc.dram_tensor(f"in_{name}", v.shape, mybir.dt.from_np(v.dtype), kind="ExternalInput").ap()
    out = nc.dram_tensor("out_0", (1, T, D), F32, kind="ExternalOutput").ap()
    build_program(nc, args, out)
    r = run(nc, [arrays], core_ids=[0])
    return r.results[0]["out_0"]
```

```python
from contextlib import ExitStack

import concourse.bass as bass
from concourse import mybir

F32 = mybir.dt.float32
F32R = mybir.dt.float32r
ALU = mybir.AluOpType
ACT = mybir.ActivationFunctionType
AX_X = mybir.AxisListType.X

P = 128
T, D = 512, 1024
NT = T // P
KT = D // P
HEADS, GROUPS, DH = 8, 2, 64
HPG = HEADS // GROUPS
NC = 32
S5W = 512
SG, SC, SN = 32, 16, 64
CH = 4
NCH = T // CH
RUN, NRUN = 8, NCH // 8
GP = SG // 2
EPS = 1.0e-6
BIG = 1.0e30
TWO_PI = 6.283185307179586
MAGIC = 12582912.0
PI_A, PI_B = 6.28125, 0.0019340515136718750
PI_C = TWO_PI - PI_A - PI_B

COL = dict(q=0, kc=512, vc=640, ksl=768, vsl=896, kwi=1024, vwi=1152, gl=1280, gn=1304, u=1816, gs=2328,
           mga=2840, mgb=3864)

VAL_N = 2 * P + 3 * HEADS
NRAW, NSPLIT = 3, 2
BLK = 1024


def weight_blocks():
    b = [(f"u{t}", 1) for t in range(4)] + [(f"q{t}", 1) for t in range(4)]
    b += [(n, 1) for n in ("ksl", "kwi", "kc", "vc", "val0", "val1", "val2")]
    b += [(f"w1k{i}", 0) for i in range(4)] + [(f"w1v{i}", 0) for i in range(4)]
    b += [(f"gs{t}", 1) for t in range(4)]
    b += [(n, 1) for n in ("gn0", "gn1", "glu0", "gn2", "glu1", "gn3")]
    for dp in range(4):
        b += [(f"pb{dp}", 1), (f"mgb{2 * dp}", 1), (f"mgb{2 * dp + 1}", 1)]
        b += [(f"pa{dp}", 1), (f"mga{2 * dp}", 1), (f"mga{2 * dp + 1}", 1)]
    b += [(f"wo{q}_{h}", 1) for q in range(4) for h in range(2)]
    return b


def attention_units():
    return [(h // 2, h % 2, h, h // HPG, h % HPG, b) for h in range(HEADS) for b in range(2)]


P_OFF = [P * (i * (i + 1) // 2) for i in range(NT + 1)]
VAL_KT = [(0, 3), (3, 6), (6, 8)]
FILL = {1: ["gn0"], 5: ["gn1"], 7: ["glu0"], 8: ["glu1"], 9: ["gn2"], 10: ["glu2"], 11: ["glu3"], 13: ["gn3"]}
D_TERM_AT, GELU_AT, Z_SPLIT_AT = 3, 4, 5


def bank_plan():
    uses, reads, jobs = [0] * 8, [0] * 8, {}

    def use(job, bank, nreads=1, nfills=1):
        before = reads[bank]
        uses[bank] += nfills
        reads[bank] += nreads
        jobs[job] = (bank, before, uses[bank], reads[bank])

    ring = [0]

    def pj(job, nreads=1, banks=tuple(range(8))):
        use(job, banks[ring[0] % len(banks)], nreads)
        ring[0] += 1

    for kt in range(KT):
        pj(f"xT{kt}")
    for r in range(2):
        pj(f"CT{r}", 3)
    for t in range(4):
        pj(f"u{t}")
    for t in range(4):
        pj(f"q{t}", 8)
    for n in ("ksl", "kwi"):
        pj(n, 5)
    for m in range(4):
        pj(f"WT{m}")
    pj("KR")
    pj("kc", 8)
    pj("TT0")
    pj("TT1")
    pj("vc", 8)
    for m in range(8):
        pj(f"S{m}")
    for i in range(NT):
        pj(f"V{i}", 2)
    for n in ("HK", "HV", "HT", "KCMP"):
        pj(n)
    pj("VCMP", 4)
    for t in range(4):
        pj(f"gs{t}")
    for g in range(GROUPS):
        pj(f"SCC{g}")
    for m in range(8):
        pj(f"Y{m}")
    for g in range(GROUPS):
        pj(f"PET{g}")
    for u in range(2 * HEADS + 1):
        if u < 2 * HEADS:
            for k in range(3):
                use(f"SC{u}_{k}", 1 + k, 2 if k == 0 else 1)
        if u >= 1:
            for k in range(3):
                use(f"PT{u - 1}_{k}", 4 + (3 * u + k) % 2)
            if (u - 1) % 4 == 0:
                use(f"O{(u - 1) // 4}", 6 + (u - 1) // 4 % 2, nfills=0)
        for j in FILL.get(u, []):
            use(j, 0)
    ring[0] = 1
    for dp in range(4):
        for kind in ("B", "MB", "A", "MA"):
            for d in (2 * dp, 2 * dp + 1):
                pj(f"{kind}{d}")
    for q in range(4):
        for m in range(2):
            pj(f"W{q}_{m}")
    return jobs


def build_program(nc, a, out):
    blocks = weight_blocks()
    block_at = {n: k for k, (n, _) in enumerate(blocks)}
    split_at, k_split = {}, 0
    for n, split in blocks:
        if split:
            split_at[n] = k_split
            k_split += 1
    split_names = [n for n, s in blocks if s]
    units = attention_units()
    NU = len(units)
    J = bank_plan()

    ctx = ExitStack()
    with ctx:
        def sb(name, shape, dt=F32):
            return ctx.enter_context(nc.sbuf_tensor(name, shape, dt))

        def shared(name, size, *sets):
            made = {}
            for tensors in sets:
                with ExitStack() as once:
                    for n, shape, dt in tensors:
                        made[n] = once.enter_context(nc.sbuf_tensor(n, shape, dt))
            sb(name, [P, size])
            return made

        hT_hi = sb("hT_hi", [P, KT, T], F32R)
        hT_lo = sb("hT_lo", [P, KT, T], F32R)
        raw = sb("raw", [P, NRAW, BLK])
        w_hi = sb("w_hi", [P, NSPLIT, BLK], F32R)
        w_lo = sb("w_lo", [P, NSPLIT, BLK], F32R)
        m = shared("room_x", 4096,
                   [("x_sb", [P, NT, D], F32)],
                   [("u_perm", [P, 4, CH, NCH], F32), ("probT", [P, 4, T], F32)],
                   [("r_sb", [P, NT, D], F32)])
        x_sb, u_perm, probT, r_sb = (m[n] for n in ("x_sb", "u_perm", "probT", "r_sb"))
        qr = sb("qr", [P, HPG, T])
        m = shared("room_q", 2048, [("qn", [P, HPG, T], F32)], [("tmp", [P, 4, T], F32)])
        qn, tmp = m["qn"], m["tmp"]
        m = shared("room_k", 1024, [("bb", [P, 2, GP, SC], F32)], [("kr", [P, 2, T], F32)], [("gfin", [P, D], F32)])
        bb, kr, gfin = m["bb"], m["kr"], m["gfin"]
        m = shared("room_v", 1024, [("c_nat", [P, 2, 4, SN], F32), ("b_nat", [P, 2, GP, SC], F32)],
                   [("v_tok", [P, NT, 2, P], F32)])
        c_nat, b_nat, v_tok = m["c_nat"], m["b_nat"], m["v_tok"]
        m = shared("room_flat", 2048,
                   [("flat_k", [P, 16, GROUPS, NC], F32), ("flat_v", [P, 16, GROUPS, NC], F32)],
                   [("peT", [P, GROUPS, NT, P], F32), ("e_cmp", [P, NT, HEADS, NC], F32)])
        flat_k, flat_v, peT, e_cmp = (m[n] for n in ("flat_k", "flat_v", "peT", "e_cmp"))
        m = shared("room_1", 4096,
                   [("W", [P, SG, CH, SC], F32), ("pr_a", [P, GP, CH, SC], F32), ("pr_b", [P, GP, CH, SC], F32)],
                   [("U_sh", [P, GP, NCH], F32), ("Y_sb", [P, GP, NCH], F32)],
                   [("oT_hi", [P, 4, T], F32R), ("oT_lo", [P, 4, T], F32R)])
        W, pr_a, pr_b, U_sh, Y_sb, oT_hi, oT_lo = (
            m[n] for n in ("W", "pr_a", "pr_b", "U_sh", "Y_sb", "oT_hi", "oT_lo"))
        m = shared("room_2", 4096,
                   [("E_re", [P, GP, CH, SC], F32), ("E_nim", [P, GP, CH, SC], F32), ("WT", [P, GP, P], F32)],
                   [("prob", [P, 2, P_OFF[NT]], F32), ("sg_nsa", [P, 2, T], F32)],
                   [("m_hi", [P, KT, T], F32R)])
        E, WT, prob, sg_nsa, m_hi = (m["E_re"], m["E_nim"]), m["WT"], m["prob"], m["sg_nsa"], m["m_hi"]
        m = shared("room_3", 2 * GP * (NCH + 1),
                   [("X", [P, 2, GP, NCH + 1], F32)],
                   [("z_hi", [P, 4, T], F32R), ("z_lo", [P, 4, T], F32R)],
                   [("m_lo", [P, KT, T], F32R)])
        X, z_hi, z_lo, m_lo = m["X"], m["z_hi"], m["z_lo"], m["m_lo"]
        m = shared("room_4", 4096,
                   [("TT", [P, GP, CH, SC], F32), ("sx_a", [P, 1024], F32), ("sx_b", [P, 1024], F32)],
                   [("yT", [P, 4, T], F32)],
                   [("f_hi", [P, 4, T], F32R), ("f_lo", [P, 4, T], F32R)])
        TT, sx_a, sx_b, yT, f_hi, f_lo = (m[n] for n in ("TT", "sx_a", "sx_b", "yT", "f_hi", "f_lo"))
        m = shared("room_t", 2048, [("rope", [P, 4, T], F32)], [("z", [P, 4, T], F32)])
        rope, z = m["rope"], m["z"]
        m = shared("room_m", 2048, [("swapped", [P, 4, T], F32)], [("sg_s5", [P, 4, T], F32)])
        swapped, sg_s5 = m["swapped"], m["sg_s5"]
        m = shared("room_5", 640, [("KR", [P, GP, SC], F32), ("shift", [P, CH - 1, P], F32)],
                   [("hidn", [GROUPS * NC, 2, 256], F32)])
        KR, shift, hidn = m["KR"], m["shift"], m["hidn"]
        m = shared("room_6", 512, [("CS", [P, SG, SC], F32)], [("v_blk", [P, GROUPS, HPG * DH], F32)])
        CS, v_blk = m["CS"], m["v_blk"]
        causal = sb("causal", [P, T])
        ident = sb("ident", [P, P])
        CT = sb("CT", [P, 2, GP, SC])
        s5p = sb("s5p", [P, 18, GP])
        pw = sb("pw", [P, 2, CH, GP])
        pq = sb("pq", [P, 2, RUN, GP])
        pwt = sb("pwt", [P, 2, CH, GP])
        hid = sb("hid", [P, 2, 2, GROUPS * NC])
        w2 = sb("w2", [P, 2, 2, DH])
        kcT = sb("kcT", [P, NC])
        pos = sb("pos", [P, 2, 16])
        cmask = sb("cmask", [P, 2, NT, NC])
        gate = sb("gate", [P, NT, HEADS, 3])
        nmax_c = sb("nmax_c", [P, NT, HEADS])
        den_c = sb("den_c", [P, NT, HEADS])
        coef_c = sb("coef_c", [P, NT, HEADS])
        nmax = sb("nmax", [P, NU, NT])
        den = sb("den", [P, NU, NT])
        coef = sb("coef", [P, NU, NT])
        g_in = sb("g_in", [P, KT])
        d_col = sb("d_col", [P, 4])
        bias_glu = sb("bias_glu", [P, 4])
        half_bias = sb("half_bias", [P, 4])
        rms = sb("rms", [P, 6, NT])
        ssq4 = sb("ssq4", [P, NT, 4])

        bank = [ctx.enter_context(nc.psum_tensor(f"bank{i}", [P, 512], F32)) for i in range(8)]

        def sem(name):
            return ctx.enter_context(nc.semaphore(name))

        filled = [sem(f"bank{i}_filled") for i in range(8)]
        drained = [sem(f"bank{i}_drained") for i in range(8)]
        x_in, consts_in, s5_in, cmp_in, x_again, gfin_in, g_in_loaded = (sem(n) for n in (
            "x_in", "consts_in", "s5_in", "cmp_in", "x_again", "gfin_in", "g_in_loaded"))
        raw_full = [sem(f"raw{i}_full") for i in range(NRAW)]
        hi_done, lo_done, part_used = (sem(n) for n in ("w_hi_done", "w_lo_done", "w_part_used"))
        ssq_done, var_done, sqrt_done, xs_done, hhi_done = (sem(n) for n in (
            "ssq_done", "variance_done", "sqrt_done", "x_scaled", "hT_hi_done"))
        dve, act = sem("dve_chain"), sem("act_chain")
        s5_dt, s5_arg, s5_act, w_built, e_built = (sem(n) for n in (
            "s5_dt", "s5_arguments", "s5_functions", "W_built", "E_built"))
        u_out, u_in, scan_done, y_out, y_in, yd_done, z_done, z_split = (sem(n) for n in (
            "u_scratch_out", "U_in", "scan_done", "y_scratch_out", "y_in", "y_with_D", "z_done",
            "z_split"))
        qr_done, kr_done, gate_done, flat_zero, vz_done = (sem(n) for n in (
            "q_roped", "k_roped", "gates_done", "flat_zeroed", "v_blk_zeroed"))
        cs_done, ce_done, cm_done, e_done, p_done, pv_done = (sem(n) for n in (
            "cmp_shifted", "cmp_exp", "cmp_masked", "exp_done", "prob_done", "pv_done"))
        bias_done, th_done, f_split, oT_split, m_split, r_done, fin_sq, fin_var, fin_sqrt, y_ready, stored = (sem(n) for n in (
            "half_bias_done", "tanh_done", "f_split", "oT_split", "merged_split", "residual_done", "final_squares", "final_variance",
            "final_sqrt", "out_ready", "stored"))

        u_scr = nc.dram_tensor("u_scratch", (S5W, CH, NCH), F32, kind="Internal").ap()
        y_scr = nc.dram_tensor("y_scratch", (S5W, CH, NCH), F32, kind="Internal").ap()

        def bk(job):
            return bank[J[job][0]]

        def open_bank(eng, job):
            b, before, _, _ = J[job]
            if before:
                eng.wait_ge(drained[b], before)

        def fill(ins, job):
            ins.then_inc(filled[J[job][0]], 1)

        def wait_fill(eng, job):
            b, _, fills, _ = J[job]
            eng.wait_ge(filled[b], fills)

        def drain(ins, job):
            ins.then_inc(drained[J[job][0]], 1)

        def wait_drained(eng, job):
            b, _, _, reads = J[job]
            eng.wait_ge(drained[b], reads)

        def last_job(name):
            base = name.rstrip("0123456789")
            n = name[len(base):]
            if base == "glu":
                return f"glu{2 * int(n) + 1}"
            if base in ("pa", "pb"):
                return f"{base[1].upper()}{2 * int(n) + 1}"
            if base in ("mga", "mgb"):
                return f"M{base[2].upper()}{n}"
            if name[:3] == "w1k" or name[:3] == "w1v":
                return f"H{name[2].upper()}" if name[3] == "3" else None
            if name[:2] == "wo":
                return f"W{name[2]}_1" if name[4] == "1" else None
            if base == "val":
                return f"V{NT - 1}" if n == "2" else None
            return name

        part_at = {n: k + 1 for k, n in enumerate(n for n, _ in blocks if last_job(n) is None)}

        def wait_used(eng, name):
            if last_job(name) is None:
                eng.wait_ge(part_used, part_at[name])
            else:
                wait_fill(eng, last_job(name))

        raw_count, count = {}, [0] * NRAW
        for k, (n, _) in enumerate(blocks):
            count[k % NRAW] += 32 if n[:3] == "val" else 16
            raw_count[n] = count[k % NRAW]

        def slot(name):
            return split_at[name] % NSPLIT

        def block_source(name):
            w_in = a["w_in"][0]
            if name[:3] == "w1k" or name[:3] == "w1v":
                w, i = a["cmp_w1_" + name[2]][0], int(name[3])
                return w.rearrange("(kt p) n -> p kt n", p=P)[:, 4 * i:4 * i + 4, :], (4, 256)
            if name[:3] == "glu":
                i = int(name[3])
                return a["w_glu"][0].rearrange("(kt p) n -> p kt n", p=P)[:, :, 256 * i:256 * i + 256], (4, 256)
            if name[:2] in ("pa", "pb"):
                w, i = a["w_proj_nsa" if name[1] == "a" else "w_proj_s5"][0], int(name[2])
                return w.rearrange("(kt p) n -> p kt n", p=P)[:, :, 256 * i:256 * i + 256], (4, 256)
            if name[:2] == "wo":
                q, h = int(name[2]), int(name[4])
                w = a["w_out"][0].rearrange("(kt p) n -> p kt n", p=P)
                return w[:, 4 * h:4 * h + 4, 256 * q:256 * q + 256], (4, 256)
            w = w_in.rearrange("(kt p) n -> p kt n", p=P)
            base = name.rstrip("0123456789")
            n = int(name[len(base):] or 0)
            if base == "val":
                k0, k1 = VAL_KT[n]
                return w[:, k0:k1, :], (k1 - k0, VAL_N)
            return w[:, :, COL[base] + P * n:COL[base] + P * n + P], (KT, P)

        def view(buf, s, dims):
            return buf[:, s, 0:dims[0] * dims[1]].rearrange("p (k n) -> p k n", n=dims[1])

        def wdims(name):
            return block_source(name)[1]

        ctx.enter_context(nc.allow_non_contiguous_dma(reason="small parameter vectors, one element per partition"))
        block = ctx.enter_context(nc.Block())

        @block.sync
        def _(sp):
            sp.dma_start(x_sb[:, :, :], a["x"][0].rearrange("(i p) d -> p i d", p=P)).then_inc(x_in, 16)

            def u_to_scratch():
                for t in range(4):
                    wait_drained(sp, f"u{t}")
                    sp.dma_start(u_scr[P * t:P * t + P], u_perm[:, t]).then_inc(u_out, 16)

            def u_from_scratch():
                sp.wait_ge(u_out, 64)
                for m in range(4):
                    wait_drained(sp, f"WT{m}")
                wait_drained(sp, "KR")
                by_pos = u_scr.rearrange("(q r c) s k -> r s c q k", r=2, c=SC)
                for par in range(2):
                    for e in range(CH):
                        row = SN * par + SC * e
                        sp.dma_start(U_sh[row:row + SC], by_pos[par, CH - 1 - e]).then_inc(u_in, 16)

            def y_through_scratch():
                for m in range(8):
                    wait_drained(sp, f"Y{m}")
                by_pos = y_scr.rearrange("(q r c) s k -> r s c q k", r=2, c=SC)
                for par in range(2):
                    for j in range(CH):
                        row = SN * par + SC * j
                        sp.dma_start(by_pos[par, j], Y_sb[row:row + SC]).then_inc(y_out, 16)
                sp.wait_ge(y_out, 16 * 2 * CH)
                sp.dma_start(yT[:, :, :], y_scr.rearrange("(t p) s k -> p t (s k)", p=P)).then_inc(y_in, 16)

            for k, (name, split) in enumerate(blocks):
                if k >= NRAW:
                    before, was_split = blocks[k - NRAW]
                    if was_split:
                        sp.wait_ge(lo_done, split_at[before] + 1)
                    else:
                        wait_used(sp, before)
                src, dims = block_source(name)
                dst, full = view(raw, k % NRAW, dims), raw_full[k % NRAW]
                if name[:3] == "val":
                    sp.dma_start(dst[:, :, 0:P], src[:, :, COL["vsl"]:COL["vsl"] + P]).then_inc(full, 16)
                    sp.dma_start(dst[:, :, P:VAL_N], src[:, :, COL["vwi"]:COL["vwi"] + VAL_N - P]).then_inc(full, 16)
                else:
                    sp.dma_start(dst, src).then_inc(full, 16)
                if name == "q3":
                    u_to_scratch()
                if name == "vc":
                    u_from_scratch()
                if name == "gn1":
                    y_through_scratch()
                if name == "pb1":
                    sp.wait_ge(oT_split, 4)
                    sp.dma_start(r_sb[:, :, :], a["x"][0].rearrange("(i p) d -> p i d", p=P)).then_inc(x_again, 16)
                    sp.dma_start(gfin[:, :], a["final_g"].partition_broadcast(P)).then_inc(gfin_in, 16)
            for i in range(NT):
                sp.wait_ge(y_ready, i + 1)
                sp.dma_start(out[0, P * i:P * i + P, :], r_sb[:, i, :]).then_inc(stored, 16)
            sp.wait_ge(stored, 16 * NT)

        @block.gpsimd
        def _(pl):
            nc.gpsimd.memset(flat_k[:, :, :, NC - 1:NC], 0.0).then_inc(flat_zero, 1)
            nc.gpsimd.memset(flat_v[:, :, :, NC - 1:NC], 0.0).then_inc(flat_zero, 1)
            for j, name in enumerate(split_names):
                pl.wait_ge(hi_done, j + 1)
                dims, k = wdims(name), block_at[name]
                w = view(raw, k % NRAW, dims)
                nc.gpsimd.tensor_tensor(view(w_lo, j % NSPLIT, dims), w, view(w_hi, j % NSPLIT, dims).bitcast(F32),
                                        ALU.subtract).then_inc(lo_done, 1)
                if name == "val0":
                    wait_fill(pl, "KR")
                    nc.gpsimd.memset(v_blk[:, :, :], 0.0).then_inc(vz_done, 1)

        @block.scalar
        def _(ac):
            def load(dst, src, s):
                ac.dma_start(dst, src).then_inc(s, 16)

            load(ident[:, :], a["ident"], consts_in)
            load(shift[:, :, :], a["shift"], consts_in)
            load(g_in[:, :], a["norm_g"][0].rearrange("(k p) -> p k", p=P), g_in_loaded)
            for r, n in enumerate(("s5_lam_re", "s5_lam_im")):
                flat = a[n][0].rearrange("g p -> (g p)")
                load(s5p[:, r, :], flat.rearrange("(q p) -> p q", p=P), s5_in)
            dt2 = a["s5_log_dt"][0].rearrange("(q r) -> r q", r=2)
            for par in range(2):
                load(s5p[SN * par:SN * par + SN, 2, :], dt2[par].partition_broadcast(SN), s5_in)
            for r, n in enumerate(("s5_b_re", "s5_b_im")):
                flat = a[n][0].rearrange("g p c -> (g p) c")
                load(b_nat[:, r], flat.rearrange("(q p) c -> p q c", p=P), s5_in)
            for r, n in enumerate(("s5_c_re", "s5_c_im")):
                load(c_nat[:, r], a[n][0].rearrange("g c p -> (g c) p").rearrange("(t q) p -> q t p", q=P), s5_in)
            load(rope[:, :, :], a["rope"], consts_in)
            load(causal[:, :], a["causal"], consts_in)
            load(cmask[:, :, :, :], a["cmask"], consts_in)
            for r, n in enumerate("kv"):
                load(w2[:, r], a["cmp_w2_" + n][0].rearrange("(h p) d -> p h d", p=P), cmp_in)
                pv = a["cmp_pos_" + n][0].rearrange("(k j) d -> j d k", j=2)
                for jp in range(2):
                    load(pos[DH * jp:DH * jp + DH, r, :], pv[jp], cmp_in)
            load(d_col[:, :], a["s5_d"][0].rearrange("(t p) -> p t", p=P), cmp_in)
            load(bias_glu[:, :], a["b_glu"][0].rearrange("(t p) -> p t", p=P), cmp_in)

            def split_hi(j):
                name = split_names[j]
                dims, k = wdims(name), block_at[name]
                ac.wait_ge(raw_full[k % NRAW], raw_count[name])
                if j >= NSPLIT:
                    wait_used(ac, split_names[j - NSPLIT])
                nc.scalar.activation(view(w_hi, j % NSPLIT, dims), view(raw, k % NRAW, dims), ACT.Copy)\
                    .then_inc(hi_done, 1)

            def after(name):
                if split_at[name] + NSPLIT < len(split_names):
                    split_hi(split_at[name] + NSPLIT)

            def evacuate(job, dst, src, func=ACT.Copy, **kw):
                wait_fill(ac, job)
                drain(nc.scalar.activation(dst, src, func, **kw), job)

            ac.wait_ge(x_in, 16)
            for i in range(NT):
                junk = (qr, qn)[i // 2][:, 2 * (i % 2):2 * (i % 2) + 2, :].rearrange("p a b -> p (a b)")
                nc.scalar.activation(junk, x_sb[:, i, :], ACT.Square, accum_out=rms[:, 0, i:i + 1]).then_inc(ssq_done, 1)
            ac.wait_ge(var_done, 1)
            nc.scalar.activation(rms[:, 2, :], rms[:, 1, :], ACT.Sqrt).then_inc(sqrt_done, 1)
            split_hi(0)
            split_hi(1)
            ac.wait_ge(s5_in, 16 * 8)
            nc.scalar.activation(s5p[:, 3, :], s5p[:, 2, :], ACT.Exp).then_inc(s5_dt, 1)
            ac.wait_ge(g_in_loaded, 16)
            for kt in range(KT):
                wait_fill(ac, f"xT{kt}")
                nc.scalar.activation(hT_hi[:, kt, :], bk(f"xT{kt}")[:, :], ACT.Copy, scale=g_in[:, kt:kt + 1])\
                    .then_inc(hhi_done, 1)
            ac.wait_ge(s5_arg, 1)
            nc.scalar.activation(s5p[:, 6, :], s5p[:, 4, :], ACT.Exp).then_inc(s5_act, 1)
            nc.scalar.activation(s5p[:, 7, :], s5p[:, 5, :], ACT.Sin).then_inc(s5_act, 1)
            nc.scalar.activation(s5p[:, 8, :], s5p[:, 5, :], ACT.Sin, scale=0.5).then_inc(s5_act, 1)

            for t in range(4):
                evacuate(f"u{t}", u_perm[:, t], bk(f"u{t}")[:, :].rearrange("p (k s) -> p s k", s=CH))
                after(f"u{t}")
            for t in range(4):
                g = t // 2
                for half in range(2):
                    evacuate(f"q{t}", qn[DH * g:DH * g + DH, 2 * (t % 2) + half, :],
                             bk(f"q{t}")[DH * half:DH * half + DH, :], scale=-0.125)
                after(f"q{t}")
            after("ksl")
            after("kwi")
            for m in range(4):
                evacuate(f"WT{m}", WT[:, 4 * m:4 * m + 4, :].rearrange("p a b -> p (a b)"), bk(f"WT{m}")[:, :])
            evacuate("KR", KR[:, :, :].rearrange("p a b -> p (a b)"), bk("KR")[:, 0:GP * SC])
            after("kc")
            for k in range(2):
                evacuate(f"TT{k}", TT[:, :, 2 * k:2 * k + 2, :].rearrange("p g j c -> p j g c"),
                         bk(f"TT{k}")[:, :].rearrange("p (j g c) -> p j g c", j=2, c=SC))
            after("vc")
            for m in range(8):
                ri, quarter = m % 2, m // 2
                evacuate(f"S{m}", X[:, ri, 4 * quarter:4 * quarter + 4, 1:NCH + 1],
                         bk(f"S{m}")[:, :].rearrange("p (q k) -> p q k", k=NCH))
            after("val0")
            for i in range(NT):
                evacuate(f"V{i}", v_tok[:, i].rearrange("p b c -> p (b c)"), bk(f"V{i}")[:, 0:2 * P])
                evacuate(f"V{i}", gate[:, i].rearrange("p h b -> p (h b)"), bk(f"V{i}")[:, 2 * P:VAL_N], ACT.Tanh, scale=0.5)
            for r, n in enumerate(("HK", "HV")):
                evacuate(n, hidn[:, r, :], bk(n)[0:GROUPS * NC, 0:256], ACT.Gelu_apprx_tanh)
            after("val1")
            after("val2")
            evacuate("HT", hid[:, :, :, :].rearrange("p r h n -> p (r h n)"), bk("HT")[:, 0:256])
            evacuate("KCMP", kcT[:, :], bk("KCMP")[:, 0:NC])
            ac.wait_ge(kr_done, 2)
            for t in range(4):
                evacuate(f"gs{t}", sg_s5[:, t, :], bk(f"gs{t}")[:, :], ACT.Silu)
                after(f"gs{t}")
            for g in range(GROUPS):
                ac.wait_ge(cs_done, g + 1)
                e = e_cmp[:, :, HPG * g:HPG * g + HPG, :]
                nc.scalar.activation(e, e, ACT.Exp, scale=-1.0).then_inc(ce_done, 1)
            for m in range(8):
                evacuate(f"Y{m}", Y_sb[:, 2 * m:2 * m + 2, :].rearrange("p a b -> p (a b)"), bk(f"Y{m}")[:, 0:2 * NCH])
            for g in range(GROUPS):
                evacuate(f"PET{g}", peT[:, g].rearrange("p i q -> p (i q)"), bk(f"PET{g}")[:, :])

            tanh_user = [None]

            def tanh_free(user):
                if tanh_user[0]:
                    wait_drained(ac, tanh_user[0])
                tanh_user[0] = user

            def fill_part(job):
                kind, t = job[:-1], int(job[-1])
                wait_fill(ac, job)
                tanh_free(job)
                bias = half_bias[:, t:t + 1] if kind == "glu" else 0.0
                nc.scalar.activation(tmp[:, 0, :], bk(job)[:, :], ACT.Tanh, scale=0.5, bias=bias).then_inc(th_done, 1)
                if kind != "glu":
                    after(job)
                elif t % 2:
                    after(f"glu{t // 2}")

            ac.wait_ge(bias_done, 1)
            for u in range(NU + 1):
                if u < NU:
                    for i in range(NT):
                        n = P * (i + 1)
                        ac.wait_ge(drained[J[f"SC{u}_{max(i - 1, 0)}"][0]],
                                   J[f"SC{u}_{max(i - 1, 0)}"][1] + (1 if i != 1 else 2))
                        pi = prob[:, u % 2, P_OFF[i]:P_OFF[i] + n]
                        nc.scalar.activation(pi, pi, ACT.Exp, scale=-1.0, bias=nmax[:, u, i:i + 1],
                                             accum_out=den[:, u, i:i + 1]).then_inc(e_done, 1)
                if u == GELU_AT:
                    for t in range(4):
                        ac.wait_ge(yd_done, t + 1)
                        nc.scalar.activation(z[:, t, :].rearrange("p (k j) -> p j k", j=CH),
                                             yT[:, t, :].rearrange("p (j k) -> p j k", k=NCH),
                                             ACT.Gelu_apprx_tanh).then_inc(z_done, 1)
                for job in FILL.get(u, []):
                    fill_part(job)
            for dp in range(4):
                for kind, user in (("MB", "B"), ("MA", "A")):
                    for d in (2 * dp, 2 * dp + 1):
                        if d % 2 == 0:
                            after(f"p{user.lower()}{dp}")
                        wait_fill(ac, f"{kind}{d}")
                        tanh_free(f"{user}{d}")
                        drain(nc.scalar.activation(tmp[:, 0, :], bk(f"{kind}{d}")[:, :], ACT.Tanh, scale=0.5), f"{kind}{d}")
                        after(f"mg{user.lower()}{d}")
            for q in range(4):
                after(f"wo{q}_0")
                after(f"wo{q}_1")
                for i in range(NT):
                    ac.wait_ge(r_done, 2 * q + i // 2 + 1)
                    junk = (qr, z)[q // 2][:, 2 * (q % 2) + i // 2, 256 * (i % 2):256 * (i % 2) + 256]
                    nc.scalar.activation(junk, r_sb[:, i, 256 * q:256 * q + 256], ACT.Square,
                                         accum_out=ssq4[:, i, q:q + 1]).then_inc(fin_sq, 1)
            ac.wait_ge(fin_var, 1)
            nc.scalar.activation(rms[:, 2, :], rms[:, 1, :], ACT.Sqrt).then_inc(fin_sqrt, 1)

        @block.tensor
        def _(pe):
            def mm3(dst, w, x, first, last):
                nc.tensor.matmul(dst, w[0], x[1], start=first, stop=False, skip_group_check=True)
                nc.tensor.matmul(dst, w[1], x[0], start=False, stop=False, skip_group_check=True)
                return nc.tensor.matmul(dst, w[0], x[0], start=False, stop=last, skip_group_check=True)

            def weights(name):
                pe.wait_ge(lo_done, split_at[name] + 1)
                dims = wdims(name)
                return [view(w, slot(name), dims) for w in (w_hi, w_lo)]

            def hT(kt, cols=slice(0, T)):
                return hT_hi[:, kt, cols], hT_lo[:, kt, cols]

            def channel_major(job, name):
                w = weights(name)
                open_bank(pe, job)
                for kt in range(KT):
                    ins = mm3(bk(job)[:, :], [v[:, kt, :] for v in w], hT(kt), kt == 0, kt == KT - 1)
                fill(ins, job)

            def half_block(job, name, x, cols):
                w = weights(name)
                open_bank(pe, job)
                for kt in range(4):
                    ins = mm3(bk(job)[:, :], [v[:, kt, cols:cols + P] for v in w], [v[:, kt, :] for v in x], kt == 0, kt == 3)
                fill(ins, job)

            def four_transposes(job, sources):
                open_bank(pe, job)
                for n, src in enumerate(sources):
                    ins = nc.tensor.transpose(bk(job)[:, P * n:P * n + P], src, ident[:, :])
                fill(ins, job)

            pe.wait_ge(consts_in, 16 * 5)
            pe.wait_ge(xs_done, NT)
            for kt in range(KT):
                four_transposes(f"xT{kt}", [x_sb[:, i, P * kt:P * kt + P] for i in range(NT)])
            pe.wait_ge(s5_in, 16 * 8)
            for r in range(2):
                open_bank(pe, f"CT{r}")
                for t in range(4):
                    ins = nc.tensor.transpose(bk(f"CT{r}")[0:SN, P * t:P * t + P], c_nat[:, r, t, :], ident[:, :])
                fill(ins, f"CT{r}")
            wait_drained(pe, f"xT{KT - 1}")
            for kt in range(KT):
                wait_drained(pe, f"xT{kt}")
            for n in ("u0", "u1", "u2", "u3", "q0", "q1", "q2", "q3", "ksl", "kwi"):
                channel_major(n, n)
            pe.wait_ge(w_built, 4)
            for m in range(4):
                four_transposes(f"WT{m}", [W[:, 2 * gp:2 * gp + 2].rearrange("p g e c -> p (g e c)")
                                           for gp in range(4 * m, 4 * m + 4)])
            open_bank(pe, "KR")
            for g in range(SG):
                gp, par = g // 2, g % 2
                ins = nc.tensor.matmul(bk("KR")[SN * par:SN * par + SN, SC * gp:SC * gp + SC],
                                       W[:, g].rearrange("p e c -> p (e c)"), CS[:, g, :], start=True, stop=True,
                                       skip_group_check=True)
            fill(ins, "KR")
            channel_major("kc", "kc")
            wait_drained(pe, "KR")
            for k in range(2):
                open_bank(pe, f"TT{k}")
                for jj in range(2):
                    j = 2 * k + jj
                    down = shift[:, j, :] if j < CH - 1 else ident[:, :]
                    ins = nc.tensor.matmul(bk(f"TT{k}")[:, 256 * jj:256 * jj + 256], down,
                                           KR[:, :, :].rearrange("p g c -> p (g c)"), start=True, stop=True,
                                           skip_group_check=True)
                fill(ins, f"TT{k}")
            channel_major("vc", "vc")
            pe.wait_ge(u_in, 16 * 2 * CH)
            for m in range(4):
                wait_drained(pe, f"WT{m}")
            for m in range(8):
                ri, quarter = m % 2, m // 2
                open_bank(pe, f"S{m}")
                for par in range(2):
                    rows = slice(SN * par, SN * par + SN)
                    for k in range(4):
                        gp = 4 * quarter + k
                        ins = nc.tensor.matmul(bk(f"S{m}")[rows, NCH * k:NCH * k + NCH],
                                               WT[rows, gp, SN * ri:SN * ri + SN], U_sh[rows, gp, :],
                                               start=True, stop=True, skip_group_check=True)
                fill(ins, f"S{m}")
            for n in range(3):
                w = weights(f"val{n}")
                k0, k1 = VAL_KT[n]
                for i in range(NT):
                    if n == 0:
                        open_bank(pe, f"V{i}")
                    for kt in range(k0, k1):
                        ins = mm3(bk(f"V{i}")[:, 0:VAL_N], hT(kt, slice(P * i, P * i + P)), [v[:, kt - k0, :] for v in w],
                                  kt == 0, kt == KT - 1)
                    if n == 2:
                        fill(ins, f"V{i}")
                if n < 2:
                    ins.then_inc(part_used, 1)
            pe.wait_ge(flat_zero, 2)
            for r, (n, flat) in enumerate((("k", flat_k), ("v", flat_v))):
                job = "H" + n.upper()
                wait_drained(pe, {"k": "kc", "v": "vc"}[n])
                open_bank(pe, job)
                for i in range(4):
                    k = block_at[f"w1{n}{i}"]
                    pe.wait_ge(raw_full[k % NRAW], raw_count[f"w1{n}{i}"])
                    w1 = view(raw, k % NRAW, (4, 256))
                    for kk in range(4):
                        ins = nc.tensor.matmul(bk(job)[0:GROUPS * NC, 0:256], flat[:, 4 * i + kk].rearrange("p g n -> p (g n)"),
                                               w1[:, kk, :], start=(i == 0 and kk == 0), stop=(i == 3 and kk == 3))
                    if i < 3:
                        ins.then_inc(part_used, 1)
                fill(ins, job)
            wait_drained(pe, "HK")
            wait_drained(pe, "HV")
            open_bank(pe, "HT")
            for r in range(2):
                for half in range(2):
                    c = 64 * (2 * r + half)
                    ins = nc.tensor.transpose(bk("HT")[:, c:c + 64], hidn[:, r, P * half:P * half + P], ident[0:64, 0:64])
            fill(ins, "HT")
            pe.wait_ge(cmp_in, 16 * 8)
            wait_drained(pe, "HT")
            open_bank(pe, "KCMP")
            for g in range(GROUPS):
                for half in range(2):
                    ins = nc.tensor.matmul(bk("KCMP")[DH * g:DH * g + DH, 0:NC], w2[:, 0, half, :],
                                           hid[:, 0, half, NC * g:NC * g + NC], start=(half == 0), stop=(half == 1))
            fill(ins, "KCMP")
            open_bank(pe, "VCMP")
            for r in range(HPG):
                for g in range(GROUPS):
                    for half in range(2):
                        ins = nc.tensor.matmul(bk("VCMP")[NC * r:NC * r + NC, DH * g:DH * g + DH],
                                               hid[:, 1, half, NC * g:NC * g + NC], w2[:, 1, half, :],
                                               start=(half == 0), stop=(half == 1))
            fill(ins, "VCMP")
            for t in range(4):
                channel_major(f"gs{t}", f"gs{t}")
            wait_drained(pe, "KCMP")
            for t in range(4):
                wait_drained(pe, f"q{t}")
            for g in range(GROUPS):
                open_bank(pe, f"SCC{g}")
                rows = slice(DH * g, DH * g + DH)
                for i in range(NT):
                    for r in range(HPG):
                        c = (i * HPG + r) * NC
                        ins = nc.tensor.matmul(bk(f"SCC{g}")[:, c:c + NC], qn[rows, r, P * i:P * i + P], kcT[rows, :],
                                               start=True, stop=True, skip_group_check=True)
                fill(ins, f"SCC{g}")
            wait_drained(pe, "TT0")
            wait_drained(pe, "TT1")
            pe.wait_ge(scan_done, 1)
            pe.wait_ge(e_built, 1)
            for m in range(8):
                open_bank(pe, f"Y{m}")
                for par in range(2):
                    rows = slice(SN * par, SN * par + SN)
                    for k in range(2):
                        gp = 2 * m + k
                        dst = bk(f"Y{m}")[rows, NCH * k:NCH * k + NCH]
                        nc.tensor.matmul(dst, TT[rows, gp].rearrange("p j c -> p (j c)"), U_sh[rows, gp, :],
                                         start=True, stop=False, skip_group_check=True)
                        for ri in range(2):
                            ins = nc.tensor.matmul(dst, E[ri][rows, gp].rearrange("p j c -> p (j c)"),
                                                   X[rows, ri, gp, 0:NCH], start=False, stop=(ri == 1),
                                                   skip_group_check=True)
                fill(ins, f"Y{m}")
            pe.wait_ge(cm_done, 1)
            for g in range(GROUPS):
                four_transposes(f"PET{g}", [e_cmp[:, i, HPG * g:HPG * g + HPG, :].rearrange("p h c -> p (h c)")
                                            for i in range(NT)])
            wait_drained(pe, "VCMP")

            def scores(u, k):
                c, half, h, g, r, b = units[u]
                rows = slice(DH * g, DH * g + DH)
                job = f"SC{u}_{k}"
                open_bank(pe, job)
                for i in ((0, 1), (2,), (3,))[k]:
                    dst = bk(job)[:, P * i:P * i + P * (i + 1)] if k == 0 else bk(job)[:, 0:P * (i + 1)]
                    ins = nc.tensor.matmul(dst, qr[rows, r, P * i:P * i + P], kr[rows, b, 0:P * (i + 1)],
                                           start=True, stop=True, skip_group_check=True)
                fill(ins, job)

            def transposes(u, k):
                job = f"PT{u}_{k}"
                open_bank(pe, job)
                col = 0
                for kt in ((0,), (1,), (2, 3))[k]:
                    for i in range(kt, NT):
                        src = prob[:, u % 2, P_OFF[i] + P * kt:P_OFF[i] + P * kt + P]
                        ins = nc.tensor.transpose(bk(job)[:, col:col + P], src, ident[:, :])
                        col += P
                fill(ins, job)

            def weighted_values(u, k):
                c, half, h, g, r, b = units[u]
                wait_drained(pe, f"PT{u}_{k}")
                o = bk(f"O{c}")
                if u % 4 == 0 and k == 0:
                    open_bank(pe, f"O{c}")
                    wait_drained(pe, f"PET{g}")
                    nc.tensor.matmul(o[:, :], v_blk[:, g, P * (c % 2):P * (c % 2) + P],
                                     peT[:, g].rearrange("p i q -> p (i q)"), start=True, stop=False, skip_group_check=True)
                col = 0
                for kt in ((0,), (1,), (2, 3))[k]:
                    n = P * (NT - kt)
                    ins = nc.tensor.matmul(o[DH * half:DH * half + DH, P * kt:T], v_tok[:, kt, b, DH * g:DH * g + DH],
                                           probT[:, (3 * u + k) % 4, col:col + n], start=False, stop=(kt == 3),
                                           skip_group_check=True)
                    col += n
                ins.then_inc(pv_done, 1)

            pe.wait_ge(qr_done, 8)
            pe.wait_ge(kr_done, 2)
            for i in range(NT):
                wait_drained(pe, f"V{i}")
            for u in range(NU + 1):
                if u < NU:
                    for k in range(3):
                        scores(u, k)
                if u >= 1:
                    pe.wait_ge(p_done, u)
                    transposes(u - 1, 0)
                    transposes(u - 1, 1)
                    weighted_values(u - 1, 0)
                    transposes(u - 1, 2)
                    weighted_values(u - 1, 1)
                for job in FILL.get(u, []):
                    kind, t = job[:-1], int(job[-1])
                    if kind == "glu":
                        pe.wait_ge(z_split, 4)
                        half_block(job, f"glu{t // 2}", (z_hi, z_lo), P * (t % 2))
                    else:
                        channel_major(job, job)
                if u >= 1:
                    weighted_values(u - 1, 2)
            for dp in range(4):
                pe.wait_ge(f_split, 4)
                for d in (2 * dp, 2 * dp + 1):
                    half_block(f"B{d}", f"pb{dp}", (f_hi, f_lo), P * (d % 2))
                for d in (2 * dp, 2 * dp + 1):
                    channel_major(f"MB{d}", f"mgb{d}")
                pe.wait_ge(oT_split, 4)
                for d in (2 * dp, 2 * dp + 1):
                    half_block(f"A{d}", f"pa{dp}", (oT_hi, oT_lo), P * (d % 2))
                for d in (2 * dp, 2 * dp + 1):
                    channel_major(f"MA{d}", f"mga{d}")
            for q in range(4):
                for h in range(2):
                    w = weights(f"wo{q}_{h}")
                    for m in range(2):
                        job = f"W{q}_{m}"
                        if h == 0:
                            open_bank(pe, job)
                        for ii in range(2):
                            i = 2 * m + ii
                            for kk in range(4):
                                kt = 4 * h + kk
                                pe.wait_ge(m_split, kt + 1) if q == 0 and m == 0 and ii == 0 else None
                                x = [v[:, kt, P * i:P * i + P] for v in (m_hi, m_lo)]
                                ins = mm3(bk(job)[:, 256 * ii:256 * ii + 256], x, [v[:, kk, :] for v in w],
                                          kt == 0 and ii == 0, kt == KT - 1)
                        if h == 1:
                            fill(ins, job)
                    if h == 0:
                        ins.then_inc(part_used, 1)

        @block.vector
        def _(ve):
            V = nc.vector
            chain = [0]

            def link(ins):
                chain[0] += 1
                ins.then_inc(dve, 1)
                ve.wait_ge(dve, chain[0])

            def tt(o, x, y, op):
                link(V.tensor_tensor(o, x, y, op))

            def ts(o, x, s1, s2, op0, op1=None):
                link(V.tensor_scalar(o, x, s1, s2, op0, op1) if op1 is not None else V.tensor_scalar(o, x, s1, None, op0))

            def stt(o, x, s, y, op0, op1):
                link(V.scalar_tensor_tensor(out=o, in0=x, scalar=s, in1=y, op0=op0, op1=op1))

            MUL, ADD, SUB = ALU.mult, ALU.add, ALU.subtract

            def inverse_root(signal_var, signal_sqrt):
                V.tensor_scalar(rms[:, 1, :], rms[:, 0, :], 1.0 / D, EPS, MUL, ADD).then_inc(signal_var, 1)
                ve.wait_ge(signal_sqrt, 1)
                link(V.reciprocal(rms[:, 3, :], rms[:, 2, :]))
                tt(rms[:, 4, :], rms[:, 3, :], rms[:, 3, :], MUL)
                tt(rms[:, 4, :], rms[:, 4, :], rms[:, 1, :], MUL)
                ts(rms[:, 4, :], rms[:, 4, :], -0.5, 1.5, MUL, ADD)
                tt(rms[:, 3, :], rms[:, 3, :], rms[:, 4, :], MUL)

            ve.wait_ge(ssq_done, NT)
            inverse_root(var_done, sqrt_done)
            for i in range(NT):
                V.tensor_scalar(x_sb[:, i, :], x_sb[:, i, :], rms[:, 3, i:i + 1], None, MUL).then_inc(xs_done, 1)

            row = lambda n: s5p[:, n, :]
            LRE, LIM, DT, MRE, ARG, MAG, SIN, SINH, N, ARE, AIM, DEN, AM1, ZRE, ZIM, T1, T2 = (
                row(n) for n in (0, 1, 3, 4, 5, 6, 7, 8, 9, 10, 11, 12, 13, 14, 15, 16, 17))
            ve.wait_ge(s5_dt, 1)
            tt(MRE, LRE, DT, MUL)
            tt(ARG, LIM, DT, MUL)
            ts(N, ARG, 1.0 / TWO_PI, MAGIC, MUL, ADD)
            ts(N, N, MAGIC, None, SUB)
            stt(ARG, N, -PI_A, ARG, MUL, ADD)
            stt(ARG, N, -PI_B, ARG, MUL, ADD)
            stt(ARG, N, -PI_C, ARG, MUL, ADD)
            V.tensor_scalar(ARG, ARG, 3.1415925, -3.1415925, ALU.min, ALU.max).then_inc(s5_arg, 1)

            ve.wait_ge(g_in_loaded, 16)
            for kt in range(KT):
                ve.wait_ge(hhi_done, kt + 1)
                drain(V.scalar_tensor_tensor(out=hT_lo[:, kt, :], in0=bk(f"xT{kt}")[:, :], scalar=g_in[:, kt:kt + 1],
                                             in1=hT_hi[:, kt, :].bitcast(F32), op0=MUL, op1=SUB), f"xT{kt}")
            for r in range(2):
                wait_fill(ve, f"CT{r}")
                sign = (1.0, -1.0)[r]
                cv = bk(f"CT{r}")[0:SN, :]
                drain(V.tensor_scalar(CS[SN * r:SN * r + SN].rearrange("p g c -> p (g c)"), cv, sign, None, MUL), f"CT{r}")
                cv = cv.rearrange("p (q r c) -> p r q c", r=2, c=SC)
                for par in range(2):
                    drain(V.tensor_scalar(CT[SN * par:SN * par + SN, r], cv[:, par], sign, None, MUL), f"CT{r}")
            ve.wait_ge(s5_act, 3)
            tt(T1, SINH, SINH, MUL)
            ts(T1, T1, -2.0, 1.0, MUL, ADD)
            tt(ARE, MAG, T1, MUL)
            tt(AIM, MAG, SIN, MUL)
            tt(T1, LRE, LRE, MUL)
            tt(T2, LIM, LIM, MUL)
            tt(DEN, T1, T2, ADD)
            link(V.reciprocal(DEN, DEN))
            ts(AM1, ARE, -1.0, None, ADD)
            tt(T1, AM1, LRE, MUL)
            tt(T2, AIM, LIM, MUL)
            tt(T1, T1, T2, ADD)
            tt(ZRE, T1, DEN, MUL)
            tt(T1, AIM, LRE, MUL)
            tt(T2, AM1, LIM, MUL)
            tt(T1, T1, T2, SUB)
            tt(ZIM, T1, DEN, MUL)

            def per_channel(v):
                return v.unsqueeze(2).broadcast_to((P, GP, SC))

            ta, tb = (t[:, :, 0, :] for t in (pr_a, pr_b))
            for o, (z0, z1), op in ((bb[:, 0], (ZRE, ZIM), SUB), (bb[:, 1], (ZIM, ZRE), ADD)):
                tt(ta, b_nat[:, 0], per_channel(z0), MUL)
                tt(tb, b_nat[:, 1], per_channel(z1), MUL)
                tt(o, ta, tb, op)

            def powers(dst, base_re, base_im, count):
                link(V.tensor_copy(dst[:, 0, 0], base_re))
                link(V.tensor_copy(dst[:, 1, 0], base_im))
                n = 1
                while n < count:
                    t0, t1 = pwt[:, 0, 0:n], pwt[:, 1, 0:n]
                    fr, fi = (dst[:, r, n - 1].unsqueeze(1).broadcast_to((P, n, GP)) for r in range(2))
                    tt(t0, dst[:, 0, 0:n], fr, MUL)
                    tt(t1, dst[:, 1, 0:n], fi, MUL)
                    tt(dst[:, 0, n:2 * n], t0, t1, SUB)
                    tt(t0, dst[:, 0, 0:n], fi, MUL)
                    tt(t1, dst[:, 1, 0:n], fr, MUL)
                    tt(dst[:, 1, n:2 * n], t0, t1, ADD)
                    n *= 2

            powers(pw, ARE, AIM, CH)

            def products(n, re, im, cross):
                shape = (P, GP, n, SC)
                pr, pi = (pw[:, r, 0:n].rearrange("p k q -> p q k").unsqueeze(3).broadcast_to(shape) for r in range(2))
                xr, xi = (v.unsqueeze(2).broadcast_to(shape) for v in (re, im))
                pa, pb = pr_a[:, :, 0:n, :], pr_b[:, :, 0:n, :]
                link(V.tensor_tensor(pa, pr, xi if cross else xr, MUL))
                link(V.tensor_tensor(pb, pi, xr if cross else xi, MUL))
                return pa, pb

            w4 = W[:, :, :, :].rearrange("p (q r) e c -> p r q e c", r=2)
            for ri in range(2):
                for par in range(2):
                    link(V.tensor_copy(w4[SN * ri:SN * ri + SN, par, :, 0, :], bb[SN * par:SN * par + SN, ri]))
                pa, pb = products(CH - 1, bb[:, 0], bb[:, 1], ri == 1)
                for par in range(2):
                    rows = slice(SN * par, SN * par + SN)
                    V.tensor_tensor(w4[SN * ri:SN * ri + SN, par, :, 1:CH, :], pa[rows], pb[rows],
                                    ADD if ri else SUB).then_inc(w_built, 1)
                ve.wait_ge(w_built, 2 * ri + 2)
            pa, pb = products(CH, CT[:, 0], CT[:, 1], False)
            tt(E[0][:, :, :, :], pa, pb, ADD)
            pa, pb = products(CH, CT[:, 0], CT[:, 1], True)
            V.tensor_tensor(E[1][:, :, :, :], pa, pb, SUB).then_inc(e_built, 1)
            ve.wait_ge(e_built, 1)

            ve.wait_ge(consts_in, 16 * 5)
            for t in range(4):
                job, g = f"q{t}", t // 2
                ve.wait_ge(drained[J[job][0]], J[job][1] + 2)
                dst = slice(DH * g, DH * g + DH)
                for half in range(2):
                    r = 2 * (t % 2) + half
                    src = slice(DH * half, DH * half + DH)
                    drain(V.tensor_tensor(qr[dst, r, :], bk(job)[src, :], rope[src, 0, :], MUL), job)
                    for s in range(2):
                        src = slice(DH * half + 32 * s, DH * half + 32 * s + 32)
                        to = slice(DH * g + 32 * (1 - s), DH * g + 32 * (1 - s) + 32)
                        drain(V.tensor_tensor(swapped[to, r, :], bk(job)[src, :], rope[src, 1, :], MUL), job)
                wait_drained(ve, job)
                for half in range(2):
                    r = 2 * (t % 2) + half
                    V.tensor_tensor(qr[dst, r, :], qr[dst, r, :], swapped[dst, r, :], ADD).then_inc(qr_done, 1)
            ve.wait_ge(qr_done, 8)
            for b, job in enumerate(("ksl", "kwi")):
                wait_fill(ve, job)
                drain(V.tensor_tensor(kr[:, b, :], bk(job)[:, :], rope[:, 2, :], MUL), job)
                for s in range(4):
                    src = slice(32 * s, 32 * s + 32)
                    to = slice(32 * (s ^ 1), 32 * (s ^ 1) + 32)
                    drain(V.tensor_tensor(swapped[to, b, :], bk(job)[src, :], rope[src, 3, :], MUL), job)
                wait_drained(ve, job)
                V.tensor_tensor(kr[:, b, :], kr[:, b, :], swapped[:, b, :], ADD).then_inc(kr_done, 1)
            powers(pq, pw[:, 0, CH - 1], pw[:, 1, CH - 1], RUN)
            ve.wait_ge(cmp_in, 16 * 8)
            V.tensor_scalar(half_bias[:, :], bias_glu[:, :], 0.5, None, MUL).then_inc(bias_done, 1)
            for r, (job, flat) in enumerate((("kc", flat_k), ("vc", flat_v))):
                wait_fill(ve, job)
                for jp in range(2):
                    to = slice(DH * jp, DH * jp + DH)
                    for g in range(GROUPS):
                        src = bk(job)[DH * g:DH * g + DH, :].rearrange("p (n k j) -> p j k n", k=8, j=2)
                        for kh in range(2):
                            ins = V.tensor_tensor(flat[to, 8 * kh:8 * kh + 8, g, 0:NC - 1], src[:, jp, :, kh:kh + NC - 1],
                                                  pos[to, r, 8 * kh:8 * kh + 8].unsqueeze(2).broadcast_to((DH, 8, NC - 1)),
                                                  ADD)
                            drain(ins, job)
            wait_drained(ve, "vc")
            link(V.memset(X[:, :, :, 0:1], 0.0))
            for m in range(8):
                wait_drained(ve, f"S{m}")
            runs = X[:, :, :, 1:NCH + 1].rearrange("p r q (m j) -> p r q m j", j=RUN)

            def both_parts(dst, src, are, aim, width):
                n = 2 * GP * width
                ta, tb = (t[:, 0:n].rearrange("p (r b c) -> p r b c", r=2, b=GP) for t in (sx_a, sx_b))
                tt(ta, src, are, MUL)
                tt(tb, src, aim, MUL)
                tt(dst, dst, ta, ADD)
                tt(dst[:, 0], dst[:, 0], tb[:, 1], SUB)
                tt(dst[:, 1], dst[:, 1], tb[:, 0], ADD)

            for j in range(1, RUN):
                A = [pw[:, r, CH - 1].unsqueeze(1).unsqueeze(3).broadcast_to((P, 2, GP, NRUN)) for r in range(2)]
                both_parts(runs[:, :, :, :, j], runs[:, :, :, :, j - 1], *A, NRUN)
            for k in range(1, NRUN):
                A = [pq[:, r, RUN - 1].unsqueeze(1).unsqueeze(3).broadcast_to((P, 2, GP, 1)) for r in range(2)]
                both_parts(runs[:, :, :, k, RUN - 1:RUN], runs[:, :, :, k - 1, RUN - 1:RUN], *A, 1)
            for q0 in (0, 8):
                qs = slice(q0, q0 + 8)
                shape = (P, 8, NRUN - 1, RUN - 1)
                ar, ai = (pq[:, r, 0:RUN - 1, qs].rearrange("p k q -> p q k").unsqueeze(2).broadcast_to(shape) for r in range(2))
                xr, xi = (runs[:, r, qs, 0:NRUN - 1, RUN - 1:RUN].broadcast_to(shape) for r in range(2))
                n = shape[1] * shape[2] * shape[3]
                ta, tb = (t[:, 0:n].rearrange("p (a b c) -> p a b c", a=8, b=NRUN - 1) for t in (sx_a, sx_b))
                for r, (s0, s1), op in ((0, (xr, xi), SUB), (1, (xi, xr), ADD)):
                    dst = runs[:, r, qs, 1:NRUN, 0:RUN - 1]
                    tt(ta, s0, ar, MUL)
                    tt(tb, s1, ai, MUL)
                    tt(dst, dst, ta, ADD)
                    last = V.tensor_tensor(dst, dst, tb, op)
                    if q0 and r:
                        last.then_inc(scan_done, 1)
                    else:
                        link(last)
            for i in range(NT):
                wait_drained(ve, f"V{i}")
            V.tensor_scalar(gate[:, :, :, :], gate[:, :, :, :], 1.0, None, ADD).then_inc(gate_done, 1)

            ve.wait_ge(vz_done, 1)
            wait_fill(ve, "VCMP")
            for r in range(HPG):
                rows = slice(NC * r, NC * r + NC)
                drain(V.tensor_copy(v_blk[rows, :, DH * r:DH * r + DH],
                                    bk("VCMP")[rows, 0:GROUPS * DH].rearrange("p (g d) -> p g d", g=GROUPS)), "VCMP")
            wait_fill(ve, "HV")
            for g in range(GROUPS):
                job, hs = f"SCC{g}", slice(HPG * g, HPG * g + HPG)
                e = e_cmp[:, :, hs, :]
                wait_fill(ve, job)
                drain(V.tensor_tensor(e, bk(job)[:, :].rearrange("p (i h c) -> p i h c", i=NT, h=HPG),
                                      cmask[:, 1].unsqueeze(2).broadcast_to((P, NT, HPG, NC)), ADD), job)
                wait_drained(ve, job)
                link(V.tensor_reduce(nmax_c[:, :, hs], e, AX_X, ALU.min))
                V.tensor_tensor(e, e, nmax_c[:, :, hs].unsqueeze(3).broadcast_to((P, NT, HPG, NC)), SUB).then_inc(cs_done, 1)
            for g in range(GROUPS):
                hs = slice(HPG * g, HPG * g + HPG)
                e = e_cmp[:, :, hs, :]
                ve.wait_ge(ce_done, g + 1)
                tt(e, e, cmask[:, 0].unsqueeze(2).broadcast_to((P, NT, HPG, NC)), MUL)
                link(V.tensor_reduce(den_c[:, :, hs], e, AX_X, ALU.add))
            ve.wait_ge(gate_done, 1)
            ts(den_c[:, :, :], den_c[:, :, :], 1.0e-30, None, ALU.max)
            link(V.reciprocal(coef_c[:, :, :], den_c[:, :, :]))
            tt(coef_c[:, :, :], coef_c[:, :, :], gate[:, :, :, 0], MUL)
            V.tensor_tensor(e_cmp[:, :, :, :], e_cmp[:, :, :, :],
                            coef_c[:, :, :].unsqueeze(3).broadcast_to((P, NT, HEADS, NC)), MUL).then_inc(cm_done, 1)

            def fill_part(n, job):
                kind, t = job[:-1], int(job[-1])
                ve.wait_ge(th_done, n + 1)
                if kind == "glu":
                    drain(V.scalar_tensor_tensor(out=z[:, t, :], in0=tmp[:, 0, :], scalar=1.0, in1=z[:, t, :],
                                                 op0=ADD, op1=MUL), job)
                    wait_drained(ve, job)
                    link(V.scalar_tensor_tensor(out=z[:, t, :], in0=z[:, t, :], scalar=2.0, in1=sg_s5[:, t, :],
                                                op0=MUL, op1=MUL))
                    link(V.tensor_copy(f_hi[:, t, :], z[:, t, :]))
                    V.tensor_tensor(f_lo[:, t, :], z[:, t, :], f_hi[:, t, :].bitcast(F32), SUB).then_inc(f_split, 1)
                else:
                    drain(V.scalar_tensor_tensor(out=sg_nsa[:, t % 2, :], in0=tmp[:, 0, :], scalar=1.0, in1=bk(job)[:, :],
                                                 op0=ADD, op1=MUL), job)

            def gate_pair(c):
                job = f"O{c}"
                ve.wait_ge(pv_done, 12 * (c + 1))
                wait_drained(ve, f"gn{c}")
                drain(V.tensor_tensor(tmp[:, 1, :], bk(job)[:, :], sg_nsa[:, c % 2, :], MUL), job)
                wait_drained(ve, job)
                link(V.tensor_copy(oT_hi[:, c, :], tmp[:, 1, :]))
                V.tensor_tensor(oT_lo[:, c, :], tmp[:, 1, :], oT_hi[:, c, :].bitcast(F32), SUB).then_inc(oT_split, 1)
                ve.wait_ge(oT_split, c + 1)

            for m in range(8):
                wait_fill(ve, f"Y{m}")
            fills = 0
            for u in range(NU + 1):
                if u < NU:
                    if u >= 2:
                        wait_fill(ve, f"PT{u - 2}_2")
                    for i in range(NT):
                        n, k = P * (i + 1), max(i - 1, 0)
                        job = f"SC{u}_{k}"
                        wait_fill(ve, job)
                        src = bk(job)[:, P:3 * P] if i == 1 else bk(job)[:, 0:n]
                        drain(V.tensor_tensor_reduce(prob[:, u % 2, P_OFF[i]:P_OFF[i] + n], src, causal[:, T - n:T], 1.0,
                                                     3.0e38, ADD, ALU.min, nmax[:, u, i:i + 1]), job)
                if u >= 1:
                    for k in range(3):
                        job, step = f"PT{u - 1}_{k}", 3 * (u - 1) + k
                        n = (T, T - P, T - P)[k]
                        wait_fill(ve, job)
                        if step >= 4:
                            ve.wait_ge(pv_done, step - 3)
                        drain(V.tensor_copy(probT[:, step % 4, 0:n], bk(job)[:, 0:n]), job)
                if u < NU:
                    h, b = units[u][2], units[u][5]
                    ve.wait_ge(e_done, 4 * (u + 1))
                    link(V.reciprocal(coef[:, u, :], den[:, u, :]))
                    tt(coef[:, u, :], coef[:, u, :], gate[:, :, h, 1 + b], MUL)
                    for i in range(NT):
                        pi = prob[:, u % 2, P_OFF[i]:P_OFF[i + 1]]
                        ins = V.tensor_scalar(pi, pi, coef[:, u, i:i + 1], None, MUL)
                    ins.then_inc(p_done, 1)
                if u == D_TERM_AT:
                    ve.wait_ge(y_in, 16)
                    for t in range(4):
                        V.scalar_tensor_tensor(out=yT[:, t, :], in0=u_perm[:, t].rearrange("p s k -> p (s k)"),
                                               scalar=d_col[:, t:t + 1], in1=yT[:, t, :], op0=MUL, op1=ADD)\
                         .then_inc(yd_done, 1)
                if u == Z_SPLIT_AT:
                    for t in range(4):
                        ve.wait_ge(z_done, t + 1)
                        link(V.tensor_copy(z_hi[:, t, :], z[:, t, :]))
                        V.tensor_tensor(z_lo[:, t, :], z[:, t, :], z_hi[:, t, :].bitcast(F32), SUB).then_inc(z_split, 1)
                    ve.wait_ge(z_split, 4)
                for job in FILL.get(u, []):
                    fill_part(fills, job)
                    fills += 1
                if u >= 5 and u % 4 == 1:
                    gate_pair(u // 4 - 1)
            gate_pair(HEADS // 2 - 1)
            for dp in range(4):
                for d in (2 * dp, 2 * dp + 1):
                    wait_drained(ve, f"MB{d}")
                    wait_fill(ve, f"B{d}")
                    drain(V.scalar_tensor_tensor(out=tmp[:, 1 + d % 2, :], in0=tmp[:, 0, :], scalar=1.0,
                                                 in1=bk(f"B{d}")[:, :], op0=ADD, op1=MUL), f"B{d}")
                for d in (2 * dp, 2 * dp + 1):
                    wait_drained(ve, f"MA{d}")
                    wait_fill(ve, f"A{d}")
                    drain(V.scalar_tensor_tensor(out=tmp[:, 3, :], in0=tmp[:, 0, :], scalar=1.0,
                                                 in1=bk(f"A{d}")[:, :], op0=ADD, op1=MUL), f"A{d}")
                    wait_drained(ve, f"A{d}")
                    wait_drained(ve, f"B{d}")
                    tt(tmp[:, 3, :], tmp[:, 3, :], tmp[:, 1 + d % 2, :], ADD)
                    link(V.tensor_copy(m_hi[:, d, :], tmp[:, 3, :]))
                    V.tensor_tensor(m_lo[:, d, :], tmp[:, 3, :], m_hi[:, d, :].bitcast(F32), SUB).then_inc(m_split, 1)
                    ve.wait_ge(m_split, d + 1)
            ve.wait_ge(x_again, 16)
            for q in range(4):
                for m in range(2):
                    job = f"W{q}_{m}"
                    wait_fill(ve, job)
                    r2 = r_sb[:, 2 * m:2 * m + 2, 256 * q:256 * q + 256]
                    V.scalar_tensor_tensor(out=r2, in0=bk(job)[:, :].rearrange("p (i c) -> p i c", i=2), scalar=0.125,
                                           in1=r2, op0=MUL, op1=ADD).then_inc(r_done, 1)
            ve.wait_ge(fin_sq, 4 * NT)
            link(V.tensor_reduce(rms[:, 0, :], ssq4[:, :, :], AX_X, ALU.add))
            inverse_root(fin_var, fin_sqrt)
            ve.wait_ge(gfin_in, 16)
            for i in range(NT):
                V.scalar_tensor_tensor(out=r_sb[:, i, :], in0=r_sb[:, i, :], scalar=rms[:, 3, i:i + 1], in1=gfin[:, :],
                                       op0=MUL, op1=MUL).then_inc(y_ready, 1)


def shape_constants():
    import numpy as np
    f = np.float32
    half = DH // 2
    inv_freq = f(10000.0) ** (-np.arange(half, dtype=f) / f(half))
    ang = np.arange(T, dtype=f)[None, :] * inv_freq[:, None]
    cos, sin = np.cos(ang).astype(f), np.sin(ang).astype(f)
    cos2, sin2 = np.tile(cos, (4, 1)), np.tile(np.concatenate([sin, -sin]), (2, 1))
    rope = np.stack([cos2 * f(-0.125), sin2 * f(-0.125), cos2, sin2], axis=1)
    causal = np.zeros((P, T), f)
    q, k = np.arange(P)[:, None], np.arange(P)[None, :]
    causal[:, T - P:] = np.where(k > q, f(BIG), f(0))
    t = (np.arange(NT)[None, :] * P + np.arange(P)[:, None])[:, :, None]
    c = np.arange(NC)[None, None, :]
    seen = (16 * c + 31 <= t) & (c < NC - 1)
    cmask = np.stack([seen.astype(f), np.where(seen, f(0), f(BIG))], axis=1)
    half_of = np.arange(P) // SN
    shift = np.stack([np.eye(P, k=SC * (CH - 1 - j), dtype=f) * (half_of[:, None] == half_of[None, :]) for j in range(CH - 1)],
                     axis=1).astype(f)
    return {"ident": np.eye(P, dtype=f), "shift": shift, "rope": rope.astype(f), "causal": causal, "cmask": cmask}


_INS = ["x", "norm_g", "w_in", "cmp_pos_k", "cmp_pos_v", "cmp_w1_k", "cmp_w2_k", "cmp_w1_v", "cmp_w2_v", "s5_lam_re",
        "s5_lam_im", "s5_log_dt", "s5_b_re", "s5_b_im", "s5_c_re", "s5_c_im", "s5_d", "w_glu", "b_glu", "w_proj_nsa",
        "w_proj_s5", "w_out", "final_g"]


def kernel(**inputs):
    import numpy as np
    import concourse.bacc as bacc
    from concourse.bass_utils import run_bass_kernel_spmd as run

    nc = bacc.Bacc("TRN2", target_bir_lowering=False, num_devices=1)
    arrays, args = {}, {}
    given = {n: np.ascontiguousarray(inputs[n]) for n in _INS} | shape_constants()
    for name, v in given.items():
        v = np.ascontiguousarray(v)
        arrays[f"in_{name}"] = v
        args[name] = nc.dram_tensor(f"in_{name}", v.shape, mybir.dt.from_np(v.dtype), kind="ExternalInput").ap()
    out = nc.dram_tensor("out_0", (1, T, D), F32, kind="ExternalOutput").ap()
    build_program(nc, args, out)
    r = run(nc, [arrays], core_ids=[0])
    return r.results[0]["out_0"]
```

```python
from contextlib import ExitStack

import concourse.bass as bass
from concourse import mybir

F32 = mybir.dt.float32
F32R = mybir.dt.float32r
ALU = mybir.AluOpType
ACT = mybir.ActivationFunctionType
AX_X = mybir.AxisListType.X

P = 128
T, D = 512, 1024
NT = T // P
KT = D // P
HEADS, GROUPS, DH = 8, 2, 64
HPG = HEADS // GROUPS
NC = 32
S5W = 512
SG, SC, SN = 32, 16, 64
CH = 4
NCH = T // CH
RUN, NRUN = 8, NCH // 8
GP = SG // 2
EPS = 1.0e-6
BIG = 1.0e30
TWO_PI = 6.283185307179586
MAGIC = 12582912.0
PI_A, PI_B = 6.28125, 0.0019340515136718750
PI_C = TWO_PI - PI_A - PI_B

COL = dict(q=0, kc=512, vc=640, ksl=768, vsl=896, kwi=1024, vwi=1152, gl=1280, gn=1304, u=1816, gs=2328,
           mga=2840, mgb=3864)

VAL_N = 2 * P + 3 * HEADS
NRAW, NSPLIT = 3, 2
BLK = 1024


def weight_blocks():
    b = [(f"u{t}", 1) for t in range(4)] + [(f"q{t}", 1) for t in range(4)]
    b += [(n, 1) for n in ("ksl", "kwi", "kc", "vc", "val0", "val1", "val2")]
    b += [(f"w1k{i}", 0) for i in range(4)] + [(f"w1v{i}", 0) for i in range(4)]
    b += [(n, 1) for n in ("gs0", "gs1", "gs2", "gs3", "gn0", "gn1", "glu0", "gn2", "glu1", "gn3")]
    for dp in range(4):
        b += [(f"pb{dp}", 1), (f"mgb{2 * dp}", 1), (f"mgb{2 * dp + 1}", 1)]
        b += [(f"pa{dp}", 1), (f"mga{2 * dp}", 1), (f"mga{2 * dp + 1}", 1)]
    b += [(f"wo{q}_{h}", 1) for q in range(4) for h in range(2)]
    return b


F_LOW_AFTER = ["gn2", "glu1", "gn3", "pb0"]
O_LOW_AFTER = ["gn2", "gn3", "mgb0", "mgb1"]


def two_tiles(step, steps):
    k = steps.index(step)
    return 2 * k, 2 * k + 1


def attention_units():
    return [(h // 2, h % 2, h, h // HPG, h % HPG, b) for h in range(HEADS) for b in range(2)]


P_OFF = [P * (i * (i + 1) // 2) for i in range(NT + 1)]
VAL_KT = [(0, 3), (3, 6), (6, 8)]
FILL = {1: ["gn0"], 4: ["gn1"], 7: ["glu0"], 8: ["glu1"], 9: ["gn2"], 11: ["glu2"], 12: ["glu3"], 13: ["gn3"]}
D_TERM_AT, GELU_AT, Z_SPLIT_AT = (3, 4), (4, 5), (5, 6)
LAG = 2


def bank_plan():
    uses, reads, jobs = [0] * 8, [0] * 8, {}

    def use(job, bank, nreads=1, nfills=1):
        before = reads[bank]
        uses[bank] += nfills
        reads[bank] += nreads
        jobs[job] = (bank, before, uses[bank], reads[bank])

    ring = [0]

    def pj(job, nreads=1, banks=tuple(range(8))):
        use(job, banks[ring[0] % len(banks)], nreads)
        ring[0] += 1

    for kt in range(KT):
        pj(f"xT{kt}")
    pj("u0")
    for r in range(2):
        pj(f"CT{r}", 3)
    for t in range(1, 4):
        pj(f"u{t}")
    for t in range(4):
        pj(f"q{t}", 8)
    for n in ("ksl", "kwi"):
        pj(n, 5)
    for m in range(4):
        pj(f"WT{m}")
    pj("KR")
    pj("kc", 8)
    pj("TT0")
    pj("TT1")
    pj("vc", 8)
    for m in range(8):
        pj(f"S{m}")
    for i in range(NT):
        pj(f"V{i}", 2)
    for n in ("HK", "HV", "HT"):
        pj(n)
    pj("KCMP", GROUPS)
    pj("VCMP", 4)
    for t in range(4):
        pj(f"gs{t}")
    for m in range(2):
        pj(f"SCC{m}", 2)
    for m in range(8):
        pj(f"Y{m}")
    for g in range(GROUPS):
        pj(f"PET{g}")
    for u in range(2 * HEADS + LAG):
        w = u - LAG
        if u < 2 * HEADS:
            for k in range(3):
                use(f"SC{u}_{k}", 1 + k, 2 if k == 0 else 1)
        if w >= 0:
            for k in range(3):
                use(f"PT{w}_{k}", 4 + (3 * w + k) % 2)
            if w % 4 == 0:
                use(f"O{w // 4}", 6 + w // 4 % 2, nfills=0)
        for j in FILL.get(u, []):
            use(j, 0)
    ring[0] = 1
    for dp in range(4):
        for kind in ("B", "MB", "A", "MA"):
            for d in (2 * dp, 2 * dp + 1):
                pj(f"{kind}{d}")
    for q in range(4):
        for m in range(2):
            pj(f"W{q}_{m}")
    return jobs


def build_program(nc, a, out):
    blocks = weight_blocks()
    block_at = {n: k for k, (n, _) in enumerate(blocks)}
    split_at, k_split = {}, 0
    for n, split in blocks:
        if split:
            split_at[n] = k_split
            k_split += 1
    split_names = [n for n, s in blocks if s]
    units = attention_units()
    NU = len(units)
    J = bank_plan()

    ctx = ExitStack()
    with ctx:
        def sb(name, shape, dt=F32):
            return ctx.enter_context(nc.sbuf_tensor(name, shape, dt))

        def shared(name, size, *sets):
            made = {}
            for tensors in sets:
                with ExitStack() as once:
                    for n, shape, dt in tensors:
                        made[n] = once.enter_context(nc.sbuf_tensor(n, shape, dt))
            sb(name, [P, size])
            return made

        hT_hi = sb("hT_hi", [P, KT, T], F32R)
        hT_lo = sb("hT_lo", [P, KT, T], F32R)
        raw = sb("raw", [P, NRAW, BLK])
        w_hi = sb("w_hi", [P, NSPLIT, BLK], F32R)
        w_lo = sb("w_lo", [P, NSPLIT, BLK], F32R)
        m = shared("room_x", 4096,
                   [("x_sb", [P, NT, D], F32)],
                   [("u_perm", [P, 4, CH, NCH], F32), ("probT", [P, 4, T], F32)],
                   [("r_sb", [P, NT, D], F32)])
        x_sb, u_perm, probT, r_sb = (m[n] for n in ("x_sb", "u_perm", "probT", "r_sb"))
        qr = sb("qr", [P, HPG, T])
        m = shared("room_q", 2048, [("qn", [P, HPG, T], F32)], [("tmp", [P, 4, T], F32)])
        qn, tmp = m["qn"], m["tmp"]
        sg_nsa = tmp[:, 2:4, :]
        m = shared("room_k", 1024, [("bb", [P, 2, GP, SC], F32)], [("kr", [P, 2, T], F32)], [("gfin", [P, D], F32)])
        bb, kr, gfin = m["bb"], m["kr"], m["gfin"]
        m = shared("room_v", 1024, [("c_nat", [P, 2, 4, SN], F32), ("b_nat", [P, 2, GP, SC], F32)],
                   [("v_tok", [P, NT, 2, P], F32)])
        c_nat, b_nat, v_tok = m["c_nat"], m["b_nat"], m["v_tok"]
        m = shared("room_flat", 2048,
                   [("flat_k", [P, 16, GROUPS, NC], F32), ("flat_v", [P, 16, GROUPS, NC], F32)],
                   [("peT", [P, GROUPS, NT, P], F32), ("e_cmp", [P, NT, HEADS, NC], F32)])
        flat_k, flat_v, peT, e_cmp = (m[n] for n in ("flat_k", "flat_v", "peT", "e_cmp"))
        m = shared("room_1", 4096,
                   [("W", [P, SG, CH, SC], F32), ("pr_a", [P, GP, CH, SC], F32), ("pr_b", [P, GP, CH, SC], F32)],
                   [("U_sh", [P, GP, NCH], F32), ("Y_sb", [P, GP, NCH], F32)],
                   [("oT_hi", [P, 4, T], F32R), ("oT_lo", [P, 4, T], F32R)])
        W, pr_a, pr_b, U_sh, Y_sb, oT_hi, oT_lo = (
            m[n] for n in ("W", "pr_a", "pr_b", "U_sh", "Y_sb", "oT_hi", "oT_lo"))
        m = shared("room_2", 4096,
                   [("E_re", [P, GP, CH, SC], F32), ("E_nim", [P, GP, CH, SC], F32), ("WT", [P, GP, P], F32)],
                   [("prob", [P, 3, P_OFF[NT]], F32)],
                   [("m_hi", [P, KT, T], F32R)])
        E, WT, prob, m_hi = (m["E_re"], m["E_nim"]), m["WT"], m["prob"], m["m_hi"]
        m = shared("room_3", 2 * GP * (NCH + 1),
                   [("X", [P, 2, GP, NCH + 1], F32)],
                   [("z_hi", [P, 4, T], F32R), ("z_lo", [P, 4, T], F32R)],
                   [("m_lo", [P, KT, T], F32R)])
        X, z_hi, z_lo, m_lo = m["X"], m["z_hi"], m["z_lo"], m["m_lo"]
        m = shared("room_4", 4096,
                   [("TT", [P, GP, CH, SC], F32), ("sx_a", [P, 1024], F32), ("sx_b", [P, 1024], F32)],
                   [("yT", [P, 4, T], F32)],
                   [("f_hi", [P, 4, T], F32R), ("f_lo", [P, 4, T], F32R)])
        TT, sx_a, sx_b, yT, f_hi, f_lo = (m[n] for n in ("TT", "sx_a", "sx_b", "yT", "f_hi", "f_lo"))
        m = shared("room_t", 2048, [("rope", [P, 4, T], F32)], [("z", [P, 4, T], F32)])
        rope, z = m["rope"], m["z"]
        m = shared("room_m", 2048, [("swapped", [P, 4, T], F32)], [("sg_s5", [P, 4, T], F32)])
        swapped, sg_s5 = m["swapped"], m["sg_s5"]
        m = shared("room_5", 640, [("KR", [P, GP, SC], F32), ("shift", [P, CH - 1, P], F32)],
                   [("hidn", [GROUPS * NC, 2, 256], F32)])
        KR, shift, hidn = m["KR"], m["shift"], m["hidn"]
        m = shared("room_6", 512, [("CS", [P, SG, SC], F32)], [("v_blk", [P, GROUPS, HPG * DH], F32)])
        CS, v_blk = m["CS"], m["v_blk"]
        causal = sb("causal", [P, T])
        ident = sb("ident", [P, P])
        CT = sb("CT", [P, 2, GP, SC])
        s5p = sb("s5p", [P, 18, GP])
        pw = sb("pw", [P, 2, CH, GP])
        pq = sb("pq", [P, 2, RUN, GP])
        pwt = sb("pwt", [P, 2, CH, GP])
        hid = sb("hid", [P, 2, 2, GROUPS * NC])
        w2 = sb("w2", [P, 2, 2, DH])
        kcT = sb("kcT", [P, GROUPS, NC])
        pos = sb("pos", [P, 2, 16])
        cmask = sb("cmask", [P, 2, NT, NC])
        gate = sb("gate", [P, NT, HEADS, 3])
        nmax_c = sb("nmax_c", [P, NT, HEADS])
        den_c = sb("den_c", [P, NT, HEADS])
        coef_c = sb("coef_c", [P, NT, HEADS])
        nmax = sb("nmax", [P, NU, NT])
        den = sb("den", [P, NU, NT])
        coef = sb("coef", [P, NU, NT])
        g_in = sb("g_in", [P, KT])
        d_col = sb("d_col", [P, 4])
        bias_glu = sb("bias_glu", [P, 4])
        half_bias = sb("half_bias", [P, 4])
        rms = sb("rms", [P, 6, NT])
        ssq4 = sb("ssq4", [P, NT, 4])

        bank = [ctx.enter_context(nc.psum_tensor(f"bank{i}", [P, 512], F32)) for i in range(8)]

        def sem(name):
            return ctx.enter_context(nc.semaphore(name))

        filled = [sem(f"bank{i}_filled") for i in range(8)]
        drained = [sem(f"bank{i}_drained") for i in range(8)]
        x_in = [sem(f"x{i}_in") for i in range(NT)]
        ident_in, consts_in, s5_in, cmp_in, x_again, gfin_in, g_in_loaded = (sem(n) for n in (
            "ident_in", "consts_in", "s5_in", "cmp_in", "x_again", "gfin_in", "g_in_loaded"))
        raw_full = [sem(f"raw{i}_full") for i in range(NRAW)]
        hi_done, lo_done, part_used = (sem(n) for n in ("w_hi_done", "w_lo_done", "w_part_used"))
        ssq_done, var_done, sqrt_done, xs_done, hhi_done = (sem(n) for n in (
            "ssq_done", "variance_done", "sqrt_done", "x_scaled", "hT_hi_done"))
        dve, act = sem("dve_chain"), sem("act_chain")
        s5_dt, s5_arg, s5_act, w_built, e_built = (sem(n) for n in (
            "s5_dt", "s5_arguments", "s5_functions", "W_built", "E_built"))
        u_out, u_in, scan_done, y_out, y_in, yd_done, z_done, z_split = (sem(n) for n in (
            "u_scratch_out", "U_in", "scan_done", "y_scratch_out", "y_in", "y_with_D", "z_done",
            "z_split"))
        qr_done, kr_done, gate_done, flat_zero, vz_done = (sem(n) for n in (
            "q_roped", "k_roped", "gates_done", "flat_zeroed", "v_blk_zeroed"))
        cs_done, ce_done, cm_done, e_done, p_done, pv_done = (sem(n) for n in (
            "cmp_shifted", "cmp_exp", "cmp_masked", "exp_done", "prob_done", "pv_done"))
        bias_done, th_done, f_split, oT_split, m_split, r_done, fin_sq, fin_var, fin_sqrt, rg_done, root_done, stored = (sem(n) for n in (
            "half_bias_done", "tanh_done", "f_split", "oT_split", "merged_split", "residual_done", "final_squares", "final_variance",
            "final_sqrt", "times_gain", "final_root", "stored"))
        y_ready = [sem(f"out{i}_ready") for i in range(NT)]
        zhi_done, fhi_done = sem("z_hi_done"), sem("f_hi_done")
        kc_zero = sem("kcT_zeroed")
        ohi_done = sem("oT_hi_done")
        inv_done = sem("inverse_root_done")

        u_scr = nc.dram_tensor("u_scratch", (S5W, CH, NCH), F32, kind="Internal").ap()
        y_scr = nc.dram_tensor("y_scratch", (S5W, CH, NCH), F32, kind="Internal").ap()

        def bk(job):
            return bank[J[job][0]]

        def open_bank(eng, job):
            b, before, _, _ = J[job]
            if before:
                eng.wait_ge(drained[b], before)

        def fill(ins, job):
            ins.then_inc(filled[J[job][0]], 1)

        def wait_fill(eng, job):
            b, _, fills, _ = J[job]
            eng.wait_ge(filled[b], fills)

        def drain(ins, job):
            ins.then_inc(drained[J[job][0]], 1)

        def wait_drained(eng, job):
            b, _, _, reads = J[job]
            eng.wait_ge(drained[b], reads)

        def last_job(name):
            base = name.rstrip("0123456789")
            n = name[len(base):]
            if base == "glu":
                return f"glu{2 * int(n) + 1}"
            if base in ("pa", "pb"):
                return f"{base[1].upper()}{2 * int(n) + 1}"
            if base in ("mga", "mgb"):
                return f"M{base[2].upper()}{n}"
            if name[:3] == "w1k" or name[:3] == "w1v":
                return f"H{name[2].upper()}" if name[3] == "3" else None
            if name[:2] == "wo":
                return f"W{name[2]}_1" if name[4] == "1" else None
            if base == "val":
                return f"V{NT - 1}" if n == "2" else None
            return name

        part_at = {n: k + 1 for k, n in enumerate(n for n, _ in blocks if last_job(n) is None)}

        def wait_used(eng, name):
            if last_job(name) is None:
                eng.wait_ge(part_used, part_at[name])
            else:
                wait_fill(eng, last_job(name))

        raw_count, count = {}, [0] * NRAW
        for k, (n, _) in enumerate(blocks):
            count[k % NRAW] += 32 if n[:3] == "val" else 16
            raw_count[n] = count[k % NRAW]

        def slot(name):
            return split_at[name] % NSPLIT

        def block_source(name):
            w_in = a["w_in"][0]
            if name[:3] == "w1k" or name[:3] == "w1v":
                w, i = a["cmp_w1_" + name[2]][0], int(name[3])
                return w.rearrange("(kt p) n -> p kt n", p=P)[:, 4 * i:4 * i + 4, :], (4, 256)
            if name[:3] == "glu":
                i = int(name[3])
                return a["w_glu"][0].rearrange("(kt p) n -> p kt n", p=P)[:, :, 256 * i:256 * i + 256], (4, 256)
            if name[:2] in ("pa", "pb"):
                w, i = a["w_proj_nsa" if name[1] == "a" else "w_proj_s5"][0], int(name[2])
                return w.rearrange("(kt p) n -> p kt n", p=P)[:, :, 256 * i:256 * i + 256], (4, 256)
            if name[:2] == "wo":
                q, h = int(name[2]), int(name[4])
                w = a["w_out"][0].rearrange("(kt p) n -> p kt n", p=P)
                return w[:, 4 * h:4 * h + 4, 256 * q:256 * q + 256], (4, 256)
            w = w_in.rearrange("(kt p) n -> p kt n", p=P)
            base = name.rstrip("0123456789")
            n = int(name[len(base):] or 0)
            if base == "val":
                k0, k1 = VAL_KT[n]
                return w[:, k0:k1, :], (k1 - k0, VAL_N)
            return w[:, :, COL[base] + P * n:COL[base] + P * n + P], (KT, P)

        def view(buf, s, dims):
            return buf[:, s, 0:dims[0] * dims[1]].rearrange("p (k n) -> p k n", n=dims[1])

        def wdims(name):
            return block_source(name)[1]

        ctx.enter_context(nc.allow_non_contiguous_dma(reason="small parameter vectors, one element per partition"))
        block = ctx.enter_context(nc.Block())

        @block.sync
        def _(sp):
            for i in range(NT):
                sp.dma_start(x_sb[:, i, :], a["x"][0, P * i:P * i + P, :]).then_inc(x_in[i], 16)

            def u_to_scratch():
                for t in range(4):
                    wait_drained(sp, f"u{t}")
                    sp.dma_start(u_scr[P * t:P * t + P], u_perm[:, t]).then_inc(u_out, 16)

            def u_from_scratch():
                sp.wait_ge(u_out, 64)
                for m in range(4):
                    wait_drained(sp, f"WT{m}")
                wait_drained(sp, "KR")
                by_pos = u_scr.rearrange("(q r c) s k -> r s c q k", r=2, c=SC)
                for par in range(2):
                    for e in range(CH):
                        row = SN * par + SC * e
                        sp.dma_start(U_sh[row:row + SC], by_pos[par, CH - 1 - e]).then_inc(u_in, 16)

            def y_through_scratch():
                for m in range(8):
                    wait_drained(sp, f"Y{m}")
                by_pos = y_scr.rearrange("(q r c) s k -> r s c q k", r=2, c=SC)
                for par in range(2):
                    for j in range(CH):
                        row = SN * par + SC * j
                        sp.dma_start(by_pos[par, j], Y_sb[row:row + SC]).then_inc(y_out, 16)
                sp.wait_ge(y_out, 16 * 2 * CH)
                sp.dma_start(yT[:, :, :], y_scr.rearrange("(t p) s k -> p t (s k)", p=P)).then_inc(y_in, 16)

            def load(dst, src, s):
                sp.dma_start(dst, src).then_inc(s, 16)

            def small_loads():
                for r, n in enumerate(("s5_lam_re", "s5_lam_im")):
                    flat = a[n][0].rearrange("g p -> (g p)")
                    load(s5p[:, r, :], flat.rearrange("(q p) -> p q", p=P), s5_in)
                dt2 = a["s5_log_dt"][0].rearrange("(q r) -> r q", r=2)
                for par in range(2):
                    load(s5p[SN * par:SN * par + SN, 2, :], dt2[par].partition_broadcast(SN), s5_in)
                for r, n in enumerate(("s5_b_re", "s5_b_im")):
                    flat = a[n][0].rearrange("g p c -> (g p) c")
                    load(b_nat[:, r], flat.rearrange("(q p) c -> p q c", p=P), s5_in)
                for r, n in enumerate(("s5_c_re", "s5_c_im")):
                    load(c_nat[:, r], a[n][0].rearrange("g c p -> (g c) p").rearrange("(t q) p -> q t p", q=P), s5_in)
                load(shift[:, :, :], a["shift"], consts_in)
                load(rope[:, :, :], a["rope"], consts_in)
                load(causal[:, :], a["causal"], consts_in)
                load(cmask[:, :, :, :], a["cmask"], consts_in)
                for r, n in enumerate("kv"):
                    load(w2[:, r], a["cmp_w2_" + n][0].rearrange("(h p) d -> p h d", p=P), cmp_in)
                    pv = a["cmp_pos_" + n][0].rearrange("(k j) d -> j d k", j=2)
                    for jp in range(2):
                        load(pos[DH * jp:DH * jp + DH, r, :], pv[jp], cmp_in)
                load(d_col[:, :], a["s5_d"][0].rearrange("(t p) -> p t", p=P), cmp_in)
                load(bias_glu[:, :], a["b_glu"][0].rearrange("(t p) -> p t", p=P), cmp_in)

            for k, (name, split) in enumerate(blocks):
                if k == NRAW:
                    small_loads()
                if k >= NRAW:
                    before, was_split = blocks[k - NRAW]
                    if was_split:
                        sp.wait_ge(lo_done, split_at[before] + 1)
                    else:
                        wait_used(sp, before)
                src, dims = block_source(name)
                dst, full = view(raw, k % NRAW, dims), raw_full[k % NRAW]
                if name[:3] == "val":
                    sp.dma_start(dst[:, :, 0:P], src[:, :, COL["vsl"]:COL["vsl"] + P]).then_inc(full, 16)
                    sp.dma_start(dst[:, :, P:VAL_N], src[:, :, COL["vwi"]:COL["vwi"] + VAL_N - P]).then_inc(full, 16)
                else:
                    sp.dma_start(dst, src).then_inc(full, 16)
                if name == "q3":
                    u_to_scratch()
                if name == "vc":
                    u_from_scratch()
                if name == "gn1":
                    y_through_scratch()
                if name == "pb1":
                    sp.wait_ge(oT_split, 4)
                    sp.dma_start(r_sb[:, :, :], a["x"][0].rearrange("(i p) d -> p i d", p=P)).then_inc(x_again, 16)
                    sp.dma_start(gfin[:, :], a["final_g"].partition_broadcast(P)).then_inc(gfin_in, 16)
            for i in range(NT):
                sp.wait_ge(y_ready[i], 1)
                sp.dma_start(out[0, P * i:P * i + P, :], r_sb[:, i, :]).then_inc(stored, 16)
            sp.wait_ge(stored, 16 * NT)

        @block.gpsimd
        def _(pl):
            nc.gpsimd.memset(flat_k[:, :, :, NC - 1:NC], 0.0).then_inc(flat_zero, 1)
            nc.gpsimd.memset(kcT[:, :, :], 0.0).then_inc(kc_zero, 1)
            nc.gpsimd.memset(flat_v[:, :, :, NC - 1:NC], 0.0).then_inc(flat_zero, 1)

            def low_part(lo, whole, hi, tiles, ready, signal):
                for t in tiles:
                    pl.wait_ge(ready, t + 1)
                    nc.gpsimd.tensor_tensor(lo[:, t, :], whole[:, t, :], hi[:, t, :].bitcast(F32),
                                            ALU.subtract).then_inc(signal, 1)

            for j, name in enumerate(split_names):
                pl.wait_ge(hi_done, j + 1)
                dims, k = wdims(name), block_at[name]
                w = view(raw, k % NRAW, dims)
                nc.gpsimd.tensor_tensor(view(w_lo, j % NSPLIT, dims), w, view(w_hi, j % NSPLIT, dims).bitcast(F32),
                                        ALU.subtract).then_inc(lo_done, 1)
                if name == "glu0":
                    low_part(z_lo, z, z_hi, range(4), zhi_done, z_split)
                if name in O_LOW_AFTER:
                    c = O_LOW_AFTER.index(name)
                    pl.wait_ge(ohi_done, c + 1)
                    nc.gpsimd.tensor_tensor(oT_lo[:, c, :], tmp[:, 1, :], oT_hi[:, c, :].bitcast(F32),
                                            ALU.subtract).then_inc(oT_split, 1)
                if name in F_LOW_AFTER:
                    low_part(f_lo, z, f_hi, [F_LOW_AFTER.index(name)], fhi_done, f_split)
                if name == "val0":
                    wait_fill(pl, "KR")
                    nc.gpsimd.memset(v_blk[:, :, :], 0.0).then_inc(vz_done, 1)

        @block.scalar
        def _(ac):
            ac.dma_start(ident[:, :], a["ident"]).then_inc(ident_in, 16)
            ac.dma_start(g_in[:, :], a["norm_g"][0].rearrange("(k p) -> p k", p=P)).then_inc(g_in_loaded, 16)

            def split_hi(j):
                name = split_names[j]
                dims, k = wdims(name), block_at[name]
                ac.wait_ge(raw_full[k % NRAW], raw_count[name])
                if j >= NSPLIT:
                    wait_used(ac, split_names[j - NSPLIT])
                nc.scalar.activation(view(w_hi, j % NSPLIT, dims), view(raw, k % NRAW, dims), ACT.Copy)\
                    .then_inc(hi_done, 1)

            def after(name):
                if split_at[name] + NSPLIT < len(split_names):
                    split_hi(split_at[name] + NSPLIT)

            def evacuate(job, dst, src, func=ACT.Copy, **kw):
                wait_fill(ac, job)
                drain(nc.scalar.activation(dst, src, func, **kw), job)

            ac.wait_ge(ident_in, 16)
            nc.scalar.activation(rms[:, 5, 0:2], ident[:, 0:2], ACT.Sqrt)
            for i in range(NT + 1):
                if i < NT:
                    ac.wait_ge(x_in[i], 16)
                    junk = (qr, qn)[i // 2][:, 2 * (i % 2):2 * (i % 2) + 2, :].rearrange("p a b -> p (a b)")
                    nc.scalar.activation(junk, x_sb[:, i, :], ACT.Square, accum_out=rms[:, 0, i:i + 1]).then_inc(ssq_done, 1)
                if i > 0:
                    ac.wait_ge(var_done, i)
                    nc.scalar.activation(rms[:, 2, i - 1:i], rms[:, 1, i - 1:i], ACT.Sqrt).then_inc(sqrt_done, 1)
            split_hi(0)
            ac.wait_ge(g_in_loaded, 16)
            for kt in range(KT):
                wait_fill(ac, f"xT{kt}")
                nc.scalar.activation(hT_hi[:, kt, :], bk(f"xT{kt}")[:, :], ACT.Copy, scale=g_in[:, kt:kt + 1])\
                    .then_inc(hhi_done, 1)
            split_hi(1)
            ac.wait_ge(s5_in, 16 * 8)
            nc.scalar.activation(s5p[:, 3, :], s5p[:, 2, :], ACT.Exp).then_inc(s5_dt, 1)
            ac.wait_ge(s5_arg, 1)
            nc.scalar.activation(s5p[:, 6, :], s5p[:, 4, :], ACT.Exp).then_inc(s5_act, 1)
            nc.scalar.activation(s5p[:, 7, :], s5p[:, 5, :], ACT.Sin).then_inc(s5_act, 1)
            nc.scalar.activation(s5p[:, 8, :], s5p[:, 5, :], ACT.Sin, scale=0.5).then_inc(s5_act, 1)

            for t in range(4):
                evacuate(f"u{t}", u_perm[:, t], bk(f"u{t}")[:, :].rearrange("p (k s) -> p s k", s=CH))
                after(f"u{t}")
            for t in range(4):
                g = t // 2
                for half in range(2):
                    evacuate(f"q{t}", qn[DH * g:DH * g + DH, 2 * (t % 2) + half, :],
                             bk(f"q{t}")[DH * half:DH * half + DH, :], scale=-0.125)
                after(f"q{t}")
            after("ksl")
            after("kwi")
            for m in range(4):
                evacuate(f"WT{m}", WT[:, 4 * m:4 * m + 4, :].rearrange("p a b -> p (a b)"), bk(f"WT{m}")[:, :])
            evacuate("KR", KR[:, :, :].rearrange("p a b -> p (a b)"), bk("KR")[:, 0:GP * SC])
            after("kc")
            for k in range(2):
                evacuate(f"TT{k}", TT[:, :, 2 * k:2 * k + 2, :].rearrange("p g j c -> p j g c"),
                         bk(f"TT{k}")[:, :].rearrange("p (j g c) -> p j g c", j=2, c=SC))
            after("vc")
            for m in range(8):
                ri, quarter = m % 2, m // 2
                evacuate(f"S{m}", X[:, ri, 4 * quarter:4 * quarter + 4, 1:NCH + 1],
                         bk(f"S{m}")[:, :].rearrange("p (q k) -> p q k", k=NCH))
            after("val0")
            for i in range(NT):
                evacuate(f"V{i}", v_tok[:, i].rearrange("p b c -> p (b c)"), bk(f"V{i}")[:, 0:2 * P])
                evacuate(f"V{i}", gate[:, i].rearrange("p h b -> p (h b)"), bk(f"V{i}")[:, 2 * P:VAL_N], ACT.Tanh, scale=0.5)
            for r, n in enumerate(("HK", "HV")):
                evacuate(n, hidn[:, r, :], bk(n)[0:GROUPS * NC, 0:256], ACT.Gelu_apprx_tanh)
            after("val1")
            after("val2")
            evacuate("HT", hid[:, :, :, :].rearrange("p r h n -> p (r h n)"), bk("HT")[:, 0:256])
            ac.wait_ge(kc_zero, 1)
            for g in range(GROUPS):
                rows = slice(DH * g, DH * g + DH)
                evacuate("KCMP", kcT[rows, g, :], bk("KCMP")[rows, 0:NC])
            ac.wait_ge(kr_done, 2)
            for t in range(4):
                evacuate(f"gs{t}", sg_s5[:, t, :], bk(f"gs{t}")[:, :], ACT.Silu)
                after(f"gs{t}")
            for m in range(2):
                ac.wait_ge(cs_done, m + 1)
                e = e_cmp[:, 2 * m:2 * m + 2]
                nc.scalar.activation(e, e, ACT.Exp, scale=-1.0).then_inc(ce_done, 1)
            for m in range(8):
                evacuate(f"Y{m}", Y_sb[:, 2 * m:2 * m + 2, :].rearrange("p a b -> p (a b)"), bk(f"Y{m}")[:, 0:2 * NCH])
            for g in range(GROUPS):
                evacuate(f"PET{g}", peT[:, g].rearrange("p i q -> p (i q)"), bk(f"PET{g}")[:, :])

            tanh_user = [None]

            def tanh_free(user):
                if tanh_user[0]:
                    wait_drained(ac, tanh_user[0])
                tanh_user[0] = user

            def fill_part(job):
                kind, t = job[:-1], int(job[-1])
                wait_fill(ac, job)
                tanh_free(job)
                bias = half_bias[:, t:t + 1] if kind == "glu" else 0.0
                nc.scalar.activation(tmp[:, 0, :], bk(job)[:, :], ACT.Tanh, scale=0.5, bias=bias).then_inc(th_done, 1)
                if kind != "glu":
                    after(job)
                elif t % 2:
                    after(f"glu{t // 2}")

            def copy_probs(w):
                step, n = 3 * w + 2, T - P
                if step >= 4:
                    ac.wait_ge(pv_done, step - 3)
                evacuate(f"PT{w}_2", probT[:, step % 4, 0:n], bk(f"PT{w}_2")[:, 0:n])

            ac.wait_ge(bias_done, 1)
            for u in range(NU + LAG):
                w = u - LAG
                if u < NU:
                    for i in range(NT):
                        n = P * (i + 1)
                        job = f"SC{u}_{max(i - 1, 0)}"
                        ac.wait_ge(drained[J[job][0]], J[job][1] + (2 if i == 1 else 1))
                        pi = prob[:, u % 3, P_OFF[i]:P_OFF[i] + n]
                        nc.scalar.activation(pi, pi, ACT.Exp, scale=-1.0, bias=nmax[:, u, i:i + 1],
                                             accum_out=den[:, u, i:i + 1]).then_inc(e_done, 1)
                        if w >= 0 and i == 1:
                            copy_probs(w)
                elif w >= 0:
                    copy_probs(w)
                if u in GELU_AT:
                    for t in two_tiles(u, GELU_AT):
                        ac.wait_ge(yd_done, t + 1)
                        nc.scalar.activation(z[:, t, :].rearrange("p (k j) -> p j k", j=CH),
                                             yT[:, t, :].rearrange("p (j k) -> p j k", k=NCH),
                                             ACT.Gelu_apprx_tanh).then_inc(z_done, 1)
                for job in FILL.get(u, []):
                    fill_part(job)
            for dp in range(4):
                for kind, user in (("MB", "B"), ("MA", "A")):
                    for d in (2 * dp, 2 * dp + 1):
                        if d % 2 == 0:
                            after(f"p{user.lower()}{dp}")
                        wait_fill(ac, f"{kind}{d}")
                        tanh_free(f"{user}{d}")
                        drain(nc.scalar.activation(tmp[:, 0, :], bk(f"{kind}{d}")[:, :], ACT.Tanh, scale=0.5), f"{kind}{d}")
                        after(f"mg{user.lower()}{d}")
            nc.scalar.activation(rms[:, 5, 2:4], ident[:, 0:2], ACT.Sqrt)
            for q in range(4):
                after(f"wo{q}_0")
                after(f"wo{q}_1")
                for m in range(2):
                    for i in (2 * m, 2 * m + 1):
                        ac.wait_ge(r_done, 2 * q + m + 1)
                        junk = (qr, z)[q // 2][:, 2 * (q % 2) + m, 256 * (i % 2):256 * (i % 2) + 256]
                        nc.scalar.activation(junk, r_sb[:, i, 256 * q:256 * q + 256], ACT.Square,
                                             accum_out=ssq4[:, i, q:q + 1]).then_inc(fin_sq, 1)
                    if q == 3:
                        ac.wait_ge(fin_var, m + 1)
                        two = slice(2 * m, 2 * m + 2)
                        nc.scalar.activation(rms[:, 2, two], rms[:, 1, two], ACT.Sqrt).then_inc(fin_sqrt, 1)
            for m in range(2):
                i = 2 * m + 1
                ac.wait_ge(rg_done, 4 + m)
                ac.wait_ge(root_done, m + 1)
                nc.scalar.activation(r_sb[:, i, :], r_sb[:, i, :], ACT.Copy, scale=rms[:, 3, i:i + 1]).then_inc(y_ready[i], 1)

        @block.tensor
        def _(pe):
            def mm3(dst, w, x, first, last):
                nc.tensor.matmul(dst, w[0], x[1], start=first, stop=False, skip_group_check=True)
                nc.tensor.matmul(dst, w[1], x[0], start=False, stop=False, skip_group_check=True)
                return nc.tensor.matmul(dst, w[0], x[0], start=False, stop=last, skip_group_check=True)

            def weights(name):
                pe.wait_ge(lo_done, split_at[name] + 1)
                dims = wdims(name)
                return [view(w, slot(name), dims) for w in (w_hi, w_lo)]

            def hT(kt, cols=slice(0, T)):
                return hT_hi[:, kt, cols], hT_lo[:, kt, cols]

            def channel_major(job, name, wait_hT=False):
                w = weights(name)
                open_bank(pe, job)
                for kt in range(KT):
                    if wait_hT:
                        wait_drained(pe, f"xT{kt}")
                    ins = mm3(bk(job)[:, :], [v[:, kt, :] for v in w], hT(kt), kt == 0, kt == KT - 1)
                fill(ins, job)

            def half_block(job, name, x, cols):
                w = weights(name)
                open_bank(pe, job)
                for kt in range(4):
                    ins = mm3(bk(job)[:, :], [v[:, kt, cols:cols + P] for v in w], [v[:, kt, :] for v in x], kt == 0, kt == 3)
                fill(ins, job)

            def four_transposes(job, sources):
                open_bank(pe, job)
                for n, src in enumerate(sources):
                    ins = nc.tensor.transpose(bk(job)[:, P * n:P * n + P], src, ident[:, :])
                fill(ins, job)

            pe.wait_ge(ident_in, 16)
            for i in range(NT):
                pe.wait_ge(xs_done, i + 1)
                for kt in range(KT):
                    ins = nc.tensor.transpose(bk(f"xT{kt}")[:, P * i:P * i + P], x_sb[:, i, P * kt:P * kt + P], ident[:, :])
                    if i == NT - 1:
                        fill(ins, f"xT{kt}")
            channel_major("u0", "u0", wait_hT=True)
            pe.wait_ge(s5_in, 16 * 8)
            for r in range(2):
                open_bank(pe, f"CT{r}")
                for t in range(4):
                    ins = nc.tensor.transpose(bk(f"CT{r}")[0:SN, P * t:P * t + P], c_nat[:, r, t, :], ident[:, :])
                fill(ins, f"CT{r}")
            for n in ("u1", "u2", "u3", "q0", "q1", "q2", "q3", "ksl", "kwi"):
                channel_major(n, n)
            pe.wait_ge(w_built, 4)
            for m in range(4):
                four_transposes(f"WT{m}", [W[:, 2 * gp:2 * gp + 2].rearrange("p g e c -> p (g e c)")
                                           for gp in range(4 * m, 4 * m + 4)])
            open_bank(pe, "KR")
            for g in range(SG):
                gp, par = g // 2, g % 2
                ins = nc.tensor.matmul(bk("KR")[SN * par:SN * par + SN, SC * gp:SC * gp + SC],
                                       W[:, g].rearrange("p e c -> p (e c)"), CS[:, g, :], start=True, stop=True,
                                       skip_group_check=True)
            fill(ins, "KR")
            channel_major("kc", "kc")
            pe.wait_ge(consts_in, 16 * 4)
            wait_drained(pe, "KR")
            for k in range(2):
                open_bank(pe, f"TT{k}")
                for jj in range(2):
                    j = 2 * k + jj
                    down = shift[:, j, :] if j < CH - 1 else ident[:, :]
                    ins = nc.tensor.matmul(bk(f"TT{k}")[:, 256 * jj:256 * jj + 256], down,
                                           KR[:, :, :].rearrange("p g c -> p (g c)"), start=True, stop=True,
                                           skip_group_check=True)
                fill(ins, f"TT{k}")
            channel_major("vc", "vc")
            pe.wait_ge(u_in, 16 * 2 * CH)
            for m in range(4):
                wait_drained(pe, f"WT{m}")
            for m in range(8):
                ri, quarter = m % 2, m // 2
                open_bank(pe, f"S{m}")
                for par in range(2):
                    rows = slice(SN * par, SN * par + SN)
                    for k in range(4):
                        gp = 4 * quarter + k
                        ins = nc.tensor.matmul(bk(f"S{m}")[rows, NCH * k:NCH * k + NCH],
                                               WT[rows, gp, SN * ri:SN * ri + SN], U_sh[rows, gp, :],
                                               start=True, stop=True, skip_group_check=True)
                fill(ins, f"S{m}")
            for n in range(3):
                w = weights(f"val{n}")
                k0, k1 = VAL_KT[n]
                for i in range(NT):
                    if n == 0:
                        open_bank(pe, f"V{i}")
                    for kt in range(k0, k1):
                        ins = mm3(bk(f"V{i}")[:, 0:VAL_N], hT(kt, slice(P * i, P * i + P)), [v[:, kt - k0, :] for v in w],
                                  kt == 0, kt == KT - 1)
                    if n == 2:
                        fill(ins, f"V{i}")
                if n < 2:
                    ins.then_inc(part_used, 1)
            pe.wait_ge(flat_zero, 2)
            for r, (n, flat) in enumerate((("k", flat_k), ("v", flat_v))):
                job = "H" + n.upper()
                wait_drained(pe, {"k": "kc", "v": "vc"}[n])
                open_bank(pe, job)
                for i in range(4):
                    k = block_at[f"w1{n}{i}"]
                    pe.wait_ge(raw_full[k % NRAW], raw_count[f"w1{n}{i}"])
                    w1 = view(raw, k % NRAW, (4, 256))
                    for kk in range(4):
                        ins = nc.tensor.matmul(bk(job)[0:GROUPS * NC, 0:256], flat[:, 4 * i + kk].rearrange("p g n -> p (g n)"),
                                               w1[:, kk, :], start=(i == 0 and kk == 0), stop=(i == 3 and kk == 3))
                    if i < 3:
                        ins.then_inc(part_used, 1)
                fill(ins, job)
            wait_drained(pe, "HK")
            wait_drained(pe, "HV")
            open_bank(pe, "HT")
            for r in range(2):
                for half in range(2):
                    c = 64 * (2 * r + half)
                    ins = nc.tensor.transpose(bk("HT")[:, c:c + 64], hidn[:, r, P * half:P * half + P], ident[0:64, 0:64])
            fill(ins, "HT")
            pe.wait_ge(cmp_in, 16 * 8)
            wait_drained(pe, "HT")
            open_bank(pe, "KCMP")
            for g in range(GROUPS):
                for half in range(2):
                    ins = nc.tensor.matmul(bk("KCMP")[DH * g:DH * g + DH, 0:NC], w2[:, 0, half, :],
                                           hid[:, 0, half, NC * g:NC * g + NC], start=(half == 0), stop=(half == 1))
            fill(ins, "KCMP")
            open_bank(pe, "VCMP")
            for r in range(HPG):
                for g in range(GROUPS):
                    for half in range(2):
                        ins = nc.tensor.matmul(bk("VCMP")[NC * r:NC * r + NC, DH * g:DH * g + DH],
                                               hid[:, 1, half, NC * g:NC * g + NC], w2[:, 1, half, :],
                                               start=(half == 0), stop=(half == 1))
            fill(ins, "VCMP")
            for t in range(4):
                channel_major(f"gs{t}", f"gs{t}")
            wait_drained(pe, "KCMP")
            for t in range(4):
                wait_drained(pe, f"q{t}")
            for m in range(2):
                open_bank(pe, f"SCC{m}")
                for ii in range(2):
                    i = 2 * m + ii
                    for r in range(HPG):
                        c = (ii * HPG + r) * GROUPS * NC
                        ins = nc.tensor.matmul(bk(f"SCC{m}")[:, c:c + GROUPS * NC], qn[:, r, P * i:P * i + P],
                                               kcT[:, :, :].rearrange("p g c -> p (g c)"), start=True, stop=True,
                                               skip_group_check=True)
                fill(ins, f"SCC{m}")
            wait_drained(pe, "TT0")
            wait_drained(pe, "TT1")
            pe.wait_ge(scan_done, 1)
            pe.wait_ge(e_built, 1)
            for m in range(8):
                open_bank(pe, f"Y{m}")
                for par in range(2):
                    rows = slice(SN * par, SN * par + SN)
                    for k in range(2):
                        gp = 2 * m + k
                        dst = bk(f"Y{m}")[rows, NCH * k:NCH * k + NCH]
                        nc.tensor.matmul(dst, TT[rows, gp].rearrange("p j c -> p (j c)"), U_sh[rows, gp, :],
                                         start=True, stop=False, skip_group_check=True)
                        for ri in range(2):
                            ins = nc.tensor.matmul(dst, E[ri][rows, gp].rearrange("p j c -> p (j c)"),
                                                   X[rows, ri, gp, 0:NCH], start=False, stop=(ri == 1),
                                                   skip_group_check=True)
                fill(ins, f"Y{m}")
            pe.wait_ge(cm_done, 1)
            for g in range(GROUPS):
                four_transposes(f"PET{g}", [e_cmp[:, i, HPG * g:HPG * g + HPG, :].rearrange("p h c -> p (h c)")
                                            for i in range(NT)])
            wait_drained(pe, "VCMP")

            def scores(u, k):
                c, half, h, g, r, b = units[u]
                rows = slice(DH * g, DH * g + DH)
                job = f"SC{u}_{k}"
                open_bank(pe, job)
                for i in ((0, 1), (2,), (3,))[k]:
                    dst = bk(job)[:, P * i:P * i + P * (i + 1)] if k == 0 else bk(job)[:, 0:P * (i + 1)]
                    ins = nc.tensor.matmul(dst, qr[rows, r, P * i:P * i + P], kr[rows, b, 0:P * (i + 1)],
                                           start=True, stop=True, skip_group_check=True)
                fill(ins, job)

            def transposes(u, k):
                job = f"PT{u}_{k}"
                open_bank(pe, job)
                col = 0
                for kt in ((0,), (1,), (2, 3))[k]:
                    for i in range(kt, NT):
                        src = prob[:, u % 3, P_OFF[i] + P * kt:P_OFF[i] + P * kt + P]
                        ins = nc.tensor.transpose(bk(job)[:, col:col + P], src, ident[:, :])
                        col += P
                fill(ins, job)

            def weighted_values(u, k):
                c, half, h, g, r, b = units[u]
                wait_drained(pe, f"PT{u}_{k}")
                o = bk(f"O{c}")
                if u % 4 == 0 and k == 0:
                    open_bank(pe, f"O{c}")
                    wait_drained(pe, f"PET{g}")
                    nc.tensor.matmul(o[:, :], v_blk[:, g, P * (c % 2):P * (c % 2) + P],
                                     peT[:, g].rearrange("p i q -> p (i q)"), start=True, stop=False, skip_group_check=True)
                col = 0
                for kt in ((0,), (1,), (2, 3))[k]:
                    n = P * (NT - kt)
                    ins = nc.tensor.matmul(o[DH * half:DH * half + DH, P * kt:T], v_tok[:, kt, b, DH * g:DH * g + DH],
                                           probT[:, (3 * u + k) % 4, col:col + n], start=False, stop=(kt == 3),
                                           skip_group_check=True)
                    col += n
                ins.then_inc(pv_done, 1)

            pe.wait_ge(qr_done, 8)
            pe.wait_ge(kr_done, 2)
            for i in range(NT):
                wait_drained(pe, f"V{i}")
            for u in range(NU + LAG):
                w = u - LAG
                if w >= 0:
                    pe.wait_ge(p_done, w + 1)
                    transposes(w, 0)
                if u < NU:
                    scores(u, 0)
                if w >= 0:
                    transposes(w, 1)
                    weighted_values(w, 0)
                if u < NU:
                    scores(u, 1)
                if w >= 0:
                    weighted_values(w, 1)
                    transposes(w, 2)
                if u < NU:
                    scores(u, 2)
                for job in FILL.get(u, []):
                    kind, t = job[:-1], int(job[-1])
                    if kind == "glu":
                        pe.wait_ge(z_split, 4)
                        half_block(job, f"glu{t // 2}", (z_hi, z_lo), P * (t % 2))
                    else:
                        channel_major(job, job)
                if w >= 0:
                    weighted_values(w, 2)
            for dp in range(4):
                pe.wait_ge(f_split, 4)
                for d in (2 * dp, 2 * dp + 1):
                    half_block(f"B{d}", f"pb{dp}", (f_hi, f_lo), P * (d % 2))
                for d in (2 * dp, 2 * dp + 1):
                    channel_major(f"MB{d}", f"mgb{d}")
                pe.wait_ge(oT_split, 4)
                for d in (2 * dp, 2 * dp + 1):
                    half_block(f"A{d}", f"pa{dp}", (oT_hi, oT_lo), P * (d % 2))
                for d in (2 * dp, 2 * dp + 1):
                    channel_major(f"MA{d}", f"mga{d}")
            for q in range(4):
                for h in range(2):
                    w = weights(f"wo{q}_{h}")
                    for m in range(2):
                        job = f"W{q}_{m}"
                        if h == 0:
                            open_bank(pe, job)
                        for ii in range(2):
                            i = 2 * m + ii
                            for kk in range(4):
                                kt = 4 * h + kk
                                if q == 0 and m == 0 and ii == 0:
                                    pe.wait_ge(m_split, kt + 1)
                                x = [v[:, kt, P * i:P * i + P] for v in (m_hi, m_lo)]
                                ins = mm3(bk(job)[:, 256 * ii:256 * ii + 256], x, [v[:, kk, :] for v in w],
                                          kt == 0 and ii == 0, kt == KT - 1)
                        if h == 1:
                            fill(ins, job)
                    if h == 0:
                        ins.then_inc(part_used, 1)

        @block.vector
        def _(ve):
            V = nc.vector
            chain = [0]

            def link(ins):
                chain[0] += 1
                ins.then_inc(dve, 1)
                ve.wait_ge(dve, chain[0])

            def tt(o, x, y, op):
                link(V.tensor_tensor(o, x, y, op))

            def ts(o, x, s1, s2, op0, op1=None):
                link(V.tensor_scalar(o, x, s1, s2, op0, op1) if op1 is not None else V.tensor_scalar(o, x, s1, None, op0))

            def stt(o, x, s, y, op0, op1):
                link(V.scalar_tensor_tensor(out=o, in0=x, scalar=s, in1=y, op0=op0, op1=op1))

            MUL, ADD, SUB = ALU.mult, ALU.add, ALU.subtract

            def variance(signal, i0, i1):
                V.tensor_scalar(rms[:, 1, i0:i1], rms[:, 0, i0:i1], 1.0 / D, EPS, MUL, ADD).then_inc(signal, 1)

            def inverse_root(signal_sqrt, count, i0, i1, signal):
                var, root, inv, t = (rms[:, n, i0:i1] for n in (1, 2, 3, 4))
                ve.wait_ge(signal_sqrt, count)
                link(V.reciprocal(inv, root))
                tt(t, inv, inv, MUL)
                tt(t, t, var, MUL)
                ts(t, t, -0.5, 1.5, MUL, ADD)
                V.tensor_tensor(inv, inv, t, MUL).then_inc(signal, 1)
                ve.wait_ge(signal, count)

            for i in range(NT):
                ve.wait_ge(ssq_done, i + 1)
                variance(var_done, i, i + 1)
                inverse_root(sqrt_done, i + 1, i, i + 1, inv_done)
                V.tensor_scalar(x_sb[:, i, :], x_sb[:, i, :], rms[:, 3, i:i + 1], None, MUL).then_inc(xs_done, 1)

            ve.wait_ge(g_in_loaded, 16)
            for kt in range(KT):
                ve.wait_ge(hhi_done, kt + 1)
                drain(V.scalar_tensor_tensor(out=hT_lo[:, kt, :], in0=bk(f"xT{kt}")[:, :], scalar=g_in[:, kt:kt + 1],
                                             in1=hT_hi[:, kt, :].bitcast(F32), op0=MUL, op1=SUB), f"xT{kt}")
            row = lambda n: s5p[:, n, :]
            LRE, LIM, DT, MRE, ARG, MAG, SIN, SINH, N, ARE, AIM, DEN, AM1, ZRE, ZIM, T1, T2 = (
                row(n) for n in (0, 1, 3, 4, 5, 6, 7, 8, 9, 10, 11, 12, 13, 14, 15, 16, 17))
            ve.wait_ge(s5_dt, 1)
            tt(MRE, LRE, DT, MUL)
            tt(ARG, LIM, DT, MUL)
            ts(N, ARG, 1.0 / TWO_PI, MAGIC, MUL, ADD)
            ts(N, N, MAGIC, None, SUB)
            stt(ARG, N, -PI_A, ARG, MUL, ADD)
            stt(ARG, N, -PI_B, ARG, MUL, ADD)
            stt(ARG, N, -PI_C, ARG, MUL, ADD)
            V.tensor_scalar(ARG, ARG, 3.1415925, -3.1415925, ALU.min, ALU.max).then_inc(s5_arg, 1)

            for r in range(2):
                wait_fill(ve, f"CT{r}")
                sign = (1.0, -1.0)[r]
                cv = bk(f"CT{r}")[0:SN, :]
                drain(V.tensor_scalar(CS[SN * r:SN * r + SN].rearrange("p g c -> p (g c)"), cv, sign, None, MUL), f"CT{r}")
                cv = cv.rearrange("p (q r c) -> p r q c", r=2, c=SC)
                for par in range(2):
                    drain(V.tensor_scalar(CT[SN * par:SN * par + SN, r], cv[:, par], sign, None, MUL), f"CT{r}")
            ve.wait_ge(s5_act, 3)
            tt(T1, SINH, SINH, MUL)
            ts(T1, T1, -2.0, 1.0, MUL, ADD)
            tt(ARE, MAG, T1, MUL)
            tt(AIM, MAG, SIN, MUL)
            tt(T1, LRE, LRE, MUL)
            tt(T2, LIM, LIM, MUL)
            tt(DEN, T1, T2, ADD)
            link(V.reciprocal(DEN, DEN))
            ts(AM1, ARE, -1.0, None, ADD)
            tt(T1, AM1, LRE, MUL)
            tt(T2, AIM, LIM, MUL)
            tt(T1, T1, T2, ADD)
            tt(ZRE, T1, DEN, MUL)
            tt(T1, AIM, LRE, MUL)
            tt(T2, AM1, LIM, MUL)
            tt(T1, T1, T2, SUB)
            tt(ZIM, T1, DEN, MUL)

            def per_channel(v):
                return v.unsqueeze(2).broadcast_to((P, GP, SC))

            ta, tb = (t[:, :, 0, :] for t in (pr_a, pr_b))
            for o, (z0, z1), op in ((bb[:, 0], (ZRE, ZIM), SUB), (bb[:, 1], (ZIM, ZRE), ADD)):
                tt(ta, b_nat[:, 0], per_channel(z0), MUL)
                tt(tb, b_nat[:, 1], per_channel(z1), MUL)
                tt(o, ta, tb, op)

            def powers(dst, base_re, base_im, count):
                link(V.tensor_copy(dst[:, 0, 0], base_re))
                link(V.tensor_copy(dst[:, 1, 0], base_im))
                n = 1
                while n < count:
                    t0, t1 = pwt[:, 0, 0:n], pwt[:, 1, 0:n]
                    fr, fi = (dst[:, r, n - 1].unsqueeze(1).broadcast_to((P, n, GP)) for r in range(2))
                    tt(t0, dst[:, 0, 0:n], fr, MUL)
                    tt(t1, dst[:, 1, 0:n], fi, MUL)
                    tt(dst[:, 0, n:2 * n], t0, t1, SUB)
                    tt(t0, dst[:, 0, 0:n], fi, MUL)
                    tt(t1, dst[:, 1, 0:n], fr, MUL)
                    tt(dst[:, 1, n:2 * n], t0, t1, ADD)
                    n *= 2

            powers(pw, ARE, AIM, CH)

            def products(n, re, im, cross):
                shape = (P, GP, n, SC)
                pr, pi = (pw[:, r, 0:n].rearrange("p k q -> p q k").unsqueeze(3).broadcast_to(shape) for r in range(2))
                xr, xi = (v.unsqueeze(2).broadcast_to(shape) for v in (re, im))
                pa, pb = pr_a[:, :, 0:n, :], pr_b[:, :, 0:n, :]
                link(V.tensor_tensor(pa, pr, xi if cross else xr, MUL))
                link(V.tensor_tensor(pb, pi, xr if cross else xi, MUL))
                return pa, pb

            w4 = W[:, :, :, :].rearrange("p (q r) e c -> p r q e c", r=2)
            for ri in range(2):
                for par in range(2):
                    link(V.tensor_copy(w4[SN * ri:SN * ri + SN, par, :, 0, :], bb[SN * par:SN * par + SN, ri]))
                pa, pb = products(CH - 1, bb[:, 0], bb[:, 1], ri == 1)
                for par in range(2):
                    rows = slice(SN * par, SN * par + SN)
                    V.tensor_tensor(w4[SN * ri:SN * ri + SN, par, :, 1:CH, :], pa[rows], pb[rows],
                                    ADD if ri else SUB).then_inc(w_built, 1)
                ve.wait_ge(w_built, 2 * ri + 2)
            pa, pb = products(CH, CT[:, 0], CT[:, 1], False)
            tt(E[0][:, :, :, :], pa, pb, ADD)
            pa, pb = products(CH, CT[:, 0], CT[:, 1], True)
            V.tensor_tensor(E[1][:, :, :, :], pa, pb, SUB).then_inc(e_built, 1)
            ve.wait_ge(e_built, 1)

            ve.wait_ge(consts_in, 16 * 4)
            for t in range(4):
                job, g = f"q{t}", t // 2
                ve.wait_ge(drained[J[job][0]], J[job][1] + 2)
                dst = slice(DH * g, DH * g + DH)
                for half in range(2):
                    r = 2 * (t % 2) + half
                    src = slice(DH * half, DH * half + DH)
                    drain(V.tensor_tensor(qr[dst, r, :], bk(job)[src, :], rope[src, 0, :], MUL), job)
                    for s in range(2):
                        src = slice(DH * half + 32 * s, DH * half + 32 * s + 32)
                        to = slice(DH * g + 32 * (1 - s), DH * g + 32 * (1 - s) + 32)
                        drain(V.tensor_tensor(swapped[to, r, :], bk(job)[src, :], rope[src, 1, :], MUL), job)
                wait_drained(ve, job)
                for half in range(2):
                    r = 2 * (t % 2) + half
                    V.tensor_tensor(qr[dst, r, :], qr[dst, r, :], swapped[dst, r, :], ADD).then_inc(qr_done, 1)
            ve.wait_ge(qr_done, 8)
            for b, job in enumerate(("ksl", "kwi")):
                wait_fill(ve, job)
                drain(V.tensor_tensor(kr[:, b, :], bk(job)[:, :], rope[:, 2, :], MUL), job)
                for s in range(4):
                    src = slice(32 * s, 32 * s + 32)
                    to = slice(32 * (s ^ 1), 32 * (s ^ 1) + 32)
                    drain(V.tensor_tensor(swapped[to, b, :], bk(job)[src, :], rope[src, 3, :], MUL), job)
                wait_drained(ve, job)
                V.tensor_tensor(kr[:, b, :], kr[:, b, :], swapped[:, b, :], ADD).then_inc(kr_done, 1)
            powers(pq, pw[:, 0, CH - 1], pw[:, 1, CH - 1], RUN)
            ve.wait_ge(cmp_in, 16 * 8)
            V.tensor_scalar(half_bias[:, :], bias_glu[:, :], 0.5, None, MUL).then_inc(bias_done, 1)
            for r, (job, flat) in enumerate((("kc", flat_k), ("vc", flat_v))):
                wait_fill(ve, job)
                for jp in range(2):
                    to = slice(DH * jp, DH * jp + DH)
                    for g in range(GROUPS):
                        src = bk(job)[DH * g:DH * g + DH, :].rearrange("p (n k j) -> p j k n", k=8, j=2)
                        for kh in range(2):
                            ins = V.tensor_tensor(flat[to, 8 * kh:8 * kh + 8, g, 0:NC - 1], src[:, jp, :, kh:kh + NC - 1],
                                                  pos[to, r, 8 * kh:8 * kh + 8].unsqueeze(2).broadcast_to((DH, 8, NC - 1)),
                                                  ADD)
                            drain(ins, job)
            wait_drained(ve, "vc")
            link(V.memset(X[:, :, :, 0:1], 0.0))
            for m in range(8):
                wait_drained(ve, f"S{m}")
            runs = X[:, :, :, 1:NCH + 1].rearrange("p r q (m j) -> p r q m j", j=RUN)

            def both_parts(dst, src, are, aim, width):
                n = 2 * GP * width
                ta, tb = (t[:, 0:n].rearrange("p (r b c) -> p r b c", r=2, b=GP) for t in (sx_a, sx_b))
                tt(ta, src, are, MUL)
                tt(tb, src, aim, MUL)
                tt(dst, dst, ta, ADD)
                tt(dst[:, 0], dst[:, 0], tb[:, 1], SUB)
                tt(dst[:, 1], dst[:, 1], tb[:, 0], ADD)

            for j in range(1, RUN):
                A = [pw[:, r, CH - 1].unsqueeze(1).unsqueeze(3).broadcast_to((P, 2, GP, NRUN)) for r in range(2)]
                both_parts(runs[:, :, :, :, j], runs[:, :, :, :, j - 1], *A, NRUN)
            for k in range(1, NRUN):
                A = [pq[:, r, RUN - 1].unsqueeze(1).unsqueeze(3).broadcast_to((P, 2, GP, 1)) for r in range(2)]
                both_parts(runs[:, :, :, k, RUN - 1:RUN], runs[:, :, :, k - 1, RUN - 1:RUN], *A, 1)
            for q0 in (0, 8):
                qs = slice(q0, q0 + 8)
                shape = (P, 8, NRUN - 1, RUN - 1)
                ar, ai = (pq[:, r, 0:RUN - 1, qs].rearrange("p k q -> p q k").unsqueeze(2).broadcast_to(shape) for r in range(2))
                xr, xi = (runs[:, r, qs, 0:NRUN - 1, RUN - 1:RUN].broadcast_to(shape) for r in range(2))
                n = shape[1] * shape[2] * shape[3]
                ta, tb = (t[:, 0:n].rearrange("p (a b c) -> p a b c", a=8, b=NRUN - 1) for t in (sx_a, sx_b))
                for r, (s0, s1), op in ((0, (xr, xi), SUB), (1, (xi, xr), ADD)):
                    dst = runs[:, r, qs, 1:NRUN, 0:RUN - 1]
                    tt(ta, s0, ar, MUL)
                    tt(tb, s1, ai, MUL)
                    tt(dst, dst, ta, ADD)
                    last = V.tensor_tensor(dst, dst, tb, op)
                    if q0 and r:
                        last.then_inc(scan_done, 1)
                    else:
                        link(last)
            for i in range(NT):
                wait_drained(ve, f"V{i}")
            V.tensor_scalar(gate[:, :, :, :], gate[:, :, :, :], 1.0, None, ADD).then_inc(gate_done, 1)

            ve.wait_ge(vz_done, 1)
            wait_fill(ve, "VCMP")
            for r in range(HPG):
                rows = slice(NC * r, NC * r + NC)
                drain(V.tensor_copy(v_blk[rows, :, DH * r:DH * r + DH],
                                    bk("VCMP")[rows, 0:GROUPS * DH].rearrange("p (g d) -> p g d", g=GROUPS)), "VCMP")
            wait_fill(ve, "HV")
            for m in range(2):
                job = f"SCC{m}"
                wait_fill(ve, job)
                for ii in range(2):
                    i = 2 * m + ii
                    src = bk(job)[:, 256 * ii:256 * ii + 256].rearrange("p (r g c) -> p g r c", g=GROUPS, c=NC)
                    drain(V.tensor_tensor(e_cmp[:, i].rearrange("p (g r) c -> p g r c", g=GROUPS), src,
                                          cmask[:, 1, i].unsqueeze(1).unsqueeze(1).broadcast_to((P, GROUPS, HPG, NC)), ADD), job)
                wait_drained(ve, job)
                tiles = slice(2 * m, 2 * m + 2)
                e, low = e_cmp[:, tiles], nmax_c[:, tiles]
                link(V.tensor_reduce(low, e, AX_X, ALU.min))
                V.tensor_tensor(e, e, low.unsqueeze(3).broadcast_to((P, 2, HEADS, NC)), SUB).then_inc(cs_done, 1)
            for m in range(2):
                tiles = slice(2 * m, 2 * m + 2)
                e = e_cmp[:, tiles]
                ve.wait_ge(ce_done, m + 1)
                tt(e, e, cmask[:, 0, tiles].unsqueeze(2).broadcast_to((P, 2, HEADS, NC)), MUL)
                link(V.tensor_reduce(den_c[:, tiles], e, AX_X, ALU.add))
            ve.wait_ge(gate_done, 1)
            ts(den_c[:, :, :], den_c[:, :, :], 1.0e-30, None, ALU.max)
            link(V.reciprocal(coef_c[:, :, :], den_c[:, :, :]))
            tt(coef_c[:, :, :], coef_c[:, :, :], gate[:, :, :, 0], MUL)
            V.tensor_tensor(e_cmp[:, :, :, :], e_cmp[:, :, :, :],
                            coef_c[:, :, :].unsqueeze(3).broadcast_to((P, NT, HEADS, NC)), MUL).then_inc(cm_done, 1)

            def fill_part(n, job):
                kind, t = job[:-1], int(job[-1])
                ve.wait_ge(th_done, n + 1)
                if job == "glu0":
                    ve.wait_ge(z_split, 4)
                if kind == "glu":
                    drain(V.scalar_tensor_tensor(out=z[:, t, :], in0=tmp[:, 0, :], scalar=1.0, in1=z[:, t, :],
                                                 op0=ADD, op1=MUL), job)
                    wait_drained(ve, job)
                    wait_drained(ve, f"gs{t}")
                    stt(z[:, t, :], z[:, t, :], 2.0, sg_s5[:, t, :], MUL, MUL)
                    V.tensor_copy(f_hi[:, t, :], z[:, t, :]).then_inc(fhi_done, 1)
                else:
                    drain(V.scalar_tensor_tensor(out=sg_nsa[:, t % 2, :], in0=tmp[:, 0, :], scalar=1.0, in1=bk(job)[:, :],
                                                 op0=ADD, op1=MUL), job)

            def gate_pair(c):
                job = f"O{c}"
                ve.wait_ge(pv_done, 12 * (c + 1))
                wait_drained(ve, f"gn{c}")
                if c > 0:
                    ve.wait_ge(oT_split, c)
                drain(V.tensor_tensor(tmp[:, 1, :], bk(job)[:, :], sg_nsa[:, c % 2, :], MUL), job)
                wait_drained(ve, job)
                V.tensor_copy(oT_hi[:, c, :], tmp[:, 1, :]).then_inc(ohi_done, 1)

            for m in range(8):
                wait_fill(ve, f"Y{m}")
            ve.wait_ge(kr_done, 2)
            fills = 0

            def masked(u, i):
                n, job = P * (i + 1), f"SC{u}_{max(i - 1, 0)}"
                wait_fill(ve, job)
                src = bk(job)[:, P:3 * P] if i == 1 else bk(job)[:, 0:n]
                drain(V.tensor_tensor_reduce(prob[:, u % 3, P_OFF[i]:P_OFF[i] + n], src, causal[:, T - n:T], 1.0,
                                             3.0e38, ADD, ALU.min, nmax[:, u, i:i + 1]), job)

            def copy_probs(w, k):
                job, step, n = f"PT{w}_{k}", 3 * w + k, T - P * k
                wait_fill(ve, job)
                if step >= 4:
                    ve.wait_ge(pv_done, step - 3)
                drain(V.tensor_copy(probT[:, step % 4, 0:n], bk(job)[:, 0:n]), job)

            def normalise(u):
                h, b = units[u][2], units[u][5]
                ve.wait_ge(e_done, 4 * (u + 1))
                link(V.reciprocal(coef[:, u, :], den[:, u, :]))
                tt(coef[:, u, :], coef[:, u, :], gate[:, :, h, 1 + b], MUL)
                for i in range(NT):
                    pi = prob[:, u % 3, P_OFF[i]:P_OFF[i + 1]]
                    ins = V.tensor_scalar(pi, pi, coef[:, u, i:i + 1], None, MUL)
                ins.then_inc(p_done, 1)

            for u in range(NU + LAG):
                w = u - LAG
                if w >= 0:
                    copy_probs(w, 0)
                if u < NU:
                    if u >= 3:
                        wait_fill(ve, f"PT{u - 3}_2")
                    masked(u, 0)
                    masked(u, 1)
                if w >= 0:
                    copy_probs(w, 1)
                for job in FILL.get(u - 1, []):
                    fill_part(fills, job)
                    fills += 1
                if 1 <= u <= NU:
                    normalise(u - 1)
                if u < NU:
                    masked(u, 2)
                    masked(u, 3)
                if u in D_TERM_AT:
                    ve.wait_ge(y_in, 16)
                    for t in two_tiles(u, D_TERM_AT):
                        V.scalar_tensor_tensor(out=yT[:, t, :], in0=u_perm[:, t].rearrange("p s k -> p (s k)"),
                                               scalar=d_col[:, t:t + 1], in1=yT[:, t, :], op0=MUL, op1=ADD)\
                         .then_inc(yd_done, 1)
                if u in Z_SPLIT_AT:
                    for t in two_tiles(u, Z_SPLIT_AT):
                        ve.wait_ge(z_done, t + 1)
                        V.tensor_copy(z_hi[:, t, :], z[:, t, :]).then_inc(zhi_done, 1)
                if u >= 6 and u % 4 == 2:
                    gate_pair(u // 4 - 1)
            gate_pair(HEADS // 2 - 1)
            ve.wait_ge(oT_split, HEADS // 2)
            for dp in range(4):
                for d in (2 * dp, 2 * dp + 1):
                    wait_drained(ve, f"MB{d}")
                    wait_fill(ve, f"B{d}")
                    drain(V.scalar_tensor_tensor(out=tmp[:, 1 + d % 2, :], in0=tmp[:, 0, :], scalar=1.0,
                                                 in1=bk(f"B{d}")[:, :], op0=ADD, op1=MUL), f"B{d}")
                for d in (2 * dp, 2 * dp + 1):
                    wait_drained(ve, f"MA{d}")
                    wait_fill(ve, f"A{d}")
                    drain(V.scalar_tensor_tensor(out=tmp[:, 3, :], in0=tmp[:, 0, :], scalar=1.0,
                                                 in1=bk(f"A{d}")[:, :], op0=ADD, op1=MUL), f"A{d}")
                    wait_drained(ve, f"A{d}")
                    wait_drained(ve, f"B{d}")
                    tt(tmp[:, 3, :], tmp[:, 3, :], tmp[:, 1 + d % 2, :], ADD)
                    link(V.tensor_copy(m_hi[:, d, :], tmp[:, 3, :]))
                    V.tensor_tensor(m_lo[:, d, :], tmp[:, 3, :], m_hi[:, d, :].bitcast(F32), SUB).then_inc(m_split, 1)
                    ve.wait_ge(m_split, d + 1)
            ve.wait_ge(x_again, 16)
            ve.wait_ge(gfin_in, 16)

            def residual(q, m):
                job = f"W{q}_{m}"
                wait_fill(ve, job)
                r2 = r_sb[:, 2 * m:2 * m + 2, 256 * q:256 * q + 256]
                V.scalar_tensor_tensor(out=r2, in0=bk(job)[:, :].rearrange("p (i c) -> p i c", i=2), scalar=0.125,
                                       in1=r2, op0=MUL, op1=ADD).then_inc(r_done, 1)

            def times_gain(q, tiles):
                r = r_sb[:, tiles, 256 * q:256 * q + 256]
                n = tiles.stop - tiles.start
                V.tensor_tensor(r, r, gfin[:, 256 * q:256 * q + 256].unsqueeze(1).broadcast_to((P, n, 256)), MUL)\
                 .then_inc(rg_done, 1)

            for q in range(3):
                for m in range(2):
                    residual(q, m)
                ve.wait_ge(fin_sq, 4 * (q + 1))
                times_gain(q, slice(0, NT))
            residual(3, 0)
            for m in range(2):
                two = slice(2 * m, 2 * m + 2)
                ve.wait_ge(fin_sq, 12 + 2 * (m + 1))
                link(V.tensor_reduce(rms[:, 0, two], ssq4[:, two, :], AX_X, ALU.add))
                variance(fin_var, two.start, two.stop)
                times_gain(3, two)
                inverse_root(fin_sqrt, m + 1, two.start, two.stop, root_done)
                if m == 0:
                    residual(3, 1)
                i = 2 * m
                ve.wait_ge(rg_done, 4 + m)
                V.tensor_scalar(r_sb[:, i, :], r_sb[:, i, :], rms[:, 3, i:i + 1], None, MUL).then_inc(y_ready[i], 1)


def shape_constants():
    import numpy as np
    f = np.float32
    half = DH // 2
    inv_freq = f(10000.0) ** (-np.arange(half, dtype=f) / f(half))
    ang = np.arange(T, dtype=f)[None, :] * inv_freq[:, None]
    cos, sin = np.cos(ang).astype(f), np.sin(ang).astype(f)
    cos2, sin2 = np.tile(cos, (4, 1)), np.tile(np.concatenate([sin, -sin]), (2, 1))
    rope = np.stack([cos2 * f(-0.125), sin2 * f(-0.125), cos2, sin2], axis=1)
    causal = np.zeros((P, T), f)
    q, k = np.arange(P)[:, None], np.arange(P)[None, :]
    causal[:, T - P:] = np.where(k > q, f(BIG), f(0))
    t = (np.arange(NT)[None, :] * P + np.arange(P)[:, None])[:, :, None]
    c = np.arange(NC)[None, None, :]
    seen = (16 * c + 31 <= t) & (c < NC - 1)
    cmask = np.stack([seen.astype(f), np.where(seen, f(0), f(BIG))], axis=1)
    half_of = np.arange(P) // SN
    shift = np.stack([np.eye(P, k=SC * (CH - 1 - j), dtype=f) * (half_of[:, None] == half_of[None, :]) for j in range(CH - 1)],
                     axis=1).astype(f)
    return {"ident": np.eye(P, dtype=f), "shift": shift, "rope": rope.astype(f), "causal": causal, "cmask": cmask}


_INS = ["x", "norm_g", "w_in", "cmp_pos_k", "cmp_pos_v", "cmp_w1_k", "cmp_w2_k", "cmp_w1_v", "cmp_w2_v", "s5_lam_re",
        "s5_lam_im", "s5_log_dt", "s5_b_re", "s5_b_im", "s5_c_re", "s5_c_im", "s5_d", "w_glu", "b_glu", "w_proj_nsa",
        "w_proj_s5", "w_out", "final_g"]


def kernel(**inputs):
    import numpy as np
    import concourse.bacc as bacc
    from concourse.bass_utils import run_bass_kernel_spmd as run

    nc = bacc.Bacc("TRN2", target_bir_lowering=False, num_devices=1)
    arrays, args = {}, {}
    given = {n: np.ascontiguousarray(inputs[n]) for n in _INS} | shape_constants()
    for name, v in given.items():
        v = np.ascontiguousarray(v)
        arrays[f"in_{name}"] = v
        args[name] = nc.dram_tensor(f"in_{name}", v.shape, mybir.dt.from_np(v.dtype), kind="ExternalInput").ap()
    out = nc.dram_tensor("out_0", (1, T, D), F32, kind="ExternalOutput").ap()
    build_program(nc, args, out)
    r = run(nc, [arrays], core_ids=[0])
    return r.results[0]["out_0"]
```
